# Optimizing a Trainium2 kernel written in Bass

```python
import jax
import jax.numpy as jnp
from jax import lax
import numpy as np
import math

D_MODEL = 1024
BATCH = 1
SEQ = 256
DEPTH = 1

GRID_W = 64
CTX_LEN = 256
D_MIX = D_MODEL
D_MLSTM = D_MIX // 2
D_CONV = D_MIX - D_MLSTM
M_HEADS = 4
V_DIM = D_MLSTM // M_HEADS
QK_DIM = V_DIM // 2
D_QK = M_HEADS * QK_DIM
N_GATES = 4 * M_HEADS
CHUNK = 128
CONV_WIDTH = 31
N_EXPERTS = 64
TOP_K = 8
D_EXPERT = D_MODEL // 4
D_SHARED = D_EXPERT
ROUTE_SCALE = 2.5
EXPERT_BLOCK = 128
EPS = 1e-6
IN_SPLITS = (D_QK, 2 * D_QK, 2 * D_QK + D_MLSTM, 2 * D_QK + 2 * D_MLSTM,
             2 * D_QK + 2 * D_MLSTM + N_GATES, 2 * D_QK + 2 * D_MLSTM + N_GATES + D_CONV)
D_IN = 2 * D_QK + 2 * D_MLSTM + N_GATES + 2 * D_CONV


def _rms_norm(x, g):
    xf = x.astype(jnp.float32)
    y = xf * lax.rsqrt(jnp.mean(xf * xf, axis=-1, keepdims=True) + EPS)
    return (y * g.astype(jnp.float32)).astype(x.dtype)

def _layer_norm(x, g, b):
    xf = x.astype(jnp.float32)
    mu = jnp.mean(xf, axis=-1, keepdims=True)
    xc = xf - mu
    y = xc * lax.rsqrt(jnp.mean(xc * xc, axis=-1, keepdims=True) + EPS)
    return (y * g.astype(jnp.float32) + b.astype(jnp.float32)).astype(x.dtype)

def _modulate(h, shift, scale):
    return h * (1.0 + scale) + shift

def _heads(t, n):
    B, T, _ = t.shape
    return t.reshape(B, T, n, -1).transpose(0, 2, 1, 3).astype(jnp.float32)

def _mlstm_chunk_states(k, v, log_i, log_f, state0):
    B, H, T, dk = k.shape
    dv = v.shape[-1]
    nc = T // CHUNK
    kc = k.reshape(B, H, nc, CHUNK, dk)
    vc = v.reshape(B, H, nc, CHUNK, dv)
    li = log_i.reshape(B, H, nc, CHUNK)
    b = jnp.cumsum(log_f.reshape(B, H, nc, CHUNK), axis=-1)
    b_tot = b[..., -1]
    g = b_tot[..., None] - b + li
    m_loc = jnp.max(g, axis=-1)
    w = jnp.exp(g - m_loc[..., None])
    C_loc = jnp.einsum('bhcs,bhcsv,bhcsk->bhcvk', w, vc, kc)
    n_loc = jnp.einsum('bhcs,bhcsk->bhck', w, kc)

    def step(state, xs):
        C, n, m = state
        bt, ml, Cl, nl = xs
        m_new = jnp.maximum(bt + m, ml)
        a = jnp.exp(bt + m - m_new)
        e = jnp.exp(ml - m_new)
        C_new = a[..., None, None] * C + e[..., None, None] * Cl
        n_new = a[..., None] * n + e[..., None] * nl
        return (C_new, n_new, m_new), (C, n, m)

    xs = (jnp.moveaxis(b_tot, 2, 0), jnp.moveaxis(m_loc, 2, 0),
          jnp.moveaxis(C_loc, 2, 0), jnp.moveaxis(n_loc, 2, 0))
    final, prev = lax.scan(step, state0, xs)
    prev = (jnp.moveaxis(prev[0], 0, 2), jnp.moveaxis(prev[1], 0, 2), jnp.moveaxis(prev[2], 0, 2))
    return prev, final

def _mlstm_chunk_outputs(q, k, v, log_i, log_f, prev):
    C_prev, n_prev, m_prev = prev
    B, H, T, dk = q.shape
    dv = v.shape[-1]
    nc = T // CHUNK
    qc = q.reshape(B, H, nc, CHUNK, dk)
    kc = k.reshape(B, H, nc, CHUNK, dk)
    vc = v.reshape(B, H, nc, CHUNK, dv)
    li = log_i.reshape(B, H, nc, CHUNK)
    b = jnp.cumsum(log_f.reshape(B, H, nc, CHUNK), axis=-1)
    lower = jnp.tril(jnp.ones((CHUNK, CHUNK), dtype=bool))
    log_d = jnp.where(lower, b[..., :, None] - b[..., None, :] + li[..., None, :], -jnp.inf)
    a = b + m_prev[..., None]
    m_t = jnp.maximum(a, jnp.max(log_d, axis=-1))
    s = jnp.einsum('bhctk,bhcsk->bhcts', qc, kc) * jnp.exp(log_d - m_t[..., None])
    e_int = jnp.exp(a - m_t)
    num = (jnp.einsum('bhcts,bhcsv->bhctv', s, vc)
           + e_int[..., None] * jnp.einsum('bhcvk,bhctk->bhctv', C_prev, qc))
    den = jnp.sum(s, axis=-1) + e_int * jnp.einsum('bhck,bhctk->bhct', n_prev, qc)
    h = num / jnp.maximum(jnp.abs(den), jnp.exp(-m_t))[..., None]
    return h.reshape(B, H, T, dv)

def _mlstm_direction(q, k, v, log_i, log_f, state0, reverse, want_out):
    if reverse:
        q, k, v = jnp.flip(q, 2), jnp.flip(k, 2), jnp.flip(v, 2)
        log_i, log_f = jnp.flip(log_i, 2), jnp.flip(log_f, 2)
    prev, final = _mlstm_chunk_states(k, v, log_i, log_f, state0)
    h = None
    if want_out:
        h = _mlstm_chunk_outputs(q, k, v, log_i, log_f, prev)
        if reverse:
            h = jnp.flip(h, 2)
    return h, final

def _mlstm_bidir(q, k, v, gates, states0, want_out):
    h_f, s_f = _mlstm_direction(q, k, v, gates[:, 0], jax.nn.log_sigmoid(gates[:, 1]),
                                states0[0], False, want_out)
    h_b, s_b = _mlstm_direction(q, k, v, gates[:, 2], jax.nn.log_sigmoid(gates[:, 3]),
                                states0[1], True, want_out)
    h = h_f + h_b if want_out else None
    return h, (s_f, s_b)

def _project(h, w_in, b_in, b_gate):
    B, T, _ = h.shape
    z = h @ w_in + b_in
    q, k, v, o, gt, ga, gb = jnp.split(z, IN_SPLITS, axis=-1)
    q = _heads(q, M_HEADS)
    k = _heads(k, M_HEADS) * (QK_DIM ** -0.5)
    v = _heads(v, M_HEADS)
    gates = (gt.reshape(B, T, 4, M_HEADS).transpose(0, 2, 3, 1).astype(jnp.float32)
             + b_gate.astype(jnp.float32)[None, :, :, None])
    u = ga * jax.nn.sigmoid(gb)
    return (q, k, v, gates), o, u

def _mlstm_group_out(h, o, norm_g):
    B, H, T, dv = h.shape
    hn = h * lax.rsqrt(jnp.mean(h * h, axis=-1, keepdims=True) + EPS) * norm_g.astype(jnp.float32)[:, None, :]
    return hn.transpose(0, 2, 1, 3).reshape(B, T, H * dv).astype(o.dtype) * jax.nn.sigmoid(o)

def _conv_group_out(u, conv_w, conv_b, ln_g, ln_b, rows):
    B, T, C = u.shape
    lhs = u.reshape(B * rows, T // rows, C)
    y = lax.conv_general_dilated(lhs, conv_w.astype(u.dtype)[:, None, :], (1,), 'SAME',
                                 dimension_numbers=('NWC', 'WIO', 'NWC'), feature_group_count=C)
    y = y.reshape(B, T, C) + conv_b
    return jax.nn.silu(_layer_norm(y, ln_g, ln_b))

def _token_mixer(hx, hc, w_in, b_in, b_gate, norm_g, conv_w, conv_b, ln_g, ln_b, w_out, b_out, ctx_out):
    B = hx.shape[0]
    rows = hx.shape[1] // GRID_W
    mx_in, ox, ux = _project(hx, w_in, b_in, b_gate)
    mc_in, oc, uc = _project(hc, w_in, b_in, b_gate)
    zero = (jnp.zeros((B, M_HEADS, V_DIM, QK_DIM), jnp.float32),
            jnp.zeros((B, M_HEADS, QK_DIM), jnp.float32),
            jnp.zeros((B, M_HEADS), jnp.float32))
    hc_m, ctx_states = _mlstm_bidir(*mc_in, (zero, zero), ctx_out)
    hx_m, _ = _mlstm_bidir(*mx_in, ctx_states, True)
    yx = jnp.concatenate([_mlstm_group_out(hx_m, ox, norm_g),
                          _conv_group_out(ux, conv_w, conv_b, ln_g, ln_b, rows)], axis=-1) @ w_out + b_out
    yc = None
    if ctx_out:
        yc = jnp.concatenate([_mlstm_group_out(hc_m, oc, norm_g),
                              _conv_group_out(uc, conv_w, conv_b, ln_g, ln_b, 1)], axis=-1) @ w_out + b_out
    return yx, yc

def _moe_ffn(h, w_router, b_router, we_gate, we_up, we_down, ws_gate, ws_up, ws_down):
    B, T, D = h.shape
    hf = h.reshape(-1, D)
    nt = hf.shape[0]
    s = jax.nn.sigmoid((hf @ w_router).astype(jnp.float32))
    _, idx = lax.top_k(s + b_router.astype(jnp.float32), TOP_K)
    s_sel = jnp.take_along_axis(s, idx, axis=-1)
    wts = s_sel / jnp.sum(s_sel, axis=-1, keepdims=True) * ROUTE_SCALE
    n_assign = nt * TOP_K
    e_flat = idx.reshape(-1)
    tok_flat = jnp.repeat(jnp.arange(nt, dtype=jnp.int32), TOP_K)
    order = jnp.argsort(e_flat)
    e_s, tok_s, w_s = e_flat[order], tok_flat[order], wts.reshape(-1)[order]
    counts = jnp.bincount(e_flat, length=N_EXPERTS)
    starts = jnp.cumsum(counts) - counts
    padded = (counts + EXPERT_BLOCK - 1) // EXPERT_BLOCK * EXPERT_BLOCK
    pend = jnp.cumsum(padded)
    pstarts = pend - padded
    dest = pstarts[e_s] + (jnp.arange(n_assign, dtype=jnp.int32) - starts[e_s])
    n_rows = -(-(n_assign + N_EXPERTS * (EXPERT_BLOCK - 1)) // EXPERT_BLOCK) * EXPERT_BLOCK
    n_blocks = n_rows // EXPERT_BLOCK
    row_tok = jnp.full((n_rows,), nt, jnp.int32).at[dest].set(tok_s)
    row_w = jnp.zeros((n_rows,), jnp.float32).at[dest].set(w_s)
    block_e = jnp.minimum(jnp.searchsorted(pend, jnp.arange(n_blocks) * EXPERT_BLOCK, side='right'),
                          N_EXPERTS - 1)
    hpad = jnp.concatenate([hf, jnp.zeros((1, D), hf.dtype)], axis=0)

    def body(acc, xs):
        rows, rw, e = xs
        xb = hpad[rows]
        y = (jax.nn.silu(xb @ we_gate[e]) * (xb @ we_up[e])) @ we_down[e]
        return acc.at[rows].add(y * rw[:, None].astype(y.dtype)), None

    acc, _ = lax.scan(body, jnp.zeros((nt + 1, D), hf.dtype),
                      (row_tok.reshape(n_blocks, EXPERT_BLOCK), row_w.reshape(n_blocks, EXPERT_BLOCK), block_e))
    shared = (jax.nn.silu(hf @ ws_gate) * (hf @ ws_up)) @ ws_down
    return (acc[:nt] + shared).reshape(B, T, D)

def first_inputs(seed: int = 0) -> dict:
    key = jax.random.key(seed)
    ks = jax.random.split(key, 32)

    def nrm(k, shape, scale):
        return jax.random.normal(k, shape, jnp.float32) * scale

    D = D_MODEL
    b_gate = jnp.stack([nrm(ks[12], (DEPTH, M_HEADS), 0.1),
                        3.0 + 3.0 * jax.random.uniform(ks[13], (DEPTH, M_HEADS), jnp.float32),
                        nrm(ks[14], (DEPTH, M_HEADS), 0.1),
                        3.0 + 3.0 * jax.random.uniform(ks[15], (DEPTH, M_HEADS), jnp.float32)], axis=1)
    return {
        "x": nrm(ks[0], (BATCH, SEQ, D), 1.0),
        "c": nrm(ks[1], (BATCH, D), 1.0),
        "ctx": nrm(ks[2], (BATCH, CTX_LEN, D), 1.0),
        "c_ctx": nrm(ks[3], (D,), 1.0),
        "w_ada": nrm(ks[4], (DEPTH, D, 6 * D), 0.5 * D ** -0.5),
        "b_ada": nrm(ks[5], (DEPTH, 6 * D), 0.02),
        "g_pre_mix": 1.0 + nrm(ks[6], (DEPTH, D), 0.1),
        "g_post_mix": 1.0 + nrm(ks[7], (DEPTH, D), 0.1),
        "g_pre_ffn": 1.0 + nrm(ks[8], (DEPTH, D), 0.1),
        "g_post_ffn": 1.0 + nrm(ks[9], (DEPTH, D), 0.1),
        "w_in": nrm(ks[10], (DEPTH, D, D_IN), D ** -0.5),
        "b_in": nrm(ks[11], (DEPTH, D_IN), 0.02),
        "b_gate": b_gate,
        "mlstm_norm_g": 1.0 + nrm(ks[16], (DEPTH, M_HEADS, V_DIM), 0.1),
        "conv_w": nrm(ks[17], (DEPTH, CONV_WIDTH, D_CONV), CONV_WIDTH ** -0.5),
        "conv_b": nrm(ks[18], (DEPTH, D_CONV), 0.02),
        "conv_ln_g": 1.0 + nrm(ks[19], (DEPTH, D_CONV), 0.1),
        "conv_ln_b": nrm(ks[20], (DEPTH, D_CONV), 0.02),
        "w_out": nrm(ks[21], (DEPTH, D_MIX, D), D_MIX ** -0.5),
        "b_out": nrm(ks[22], (DEPTH, D), 0.02),
        "w_router": nrm(ks[23], (DEPTH, D, N_EXPERTS), D ** -0.5),
        "b_router": nrm(ks[24], (DEPTH, N_EXPERTS), 0.01),
        "we_gate": nrm(ks[25], (DEPTH, N_EXPERTS, D, D_EXPERT), D ** -0.5),
        "we_up": nrm(ks[26], (DEPTH, N_EXPERTS, D, D_EXPERT), D ** -0.5),
        "we_down": nrm(ks[27], (DEPTH, N_EXPERTS, D_EXPERT, D), D_EXPERT ** -0.5),
        "ws_gate": nrm(ks[28], (DEPTH, D, D_SHARED), D ** -0.5),
        "ws_up": nrm(ks[29], (DEPTH, D, D_SHARED), D ** -0.5),
        "ws_down": nrm(ks[30], (DEPTH, D_SHARED, D), D_SHARED ** -0.5),
    }

def first_block(x, c, ctx, c_ctx, w_ada, b_ada, g_pre_mix, g_post_mix, g_pre_ffn, g_post_ffn,
              w_in, b_in, b_gate, mlstm_norm_g, conv_w, conv_b, conv_ln_g, conv_ln_b, w_out, b_out,
              w_router, b_router, we_gate, we_up, we_down, ws_gate, ws_up, ws_down):
    for l in range(DEPTH):
        ctx_out = l < DEPTH - 1
        mx = [t[:, None, :] for t in jnp.split(jax.nn.silu(c) @ w_ada[l] + b_ada[l], 6, axis=-1)]
        mc = jnp.split(jax.nn.silu(c_ctx) @ w_ada[l] + b_ada[l], 6, axis=-1)
        hx = _modulate(_rms_norm(x, g_pre_mix[l]), mx[0], mx[1])
        hc = _modulate(_rms_norm(ctx, g_pre_mix[l]), mc[0], mc[1])
        yx, yc = _token_mixer(hx, hc, w_in[l], b_in[l], b_gate[l], mlstm_norm_g[l], conv_w[l], conv_b[l],
                              conv_ln_g[l], conv_ln_b[l], w_out[l], b_out[l], ctx_out)
        x = x + mx[2] * _rms_norm(yx, g_post_mix[l])
        hx = _modulate(_rms_norm(x, g_pre_ffn[l]), mx[3], mx[4])
        x = x + mx[5] * _rms_norm(_moe_ffn(hx, w_router[l], b_router[l], we_gate[l], we_up[l], we_down[l],
                                           ws_gate[l], ws_up[l], ws_down[l]), g_post_ffn[l])
        if ctx_out:
            ctx = ctx + mc[2] * _rms_norm(yc, g_post_mix[l])
            hc = _modulate(_rms_norm(ctx, g_pre_ffn[l]), mc[3], mc[4])
            ctx = ctx + mc[5] * _rms_norm(_moe_ffn(hc, w_router[l], b_router[l], we_gate[l], we_up[l], we_down[l],
                                                 ws_gate[l], ws_up[l], ws_down[l]), g_post_ffn[l])
    return x


N_HEADS = 8
HEAD_DIM = 64
ATTN_WIDTH = N_HEADS * HEAD_DIM
MOBA_BLOCK = 256
MOBA_TOPK = 3
MOBA_Q_CHUNK = 64
POOL_WINDOWS = (2, 4, 8, 16)
POOL_GROUPS = len(POOL_WINDOWS)
POOL_WIDTH = D_MODEL // 2
POOL_GROUP_WIDTH = POOL_WIDTH // POOL_GROUPS
N_BRANCHES = 2
IN_WIDTH = 3 * ATTN_WIDTH + POOL_WIDTH + N_BRANCHES * D_MODEL
REL_BUCKETS = 32
REL_MAX_DIST = 128
N_EXPERT_GROUPS = 4
EXPERTS_PER_GROUP = 8
N_EXPERTS_2 = N_EXPERT_GROUPS * EXPERTS_PER_GROUP
EXPERT_TOPK = 2
D_EXPERT_2 = D_MODEL // 2
N_MOD = 6
NEG_INF = -1e30


def rms_norm(x, g):
    xf = x.astype(jnp.float32)
    xf = xf * lax.rsqrt(jnp.mean(xf * xf, axis=-1, keepdims=True) + EPS)
    return (xf * g.astype(jnp.float32)).astype(x.dtype)

def t5_bucket(rel):
    n = jnp.maximum(rel, 0)
    max_exact = REL_BUCKETS // 2
    nf = jnp.maximum(n, 1).astype(jnp.float32)
    large = max_exact + (jnp.log(nf / max_exact) / math.log(REL_MAX_DIST / max_exact)
                         * (REL_BUCKETS - max_exact)).astype(jnp.int32)
    large = jnp.minimum(large, REL_BUCKETS - 1)
    return jnp.where(n < max_exact, n, large)

def moba_attention(q, k, v, rel_bias):
    B, S, H, Dh = q.shape
    nb = -(-S // MOBA_BLOCK)
    pad = nb * MOBA_BLOCK - S
    topk = min(MOBA_TOPK, nb)
    scale = Dh ** -0.5
    qh = q.transpose(0, 2, 1, 3)
    kp = jnp.pad(k.transpose(0, 2, 1, 3), ((0, 0), (0, 0), (0, pad), (0, 0)))
    vp = jnp.pad(v.transpose(0, 2, 1, 3), ((0, 0), (0, 0), (0, pad), (0, 0)))
    kb = kp.reshape(B, H, nb, MOBA_BLOCK, Dh)
    vb = vp.reshape(B, H, nb, MOBA_BLOCK, Dh)
    k_mean = jnp.mean(kb.astype(jnp.float32), axis=3)
    bias_t = rel_bias.T
    b_idx = jnp.arange(B)[:, None, None, None]
    h_idx = jnp.arange(H)[None, :, None, None]
    h_idx5 = jnp.arange(H)[None, :, None, None, None]
    blk_offsets = jnp.arange(MOBA_BLOCK)

    def attend_chunk(ci):
        q0 = ci * MOBA_Q_CHUNK
        blk = q0 // MOBA_BLOCK
        qc = lax.dynamic_slice_in_dim(qh, q0, MOBA_Q_CHUNK, axis=2)
        qpos = q0 + jnp.arange(MOBA_Q_CHUNK)
        gate = jnp.einsum('bhqd,bhnd->bhqn', qc.astype(jnp.float32), k_mean)
        gate = jnp.where(jnp.arange(nb) < blk, gate, -jnp.inf)
        _, sel = lax.top_k(gate, topk)
        sel_valid = sel < blk
        ks = kb[b_idx, h_idx, sel]
        vs = vb[b_idx, h_idx, sel]
        s_sel = jnp.einsum('bhqd,bhqjkd->bhqjk', qc, ks).astype(jnp.float32) * scale
        kpos_sel = sel[..., None] * MOBA_BLOCK + blk_offsets
        bucket_sel = t5_bucket(qpos[None, None, :, None, None] - kpos_sel)
        s_sel = s_sel + bias_t[h_idx5, bucket_sel].astype(jnp.float32)
        s_sel = jnp.where(sel_valid[..., None], s_sel, NEG_INF)
        ko = lax.dynamic_index_in_dim(kb, blk, axis=2, keepdims=False)
        vo = lax.dynamic_index_in_dim(vb, blk, axis=2, keepdims=False)
        s_own = jnp.einsum('bhqd,bhkd->bhqk', qc, ko).astype(jnp.float32) * scale
        rel_own = qpos[:, None] - (blk * MOBA_BLOCK + blk_offsets)[None, :]
        s_own = s_own + bias_t[:, t5_bucket(rel_own)][None].astype(jnp.float32)
        s_own = jnp.where(rel_own >= 0, s_own, NEG_INF)
        logits = jnp.concatenate(
            [s_sel.reshape(B, H, MOBA_Q_CHUNK, topk * MOBA_BLOCK), s_own], axis=-1)
        p = jax.nn.softmax(logits, axis=-1).astype(v.dtype)
        p_sel = p[..., :topk * MOBA_BLOCK].reshape(B, H, MOBA_Q_CHUNK, topk, MOBA_BLOCK)
        p_own = p[..., topk * MOBA_BLOCK:]
        return (jnp.einsum('bhqjk,bhqjkd->bhqd', p_sel, vs)
                + jnp.einsum('bhqk,bhkd->bhqd', p_own, vo))

    out = lax.map(attend_chunk, jnp.arange(S // MOBA_Q_CHUNK))
    return out.transpose(1, 0, 3, 2, 4).reshape(B, S, H * Dh)

def pool_mixer(u, pool_w, pool_scale):
    B, S, P = u.shape
    uf = u.astype(jnp.float32)
    cs = jnp.pad(jnp.cumsum(uf, axis=1), ((0, 0), (1, 0), (0, 0)))
    t = jnp.arange(S)
    outs = []
    for g, w in enumerate(POOL_WINDOWS):
        lo_c, hi_c = g * POOL_GROUP_WIDTH, (g + 1) * POOL_GROUP_WIDTH
        csg = cs[..., lo_c:hi_c]
        lo = jnp.maximum(t + 1 - w, 0)
        cnt = (t + 1 - lo).astype(jnp.float32)
        mean = (csg[:, 1:] - csg[:, lo]) / cnt[None, :, None]
        d = (mean - uf[..., lo_c:hi_c]).astype(u.dtype)
        outs.append(jnp.einsum('bsc,cd->bsd', d, pool_w[g]))
    return jnp.concatenate(outs, axis=-1) * pool_scale

def hier_moe(h, w_rg, b_rg, w_re, b_re, w_g, w_u, w_d):
    B, S, D = h.shape
    N = B * S
    hf = h.reshape(N, D)
    z_group = (hf @ w_rg).astype(jnp.float32) + b_rg.astype(jnp.float32)
    p_group = jax.nn.softmax(z_group, axis=-1)
    pg_top, g_idx = lax.top_k(p_group, 1)
    z_exp = ((hf @ w_re).astype(jnp.float32) + b_re.astype(jnp.float32)).reshape(
        N, N_EXPERT_GROUPS, EXPERTS_PER_GROUP)
    z_in_group = z_exp[jnp.arange(N), g_idx[:, 0]]
    ze_top, e_idx = lax.top_k(z_in_group, EXPERT_TOPK)
    weights = pg_top * jax.nn.softmax(ze_top, axis=-1)
    expert_id = g_idx * EXPERTS_PER_GROUP + e_idx
    combine = jnp.einsum('nk,nke->ne', weights,
                         jax.nn.one_hot(expert_id, N_EXPERTS_2, dtype=jnp.float32)).astype(h.dtype)
    y = jnp.zeros_like(hf)
    for e in range(N_EXPERTS_2):
        act = jax.nn.silu(hf @ w_g[e]) * (hf @ w_u[e])
        y = y + combine[:, e:e + 1] * (act @ w_d[e])
    return y.reshape(B, S, D)

def second_inputs(seed: int = 0) -> dict:
    key = jax.random.key(seed)
    ks = jax.random.split(key, 22)
    f32 = jnp.float32
    D = D_MODEL
    PGW = POOL_GROUP_WIDTH

    def nrm(k, shape, s):
        return jax.random.normal(k, shape, f32) * s

    return {
        "x": nrm(ks[0], (BATCH, SEQ, D), 1.0),
        "c": nrm(ks[1], (BATCH, D), 1.0),
        "w_ada": nrm(ks[2], (DEPTH, D, N_MOD * D), 0.5 * D ** -0.5),
        "b_ada": nrm(ks[3], (DEPTH, N_MOD * D), 0.02),
        "norm1_g": 1.0 + nrm(ks[4], (DEPTH, D), 0.05),
        "w_in": nrm(ks[5], (DEPTH, D, IN_WIDTH), D ** -0.5),
        "b_gate": nrm(ks[6], (DEPTH, N_BRANCHES * D), 0.02),
        "rel_bias": nrm(ks[7], (REL_BUCKETS, N_HEADS), 0.5),
        "pool_w": nrm(ks[8], (DEPTH, POOL_GROUPS, PGW, PGW), PGW ** -0.5),
        "pool_scale": 1.0 + nrm(ks[9], (DEPTH, POOL_WIDTH), 0.1),
        "w_branch_attn": nrm(ks[10], (DEPTH, ATTN_WIDTH, D), ATTN_WIDTH ** -0.5),
        "w_branch_pool": nrm(ks[11], (DEPTH, POOL_WIDTH, D), POOL_WIDTH ** -0.5),
        "w_out": nrm(ks[12], (DEPTH, D, D), D ** -0.5),
        "norm2_g": 1.0 + nrm(ks[13], (DEPTH, D), 0.05),
        "w_router_group": nrm(ks[14], (DEPTH, D, N_EXPERT_GROUPS), D ** -0.5),
        "b_router_group": nrm(ks[15], (DEPTH, N_EXPERT_GROUPS), 0.01),
        "w_router_expert": nrm(ks[16], (DEPTH, D, N_EXPERTS_2), D ** -0.5),
        "b_router_expert": nrm(ks[17], (DEPTH, N_EXPERTS_2), 0.01),
        "w_expert_gate": nrm(ks[18], (DEPTH, N_EXPERTS_2, D, D_EXPERT_2), D ** -0.5),
        "w_expert_up": nrm(ks[19], (DEPTH, N_EXPERTS_2, D, D_EXPERT_2), D ** -0.5),
        "w_expert_down": nrm(ks[20], (DEPTH, N_EXPERTS_2, D_EXPERT_2, D), D_EXPERT_2 ** -0.5),
        "norm_f_g": 1.0 + nrm(ks[21], (D,), 0.05),
    }

def second_block(x, c, w_ada, b_ada, norm1_g, w_in, b_gate, rel_bias, pool_w, pool_scale,
              w_branch_attn, w_branch_pool, w_out, norm2_g, w_router_group, b_router_group,
              w_router_expert, b_router_expert, w_expert_gate, w_expert_up, w_expert_down,
              norm_f_g):
    B, S, D = x.shape
    c_act = jax.nn.silu(c)
    split_pts = [ATTN_WIDTH, 2 * ATTN_WIDTH, 3 * ATTN_WIDTH, 3 * ATTN_WIDTH + POOL_WIDTH]
    for l in range(DEPTH):
        mod = (c_act @ w_ada[l] + b_ada[l])[:, None, :]
        shift1, scale1, gate1, shift2, scale2, gate2 = jnp.split(mod, N_MOD, axis=-1)
        h = rms_norm(x, norm1_g[l]) * (1 + scale1) + shift1
        proj = h @ w_in[l]
        q, k, v, u, z_gate = jnp.split(proj, split_pts, axis=-1)
        q = q.reshape(B, S, N_HEADS, HEAD_DIM)
        k = k.reshape(B, S, N_HEADS, HEAD_DIM)
        v = v.reshape(B, S, N_HEADS, HEAD_DIM)
        y_attn = moba_attention(q, k, v, rel_bias) @ w_branch_attn[l]
        y_pool = pool_mixer(u, pool_w[l], pool_scale[l]) @ w_branch_pool[l]
        g_attn, g_pool = jnp.split(jax.nn.sigmoid(z_gate + b_gate[l]), N_BRANCHES, axis=-1)
        mixed = (g_attn * y_attn + g_pool * y_pool) @ w_out[l]
        x = x + gate1 * mixed
        h2 = rms_norm(x, norm2_g[l]) * (1 + scale2) + shift2
        y_moe = hier_moe(h2, w_router_group[l], b_router_group[l], w_router_expert[l],
                         b_router_expert[l], w_expert_gate[l], w_expert_up[l], w_expert_down[l])
        x = x + gate2 * y_moe
    return rms_norm(x, norm_f_g)


def setup_inputs(seed=0):
    out = dict(first_inputs(seed))
    for name, value in second_inputs(seed + 1).items():
        if name != "x":
            out[name + "_2"] = value
    return out


def reference(
    x, c, ctx, c_ctx, w_ada, b_ada, g_pre_mix, g_post_mix, g_pre_ffn, g_post_ffn, w_in, b_in,
    b_gate, mlstm_norm_g, conv_w, conv_b, conv_ln_g, conv_ln_b, w_out, b_out, w_router,
    b_router, we_gate, we_up, we_down, ws_gate, ws_up, ws_down, c_2, w_ada_2, b_ada_2,
    norm1_g_2, w_in_2, b_gate_2, rel_bias_2, pool_w_2, pool_scale_2, w_branch_attn_2,
    w_branch_pool_2, w_out_2, norm2_g_2, w_router_group_2, b_router_group_2, w_router_expert_2,
    b_router_expert_2, w_expert_gate_2, w_expert_up_2, w_expert_down_2, norm_f_g_2,
):
    x = first_block(
        x, c, ctx, c_ctx, w_ada, b_ada, g_pre_mix, g_post_mix, g_pre_ffn, g_post_ffn, w_in,
        b_in, b_gate, mlstm_norm_g, conv_w, conv_b, conv_ln_g, conv_ln_b, w_out, b_out,
        w_router, b_router, we_gate, we_up, we_down, ws_gate, ws_up, ws_down,
    )
    return second_block(
        x, c_2, w_ada_2, b_ada_2, norm1_g_2, w_in_2, b_gate_2, rel_bias_2, pool_w_2,
        pool_scale_2, w_branch_attn_2, w_branch_pool_2, w_out_2, norm2_g_2, w_router_group_2,
        b_router_group_2, w_router_expert_2, b_router_expert_2, w_expert_gate_2, w_expert_up_2,
        w_expert_down_2, norm_f_g_2,
    )


_drawn_inputs = setup_inputs


def setup_inputs(seed=0):
    import zlib

    import numpy as np

    out = dict(_drawn_inputs(seed))
    spreads = {}
    factors = {'conv_b': 2.822,
     'conv_ln_b': 3.227,
     'b_ada_2': 3.428,
     'norm1_g_2': 5.169,
     'b_gate_2': 8.0,
     'rel_bias_2': 3.337,
     'pool_scale_2': 3.667,
     'norm2_g_2': 3.53,
     'b_router_group_2': 8.0,
     'b_router_expert_2': 8.0}
    for name, (base, spread) in spreads.items():
        noise = np.random.default_rng([zlib.crc32(name.encode()), seed]).standard_normal(out[name].shape)
        drawn = base * np.exp(spread * noise) if base else spread * noise
        out[name] = jnp.asarray(drawn.astype(out[name].dtype))
    for name, factor in factors.items():
        out[name] = (out[name] * factor).astype(out[name].dtype)
    return out
```

```python
import concourse.bass as bass
from concourse import mybir
from contextlib import ExitStack
import numpy as np

F32 = mybir.dt.float32
BF16 = mybir.dt.bfloat16
I32 = mybir.dt.int32
ALU = mybir.AluOpType
ACT = mybir.ActivationFunctionType
AX_X = mybir.AxisListType.X

P = 128
T = 256
NB = T // P
D = 1024
KD = D // P
EPS = 1e-6
NEG = -1e30

HEADS, DK, DV = 4, 64, 128
TAPS, CONV_C, ROW, ROWS = 31, 512, 64, 4
HALO = TAPS // 2
E1, F1, TOP1, ROUTE_SCALE = 64, 256, 8, 2.5
HEADS2, DH2 = 8, 64
POOL_WINDOWS = (2, 4, 8, 16)
GROUPS2, PER_GROUP2, E2, F2 = 4, 8, 32, 512
BUCKETS, MAX_DIST = 32, 128

G1, G2 = 2, 4
CAP1, CAP2 = P // G1, P // G2
NG1, NG2 = E1 // G1, E2 // G2
OVER1, OVER2 = T * TOP1 // (CAP1 + 1), T * 2 // (CAP2 + 1)

BUFN = 8192
ITEMS = ["ada0", "ada1", "in_qkv", "in_og", "in_conv", "ada2", "ada3", "ada4", "ada5",
         "adb0", "adb1", "adb2", "adb3", "adb4", "adb5", "w_out", "shared"]
AT = {n: i for i, n in enumerate(ITEMS)}
ITEMS2 = ["in2_qk", "in2_vu", "in2_ga", "in2_gp", "branches", "w_out2"]
AT2 = {n: i for i, n in enumerate(ITEMS2)}

C_C, C_CTX, C_2, C_GPRE, C_GFFN, C_N1, C_N2 = 0, 8, 16, 24, 32, 40, 48
C_CONVB, C_LNG, C_LNB, C_POOLS, C_BQK, C_BCONV, N_COLS = 56, 60, 64, 68, 72, 76, 84

STATE_CHUNK = ((2, 3), (3, 2), (0, 1))
ADA = [n for n in ITEMS if n[:2] == "ad"]
ada_done = [sum(2 if n[3] in "25" else 1 for n in ADA[:k]) for k in range(len(ADA) + 1)]


def shape_constants():
    i = np.arange(T + P - 1)
    dist = np.maximum(T - 1 - i, 0)
    exact = BUCKETS // 2
    nf = np.maximum(dist, 1).astype(np.float32)
    large = exact + (np.log(nf / np.float32(exact)) / np.float32(np.log(MAX_DIST / exact))
                     * np.float32(BUCKETS - exact)).astype(np.int32)
    bucket = np.where(dist < exact, dist, np.minimum(large, BUCKETS - 1))
    onehot = (bucket[None, :] == np.arange(BUCKETS)[:, None]).astype(np.float32)
    s, t = np.arange(T)[:, None], np.arange(T)[None, :]
    band = np.stack([((s <= t) & (s > t - w)) / np.minimum(t + 1, w) - (s == t) for w in POOL_WINDOWS])
    return {"bucket": onehot, "band": band.astype(np.float32)}


class Steps:

    def __init__(self, eng, own):
        self.eng, self.own, self.n = eng, own, {}

    def __call__(self, ins, sem=None, wait=True):
        sem = self.own if sem is None else sem
        self.n[sem] = self.n.get(sem, 0) + 1
        ins.then_inc(sem, 1)
        if wait:
            self.eng.wait_ge(sem, self.n[sem])


class Sems(dict):

    def __init__(self, nc, ctx):
        self.nc, self.ctx = nc, ctx

    def __missing__(self, name):
        self[name] = self.ctx.enter_context(self.nc.semaphore(name))
        return self[name]


def outer(ap, n):
    return ap.unsqueeze(1).to_broadcast([ap.shape[0], n, ap.shape[1]])


def inner(ap, n):
    return ap.unsqueeze(2).to_broadcast([ap.shape[0], ap.shape[1], n])


def two_block_network(nc, A, out):
    ctx = ExitStack()
    with ctx:
        S = Sems(nc, ctx)
        bias_dram = nc.dram_tensor("bias_by_distance", (HEADS2, T + P - 1), F32).ap()

        def sb(name, shape, dt=F32):
            return ctx.enter_context(nc.sbuf_tensor(name, shape, dt))

        W = sb("W", [P, 3 * BUFN])
        BUF = [W[:, i * BUFN:(i + 1) * BUFN] for i in range(3)]
        x = sb("x", [P, NB, D])
        hT = sb("hT", [P, KD, T])
        xn = sb("xn", [P, NB, D])
        gate = sb("gate", [P, 2, D])
        gate2 = sb("gate2", [P, 2, D])
        cols = sb("cols", [P, N_COLS])
        adab = sb("adab", [P, 2, 48])
        convw = sb("convw", [P, TAPS * 4])
        sc = sb("sc", [P, KD, 32])
        modc = sb("modc", [P, 2, 4, KD, 3])
        ada_rows = sb("ada_rows", [P, D])
        ident = sb("ident", [P, P])
        ones = sb("ones", [P, P])
        zeros = sb("zeros", [P, P])
        tri = sb("tri", [P, 2, P])
        iota = sb("iota", [P, P])
        sel3 = sb("sel3", [P, 3])
        selrow = sb("selrow", [P, 2, P])
        small = sb("small", [P, 480])
        flip = sb("flip", [P, P])
        brt = sb("brt", [P, 104])
        am = sb("am", [P, 2, KD])

        NS = 14784
        scr = sb("scr", [P, NS])

        class Carve:
            def __init__(self, base=0):
                self.at = base

            def __call__(self, *shape, dt=F32):
                n = int(np.prod(shape))
                words = n if dt != BF16 else (n + 1) // 2
                ap = scr[:, self.at:self.at + words]
                self.at += words
                assert self.at <= NS, self.at
                if dt != F32:
                    ap = ap.bitcast(dt)
                if len(shape) == 1:
                    return ap
                names = "abcde"[:len(shape)]
                kw = {c: s for c, s in zip(names[1:], shape[1:])}
                return ap.rearrange(f"p ({' '.join(names)}) -> p {' '.join(names)}", **kw)

        cv = Carve()
        hT_words = hT[:].rearrange("p a b -> p (a b)")
        ctxt = cv(NB, D)
        hTc = cv(KD, T)
        hTc_words = hTc.rearrange("p a b -> p (a b)")
        qT = cv(2, T)
        kT = cv(2, T)
        knat = cv(4, 256)
        v1 = cv(4, HEADS, DV + 1)
        osig = cv(NB, 512)
        upad = cv(4, ROWS, ROW + 2 * HALO)
        rowb = cv(1296)
        normg = cv(512)
        G = cv(4, 16)
        LF = cv(4, 2, 4)
        lft = cv(4, 2, 4)
        wst = cv(32)
        mneg = cv(2, P)
        mbig = cv(2, P)
        convt = cv(2, T)
        rowv = cv(D)
        vecs = hTc_words[:, 0:3 * P].rearrange("p (c n) -> p c n", c=3)
        relb = hTc_words[0:BUCKETS, 400:408]
        onehot = hTc_words[0:BUCKETS, 512:512 + T + P - 1]
        biasrow = hTc_words[0:HEADS2, 1024:1024 + T + P - 1]
        mixT = ctxt.rearrange("p a b -> p (a b)").rearrange("p (k t) -> p k t", k=KD)
        kw = hTc_words[:, 0:6 * 256].rearrange("p (c n) -> p c n", c=6)
        dt4 = hTc_words[:, 1536:2048].rearrange("p (h t) -> p h t", h=HEADS)
        diag = hT_words[:, 0:1024].rearrange("p (b h t) -> p b h t", b=2, h=HEADS)
        cacc = hT_words[:, 1024:2048].rearrange("p (c t) -> p c t", c=4)
        hm = xn[:, 0, :].rearrange("p (b n) -> p b n", b=NB)
        qk = xn[:, 1, :].rearrange("p (c h t) -> p c h t", c=2, h=HEADS)
        usig = xn[:, 1, :].rearrange("p (c t) -> p c t", c=4)
        state = rowb[:, 0:1032].rearrange("p (w d h n) -> p w d h n", w=2, d=2, h=2)
        stmp = rowb[:, 1032:1290].rearrange("p (h n) -> p h n", h=2)
        knat_words = knat.rearrange("p a b -> p (a b)")
        nd = knat_words[:, 0:516].rearrange("p (h n) -> p h n", h=HEADS)
        gsq = knat_words.rearrange("p (g n) -> p g n", n=P)
        ctmp = upad.rearrange("p a b c -> p (a b c)")[:, 0:1024].rearrange("p (c t) -> p c t", c=4)
        iota_i = convt[:, 0, 0:P].bitcast(I32)
        cmean, crstd = convt[:, 0, :], convt[:, 1, :]

        r_ = small[:, 0:32]
        b_ = small[:, 32:64]
        bt_ = small[:, 64:96]
        rmax = small[:, 96:128]
        cmax = small[:, 128:144]
        m_t = small[:, 144:160]
        m_run = small[:, 160:192]
        mx_ = small[:, 192:200]
        dae = small[:, 200:248]
        ae2 = small[:, 248:272]
        ee = small[:, 272:304]
        den = small[:, 304:308]
        st = small[:, 308:340]
        onec = small[:, 340:341]
        zeroc = small[:, 341:342]

        rowd = {"b_mix": scr[:, 4096:5120], "post_mix": scr[:, 5120:6144], "b_ffn": scr[:, 6144:7168],
                "post_ffn": scr[:, 7168:8192], "b_mix2": scr[:, 8208:9232], "b_ffn2": hT_words[:, 0:1024]}

        ce = Carve()
        hs = ce(3, NB, D, dt=BF16)
        hTe = ce(KD, P)
        Sb = ce(NB, P, dt=BF16)
        Sw = ce(2, NB, P)
        Ct = ce(T)
        sg = ce(512)
        av = ce(512)
        aT = ce(4, P)
        Y = ce(D)
        mask = ce(NB, E1)
        wts = ce(NB, E1)
        rank = ce(NB, E1)
        sel = ce(NB, E1)
        tmpr = ce(NB, E1)
        max8 = ce(NB, 8)
        a_sh = ce(NB, F1)
        sg_sh = ce(NB, F1)
        aT_sh = ce(2, T)
        wr = ce(KD, E1)
        rt = ce(64)
        desc = ce(E1)
        over_row = tmpr.rearrange("p b e -> p (b e)")
        over_expert = over_row[:, 0:32].bitcast(I32)
        over_start = over_row[:, 32:64]
        over_pick = over_row[:, 64:96]
        over_idx, over_from, over_flag, over_place = (rt[:, c:c + 1] for c in (40, 41, 42, 43))
        over_shift = rt[:, 44:44 + NB]
        over_count = [small[:, 342 + n:343 + n].bitcast(I32) for n in range(2)]
        wr2 = wr.rearrange("p k n -> p (k n)")[:, 0:KD * 36].rearrange("p (k n) -> p k n", k=KD)

        c2 = Carve()
        qT2 = c2(4, T)
        kT2 = c2(4, T)
        vv2 = c2(NB, 512)
        u2 = c2(NB, 512)
        zg = c2(NB, 2 * D)
        oT2 = c2(4, T)
        dT2 = c2(4, T)
        plT2 = c2(4, T)
        poolw = c2(4, P)
        pexp = c2(2, 384)
        pT = c2(2, 384)
        TB = BUF[2][:, 0:2048].rearrange("p (h j) -> p h j", h=HEADS2)
        TBr = zg.rearrange("p b d -> p (b d)")[:, 0:2048].rearrange("p (h j) -> p h j", h=HEADS2)
        rowf = gate[:, 0, :]
        band = BUF[2][:, 2048:4096].rearrange("p (g s t) -> p g s t", g=4, s=NB)
        bgrow = BUF[2][:, 4096:6144]
        w2buf = [BUF[i % 2] for i in range(len(ITEMS2))]
        w2k = [w.rearrange("p (k n) -> p k n", k=KD) for w in w2buf]

        PS = [ctx.enter_context(nc.psum_tensor(f"PS{i}", [P, 512], F32)) for i in range(8)]

        def ada_item(n):
            return (0, int(n[3])) if n[:3] == "ada" else (1, int(n[3]))

        def is_gate(n):
            return ada_item(n)[1] in (2, 5)

        def col_at(n):
            s = ada_item(n)[1]
            return {0: 0, 1: 1, 3: 2, 4: 3}[s]

        gu1 = [BUF[s].rearrange("p (e k n) -> p e k n", e=G1, k=KD) for s in range(2)]
        dn1 = [BUF[2][:, s * 4096:(s + 1) * 4096].rearrange("p (e c n) -> p e c n", e=G1, c=2) for s in range(2)]
        gu2 = [BUF[s].rearrange("p (e k n) -> p e k n", e=G2, k=4) for s in range(3)]
        dn2 = [BUF[s].rearrange("p (e c n) -> p e c n", e=G2, c=2) for s in range(3)]

        wv = {n: BUF[i % 3] for n, i in AT.items()}
        ada_w = {n: wv[n].rearrange("p (k n) -> p k n", k=KD) for n in ITEMS if n[:3] in ("ada", "adb")}
        w_qkv = wv["in_qkv"].rearrange("p (k n) -> p k n", k=KD)
        w_og = wv["in_og"][:, 0:KD * 528].rearrange("p (k n) -> p k n", k=KD)
        w_conv = wv["in_conv"].rearrange("p (k n) -> p k n", k=KD)
        w_o = wv["w_out"].rearrange("p (k n) -> p k n", k=KD)
        sh_gu = wv["shared"][:, 0:4096].rearrange("p (k n) -> p k n", k=KD)
        sh_dn = wv["shared"][:, 4096:6144].rearrange("p (c n) -> p c n", c=2)

        def over_weights(F):
            return (BUF[0][:, 0:KD * F].rearrange("p (k n) -> p k n", k=KD), BUF[1][:, 0:KD * F].rearrange("p (k n) -> p k n", k=KD),
                    BUF[2][:, 0:F // P * D].rearrange("p (c n) -> p c n", c=F // P))

        def over_counts(eng, L):
            eng.wait_ge(S["over_known"], L)
            most = (OVER1, OVER2)[L - 1]
            count = eng.value_load(over_count[L - 1][0:1, :], min_val=0, max_val=most)
            return count, (eng.value_load(over_count[0][0:1, :], min_val=0, max_val=OVER1) if L == 2 else 0), most

        block = ctx.enter_context(nc.Block())

        @block.sync
        def _(sp):
            sp.dma_start(x[:], A["x"][0].rearrange("(b p) d -> p b d", p=P)).then_inc(S["x_loaded"], 16)
            sp.dma_start(ctxt, A["ctx"][0].rearrange("(b p) d -> p b d", p=P)).then_inc(S["ctx_loaded"], 16)

            def rows(ap):
                return ap.rearrange("(k p) n -> p k n", p=P)

            for n, i in AT.items():
                if i >= 3:
                    sp.wait_ge(S["stream_used"], i - 2)
                loaded = S[f"stream_loaded{i % 3}"]
                if n[:3] in ("ada", "adb"):
                    b, s = ada_item(n)
                    w = A["w_ada_2" if b else "w_ada"][0]
                    sp.dma_start(ada_w[n], rows(w[:, s * D:(s + 1) * D])).then_inc(loaded, 16)
                elif n == "in_qkv":
                    sp.dma_start(w_qkv, rows(A["w_in"][0][:, 0:1024])).then_inc(loaded, 16)
                elif n == "in_og":
                    sp.dma_start(w_og, rows(A["w_in"][0][:, 1024:1552])).then_inc(loaded, 16)
                elif n == "in_conv":
                    sp.dma_start(w_conv, rows(A["w_in"][0][:, 1552:2576])).then_inc(loaded, 16)
                elif n == "w_out":
                    sp.dma_start(w_o, rows(A["w_out"][0])).then_inc(loaded, 16)
                else:
                    sp.dma_start(sh_gu[:, :, 0:F1], rows(A["ws_gate"][0])).then_inc(loaded, 16)
                    sp.dma_start(sh_gu[:, :, F1:2 * F1], rows(A["ws_up"][0])).then_inc(loaded, 16)
                    sp.dma_start(sh_dn, rows(A["ws_down"][0])).then_inc(loaded, 16)
            def load_gu1(g, s):
                for e in range(G1):
                    dst = gu1[s][:, e, :, :]
                    sp.dma_start(dst[:, :, 0:F1], rows(A["we_gate"][0, g * G1 + e])).then_inc(S[f"e1_gu{s}"], 16)
                    sp.dma_start(dst[:, :, F1:2 * F1], rows(A["we_up"][0, g * G1 + e])).then_inc(S[f"e1_gu{s}"], 16)

            def load_dn1(g, s):
                for e in range(G1):
                    sp.dma_start(dn1[s][:, e, :, :], rows(A["we_down"][0, g * G1 + e])).then_inc(S[f"e1_dn{s}"], 16)

            sp.wait_ge(S["stream_used"], AT["w_out"] + 1)
            load_gu1(0, 0)
            load_dn1(0, 0)
            sp.wait_ge(S["stream_used"], AT["shared"] + 1)
            load_gu1(1, 1)
            load_dn1(1, 1)
            with sp.Fori(0, NG1 // 2 - 1) as i:
                for s in range(2):
                    sp.wait_ge(S["e1_gateup"], 2 * i + s + 1)
                    load_gu1(2 * i + 2 + s, s)
                    sp.wait_ge(S["e1_down"], 2 * i + s + 1)
                    load_dn1(2 * i + 2 + s, s)

            def over_loads(L, F, names):
                count, before, most = over_counts(sp, L)
                with sp.Fori(0, most) as i:
                    with sp.If(i < count):
                        expert = sp.value_load(over_expert[0:1, bass.ds(i, 1)], min_val=1, max_val=(E1, E2)[L - 1]) - 1
                        sp.wait_ge(S["over_done"], i + before + L)
                        for dst, name in zip(over_weights(F), names):
                            sp.dma_start(dst, rows(A[name][0, expert])).then_inc(S["over_loaded"], 16)
                return count

            count = over_loads(1, F1, ("we_gate", "we_up", "we_down"))
            with sp.If(count > 0):
                sp.wait_ge(S["y_done"], 1)

            for n, i in AT2.items():
                if i < 2:
                    sp.wait_ge(S["e1_gateup"], NG1 - 1 + i)
                else:
                    sp.wait_ge(S["stream2_used"], i - 1)
                loaded = S[f"stream2_loaded{i % 2}"]
                if i < 4:
                    sp.dma_start(w2k[i], rows(A["w_in_2"][0][:, i * D:(i + 1) * D])).then_inc(loaded, 16)
                elif n == "branches":
                    sp.dma_start(w2k[i][:, 0:4, :], rows(A["w_branch_attn_2"][0])).then_inc(loaded, 16)
                    sp.dma_start(w2k[i][:, 4:8, :], rows(A["w_branch_pool_2"][0])).then_inc(loaded, 16)
                else:
                    sp.dma_start(w2k[i], rows(A["w_out_2"][0])).then_inc(loaded, 16)
                if i == 0:
                    sp.wait_ge(S["e1_down"], NG1)
                    sp.dma_start(band, A["band"].rearrange("g (b p) t -> p g b t", p=P)).then_inc(S["band_loaded"], 16)
                    sp.dma_start(bgrow, A["b_gate_2"][0].partition_broadcast(P)).then_inc(S["band_loaded"], 16)

            def load2(g, q):
                kind, half = q // 2, q % 2
                w = A[("w_expert_gate_2", "w_expert_up_2", "w_expert_down_2")[kind]]
                for e in range(G2):
                    if kind < 2:
                        src = rows(w[0, g * G2 + e])[:, 4 * half:4 * half + 4, :]
                        dst = gu2[q % 3][:, e, :, :]
                    else:
                        src = rows(w[0, g * G2 + e])[:, 2 * half:2 * half + 2, :]
                        dst = dn2[q % 3][:, e, :, :]
                    sp.dma_start(dst, src).then_inc(S[f"e2_piece{q % 3}"], 16)

            sp.wait_ge(S["stream2_used"], 5)
            load2(0, 0)
            sp.wait_ge(S["pool_done"], 1)
            sp.wait_ge(S["attn_done"], 1)
            load2(0, 2)
            sp.wait_ge(S["stream2_used"], 6)
            load2(0, 1)
            for q in range(3, 6):
                sp.wait_ge(S["e2_gateup"], q - 2)
                load2(0, q)
            with sp.Fori(0, NG2 - 1) as g:
                for q in range(6):
                    if q < 1:
                        sp.wait_ge(S["e2_gateup"], 4 * g + 4)
                    elif q < 3:
                        sp.wait_ge(S["e2_down"], 2 * g + q)
                    else:
                        sp.wait_ge(S["e2_gateup"], 4 * g + 4 + q - 2)
                    load2(g + 1, q)

            over_loads(2, F2, ("w_expert_gate_2", "w_expert_up_2", "w_expert_down_2"))

            sp.wait_ge(S["out_ready"], 2)
            sp.dma_start(out[0].rearrange("(b p) d -> p b d", p=P), xn[:]).then_inc(S["stored"], 16)
            sp.wait_ge(S["stored"], 16)

        @block.gpsimd
        def _(pool):
            step = Steps(pool, S["pool_step"])
            g = nc.gpsimd
            step(g.memset(ones[:], 1.0), wait=False)
            step(g.memset(zeros[:], 0.0), wait=False)
            step(g.memset(ident[:], 0.0), wait=False)
            step(g.memset(mneg, 0.0), wait=False)
            step(g.memset(mbig, 0.0), wait=False)
            step(g.memset(sc[:], 0.0), wait=False)
            step(g.memset(onec, 1.0), wait=False)
            step(g.memset(zeroc, 0.0), wait=False)
            step(g.memset(upad, 0.0), wait=False)
            step(g.memset(v1[:, :, :, DV:DV + 1], 1.0))

            def keep(out_, in_, base, mult, stepf, fill, op=ALU.is_ge, wait=True):
                step(g.affine_select(out=out_, in_=in_, compare_op=op, fill=fill, base=base,
                                     pattern=[[stepf, P]], channel_multiplier=mult), wait=wait)

            keep(ident[:], ident[:], 0, 1, -1, 1.0, ALU.not_equal, wait=False)
            keep(tri[:, 0, :], ones[:], 0, -1, 1, 0.0, wait=False)
            keep(tri[:, 1, :], ones[:], 0, 1, -1, 0.0, wait=False)
            keep(mneg[:, 0, :], mneg[:, 0, :], 0, 1, -1, NEG, wait=False)
            keep(mneg[:, 1, :], mneg[:, 1, :], 0, -1, 1, NEG, wait=False)
            keep(mbig[:, 0, :], mbig[:, 0, :], 0, -1, 1, 1e4, wait=False)
            keep(mbig[:, 1, :], mbig[:, 1, :], 0, 1, -1, 1e4, wait=False)
            step(g.iota(iota_i, pattern=[[1, P]], base=0, channel_multiplier=0))
            step(g.memset(flip[:], 0.0))
            keep(flip[:], flip[:], 1 - P, 1, 1, 1.0, ALU.not_equal)
            step(g.tensor_copy(iota[:], iota_i), S["consts"])

            pool.wait_ge(S["u_ready"], 4)
            for i in range(4):
                acc = cacc[:, i, :].rearrange("p (r t) -> p r t", r=ROWS)
                for j in range(TAPS):
                    w = convw[:, 4 * j + i:4 * j + i + 1]
                    src = upad[:, i, :, j:j + ROW]
                    if j == 0:
                        step(g.tensor_scalar(acc, src, w, cols[:, C_CONVB + i:C_CONVB + i + 1], ALU.mult, ALU.add))
                    else:
                        tmp = convt[:, j % 2, :].rearrange("p (r t) -> p r t", r=ROWS)
                        step(g.tensor_scalar(tmp, src, w, None, ALU.mult))
                        if j < TAPS - 1:
                            step(g.tensor_tensor(acc, acc, tmp, ALU.add))
                        else:
                            step(g.tensor_tensor(acc, acc, tmp, ALU.add), S["conv_ready"])
            pool.wait_ge(S["hn_ready"], 1)
            for name, src in (("b_mix", A["b_ada"][0][2 * D:3 * D]), ("post_mix", A["g_post_mix"][0]),
                              ("b_ffn", A["b_ada"][0][5 * D:6 * D]), ("post_ffn", A["g_post_ffn"][0]),
                              ("b_mix2", A["b_ada_2"][0][2 * D:3 * D]), ("b_ffn2", A["b_ada_2"][0][5 * D:6 * D])):
                pool.dma_start(rowd[name], src.partition_broadcast(P)).then_inc(S["rowd_loaded"], 16)
            pool.wait_ge(S["gates_made"], 1)
            pool.wait_ge(S["mixT_conv"], 4)
            pool.dma_start(wr, A["w_router"][0].rearrange("(k p) n -> p k n", p=P)).then_inc(S["wr_loaded"], 16)

            pool.wait_ge(S["x2_ready"], 1)
            pool.wait_ge(S["bias_stored"], 16)
            pool.dma_start(TBr, bass.AP(bias_dram.tensor, 0, [[1, P], [T + P - 1, HEADS2], [1, T]])).then_inc(S["bias_loaded"], 16)
            pool.dma_start(rowf, A["norm_f_g_2"].partition_broadcast(P)).then_inc(S["normf_loaded"], 16)
            pool.dma_start(poolw, A["pool_w_2"][0].rearrange("g c d -> c g d")).then_inc(S["poolw_loaded"], 16)
            pool.wait_ge(S["tb_flipped"], 4)
            step(g.affine_select(out=TB, in_=TB, compare_op=ALU.is_ge, fill=NEG, base=P, pattern=[[0, HEADS2], [-1, T]],
                                 channel_multiplier=1), S["tb_ready"])
            pool.wait_ge(S["x3_ready"], 1)
            for dst, name in ((wr2[:, :, 0:4], "w_router_group_2"), (wr2[:, :, 4:36], "w_router_expert_2")):
                pool.dma_start(dst, A[name][0].rearrange("(k p) n -> p k n", p=P)).then_inc(S["wr_loaded"], 16)
            step(g.tensor_scalar(desc, iota[:, 0:E1], -1.0, float(E1), ALU.mult, ALU.add), S["desc_ready"])

        @block.scalar
        def _(act):
            a = nc.scalar
            step = Steps(act, S["act_step"])

            def vec(tile, at, ap, n):
                act.dma_start(vecs[at:at + n, tile, :], ap.rearrange("(k p) -> k p", p=P)).then_inc(S["vec_loaded"], 16)

            vec(0, C_C, A["c"][0], 8)
            vec(0, C_CTX, A["c_ctx"], 8)
            vec(0, C_2, A["c_2"][0], 8)
            vec(0, C_GPRE, A["g_pre_mix"][0], 8)
            vec(0, C_GFFN, A["g_pre_ffn"][0], 8)
            vec(0, C_N1, A["norm1_g_2"][0], 8)
            vec(0, C_N2, A["norm2_g_2"][0], 8)
            vec(0, C_CONVB, A["conv_b"][0], 4)
            vec(0, C_LNG, A["conv_ln_g"][0], 4)
            vec(0, C_LNB, A["conv_ln_b"][0], 4)
            vec(0, C_POOLS, A["pool_scale_2"][0], 4)
            vec(0, C_BQK, A["b_in"][0][0:512], 4)
            vec(0, C_BCONV, A["b_in"][0][1552:2576], 8)
            vec(1, 0, A["b_ada"][0], 48)
            vec(1, 48, A["b_ada_2"][0], 48)
            act.dma_start(vecs[0:TAPS * 4, 2, :], A["conv_w"][0].rearrange("t (c p) -> (t c) p", p=P)).then_inc(S["vec_loaded"], 16)

            def row(dst, ap):
                act.dma_start(dst, ap.partition_broadcast(P)).then_inc(S["row_loaded"], 16)

            row(rowb, A["b_in"][0][256:1552])
            row(normg, A["mlstm_norm_g"][0].rearrange("h d -> (h d)"))
            row(rowv, A["b_out"][0])
            row(brt[:, 0:64], A["b_router"][0])
            row(brt[:, 64:68], A["b_router_group_2"][0])
            row(brt[:, 68:100], A["b_router_expert_2"][0])
            act.dma_start(relb, A["rel_bias_2"]).then_inc(S["rel_loaded"], 16)
            act.dma_start(onehot, A["bucket"]).then_inc(S["rel_loaded"], 16)
            row(small[:, 344:360], A["b_gate"][0].rearrange("a b -> (a b)"))

            act.wait_ge(S["bias_mm"], 1)
            step(a.copy(biasrow, PS[7][0:HEADS2, 0:T + P - 1]))
            act.dma_start(bias_dram, biasrow).then_inc(S["bias_stored"], 16)
            act.wait_ge(S["consts"], 1)
            act.wait_ge(S["cols_ready"], 1)
            for v in range(3):
                step(a.activation(sc[:, :, v], cols[:, 8 * v:8 * v + 8], ACT.Silu), S["sc_ready"], wait=False)

            for n, (src, loaded) in enumerate(((x, "x_loaded"), (ctxt, "ctx_loaded"))):
                act.wait_ge(S[loaded], 16)
                for b in range(NB):
                    step(a.activation(xn[:, b, :], src[:, b, :], ACT.Square,
                                      accum_out=st[:, 2 * n + b:2 * n + b + 1]), S["norm_sq"])
            act.wait_ge(S["norm_ms"], 1)
            step(a.activation(st[:, 4:8], st[:, 4:8], ACT.Sqrt), S["norm_root"])

            def ada(n):
                i, k = AT[n], [m for m in ITEMS if m[:2] == "ad"].index(n)
                act.wait_ge(S["stream_used"], i + 1)
                for h in range(2):
                    step(a.copy(ada_rows[:, h * 512:(h + 1) * 512], PS[5 + h][:]), S["ada_rows_ready"], wait=False)
                act.wait_ge(S["ada_summed"], k + 1)
                b, s = ada_item(n)
                if is_gate(n):
                    dst = gate if b == 0 else gate2
                    for h in range(2):
                        step(a.copy(dst[:, s // 3, h * 512:(h + 1) * 512], PS[5 + h][:]), S["ada_ready"], wait=False)
                else:
                    step(a.copy(modc[:, b, col_at(n), :, :].rearrange("p k v -> p (k v)"), PS[5][:, 0:24]),
                         S["ada_ready"], wait=False)
            ada("ada0")
            ada("ada1")

            act.wait_ge(S["bias_stored"], 16)
            for k in range(KD):
                act.wait_ge(S["modT"], 5 + k // 2)
                act.wait_ge(S["am_ready"], 1)
                step(a.activation(hTc[:, k, :], PS[4 + k // 2][:, (k % 2) * T:(k % 2 + 1) * T], ACT.Identity, scale=am[:, 1, k:k + 1], bias=modc[:, 0, 0, k, 1:2]),
                     S["hTc_ready"], wait=False)

            for i in range(4):
                act.wait_ge(S["proj_mm"], 12 + i)
                act.wait_ge(S["modT"], 8)
                step(a.activation(usig[:, i, :], PS[(11 + i) % 5][:, T:2 * T], ACT.Sigmoid,
                                  bias=cols[:, C_BCONV + 4 + i:C_BCONV + 5 + i]), S["usig_ready"], wait=False)
            act.wait_ge(S["o_ready"], 1)
            step(a.activation(osig, osig, ACT.Sigmoid), S["osig_ready"], wait=False)
            act.wait_ge(S["exp_in"], 1)
            step(a.activation(lft, lft, ACT.Exp))
            step(a.activation(lft, lft, ACT.Ln, bias=onec), S["exp_out"])
            ada("ada2")
            act.wait_ge(S["exp_in"], 2)
            step(a.activation(wst, wst, ACT.Exp), S["exp_out"])
            act.wait_ge(S["exp_in"], 3)
            step(a.activation(dae, dae, ACT.Exp), S["exp_out"])
            act.wait_ge(S["qk_mm"], 2)
            for r in range(2):
                step(a.copy(qk.rearrange("p c (q r) t -> p c q r t", r=2)[:, :, :, r, :],
                            PS[r][:].rearrange("p (c q t) -> p c q t", c=2, q=2)), S["qk_ready"], wait=False)
            ada("ada3")
            act.wait_ge(S["exp_in"], 4)
            step(a.activation(ee, ee, ACT.Exp), S["exp_out"])
            for gi in range(4):
                act.wait_ge(S["exp_in"], gi + 5)
                step(a.activation(dt4, dt4, ACT.Exp, scale=-1.0), S["exp_out"])
            ada("ada4")
            act.wait_ge(S["norm_ms"], 2)
            step(a.activation(st[:, 8:16], st[:, 8:16], ACT.Sqrt), S["norm_root"])
            ada("ada5")
            act.wait_ge(S["norm_ms"], 3)
            step(a.activation(crstd, crstd, ACT.Sqrt), S["norm_root"])
            for i in range(4):
                act.wait_ge(S["cn_ready"], 1)
                step(a.activation(mixT[:, 4 + i, :], ctmp[:, i, :], ACT.Silu, scale=cols[:, C_LNG + i:C_LNG + i + 1],
                                  bias=cols[:, C_LNB + i:C_LNB + i + 1]), S["mixT_conv"], wait=False)
            for n in ("adb0", "adb1", "adb2", "adb3", "adb4", "adb5"):
                ada(n)

            def norm(n, src):
                act.wait_ge(S["norm_in"], n + 1)
                for b in range(NB):
                    step(a.activation(ada_rows[:], src[:, b, :], ACT.Square, accum_out=st[:, 24 + b:25 + b]), S["norm_sq"])
                act.wait_ge(S["norm_ms"], n + 4)
                step(a.activation(st[:, 26:28], st[:, 26:28], ACT.Sqrt), S["norm_root"])

            def experts(L, G, NG, F, GU):
                DN = GU // 2 if GU > 1 else 1
                pre, before = f"e{L}_", (L - 1) * NG1

                def rows_out(n):
                    for q in range(2):
                        act.wait_ge(S["x_gather"], 2 * (n + before) + 1 + q)
                        a.copy(hTe[:, 4 * q:4 * q + 4, :], PS[4 + q][:].rearrange("p (k s) -> p k s", k=4)).then_inc(S["x_hTe"], 1)

                def body(g, last=False):
                    act.wait_ge(S[pre + "gateup"], GU * g + max(GU // 2, 1))
                    a.activation(sg[:, 0:F], PS[4][:, 0:F], ACT.Silu).then_inc(S["x_sg"], 1)
                    if not last:
                        rows_out(g + 1)
                    act.wait_ge(S[pre + "down"], DN * g + DN)
                    for h in range(2):
                        a.copy(Y[:, h * 512:(h + 1) * 512], PS[6 + h][:]).then_inc(S["x_Y"], 1)

                rows_out(0)
                body(0)
                with act.Fori(0, NG // 2 - 1) as i:
                    body(2 * i + 1)
                    body(2 * i + 2)
                body(NG - 1, last=True)

                count, items, most = over_counts(act, L)
                with act.Fori(0, most) as i:
                    with act.If(i < count):
                        n = i + items
                        for q in range(2):
                            act.wait_ge(S["over_gather"], 2 * n + 1 + q)
                            a.copy(hTe[:, 4 * q:4 * q + 4, :], PS[4 + q][:].rearrange("p (k s) -> p k s", k=4)).then_inc(S["over_hTe"], 1)
                        act.wait_ge(S["over_gateup"], 2 * n + 1)
                        a.activation(sg[:, 0:F], PS[4][:, 0:F], ACT.Silu).then_inc(S["over_sg"], 1)
                        act.wait_ge(S["over_down"], n + 1)
                        for h in range(2):
                            a.copy(Y[:, h * 512:(h + 1) * 512], PS[6 + h][:]).then_inc(S["over_Y"], 1)

            norm(0, xn)
            norm(1, x)
            act.wait_ge(S["router_mm"], 1)
            step(a.activation(sel, PS[4][:, 0:NB * E1].rearrange("p (b e) -> p b e", b=NB), ACT.Sigmoid), S["route_sig"])
            for b in range(NB):
                act.wait_ge(S["sh_gateup"], b + 1)
                step(a.activation(sg_sh[:, b, :], PS[5 + b][:, 0:F1], ACT.Silu), S["sh_sg"], wait=False)
            experts(1, G1, NG1, F1, 1)
            norm(2, xn)

            norm(3, x)
            for n in range(8):
                act.wait_ge(S["zg_biased"], n + 1)
                half, b, h = n // 4, n // 2 % 2, n % 2
                q = slice(half * D + h * 512, half * D + h * 512 + 512)
                step(a.activation(zg[:, b, q], zg[:, b, q], ACT.Sigmoid), S["zg_ready"], wait=False)
            for h in range(HEADS2):
                act.wait_ge(S["smax_ready"], h + 1)
                for b in range(NB):
                    q = slice(0, P) if b == 0 else slice(P, P + T)
                    step(a.activation(pexp[:, h % 2, q], pexp[:, h % 2, q], ACT.Exp, bias=st[:, 2 * (h % 2) + b:2 * (h % 2) + b + 1],
                                      accum_out=st[:, 4 + 2 * (h % 2) + b:5 + 2 * (h % 2) + b]), S["sexp_ready"])
            norm(4, x)
            act.wait_ge(S["zexp_in"], 1)
            step(a.activation(rt[:, 0:8], rt[:, 0:8], ACT.Exp), S["zexp"])
            act.wait_ge(S["zexp_in"], 2)
            step(a.activation(rt[:, 24:26], rt[:, 24:26], ACT.Exp), S["zexp"])
            experts(2, G2, NG2, F2, 4)
            norm(5, x)



        @block.tensor
        def _(pe):
            mm, tr = nc.tensor.matmul, nc.tensor.transpose

            pe.wait_ge(S["vec_loaded"], 16 * 16)
            pe.wait_ge(S["consts"], 1)
            tr(PS[0][:, 0:N_COLS], vecs[0:N_COLS, 0, :], ident[0:N_COLS, 0:N_COLS])
            tr(PS[0][:, 128:224], vecs[0:96, 1, :], ident[0:96, 0:96])
            tr(PS[0][:, 256:380], vecs[0:TAPS * 4, 2, :], ident[0:TAPS * 4, 0:TAPS * 4]).then_inc(S["vecT"], 1)
            pe.wait_ge(S["rel_loaded"], 32)
            mm(PS[7][0:HEADS2, 0:T + P - 1], relb, onehot, start=True, stop=True).then_inc(S["bias_mm"], 1)

            def ada(n):
                i, k = AT[n], [m for m in ITEMS if m[:2] == "ad"].index(n)
                pe.wait_ge(S[f"stream_loaded{i % 3}"], 16 * (i // 3 + 1))
                if k:
                    pe.wait_ge(S["ada_ready"], ada_done[k])
                for h in range(2):
                    for kk in range(2):
                        for j in range(4):
                            last = mm(PS[5 + h][32 * j:32 * j + 32, :], sc[:, 2 * j + kk, :],
                                      ada_w[n][:, 2 * j + kk, h * 512:(h + 1) * 512], start=(kk == 0), stop=(kk == 1))
                last.then_inc(S["stream_used"], 1)
                pe.wait_ge(S["ada_rows_ready"], 2 * (k + 1))
                b, s = ada_item(n)
                if is_gate(n):
                    for h in range(2):
                        last = mm(PS[5 + h][:, :], selrow[:, b, :], ada_rows[:, h * 512:(h + 1) * 512], start=True, stop=True)
                else:
                    for j in range(KD):
                        last = mm(PS[5][:, 3 * j:3 * j + 3], ada_rows[:, j * P:(j + 1) * P], sel3[:], start=True, stop=True)
                last.then_inc(S["ada_summed"], 1)

            pe.wait_ge(S["sc_ready"], 3)
            pe.wait_ge(S["sel_ready"], 1)
            ada("ada0")
            ada("ada1")

            for n, src in enumerate((xn, ctxt)):
                pe.wait_ge(S["xnorm_ready"], n + 1)
                if n:
                    pe.wait_ge(S["ada_ready"], ada_done[2])
                for k in range(KD):
                    for b in range(NB):
                        last = tr(PS[4 * n + k // 2][:, (k % 2) * T + b * P:(k % 2) * T + (b + 1) * P],
                                  src[:, b, k * P:(k + 1) * P], ident[:])
                    if k % 2:
                        last.then_inc(S["modT"], 1)

            pe.wait_ge(S["h_ready"], KD)
            pe.wait_ge(S["hTc_ready"], KD)
            rows_of = [(hT, 0), (hT, 1), (hTc, 0), (hTc, 1)]

            def project(t, parts, signal=None):
                if t >= 5:
                    pe.wait_ge(S["proj_ev"], t - 4)
                for at, n, lhs, rhs in parts:
                    for k in range(KD):
                        last = mm(PS[t % 5][:, at:at + n], lhs(k), rhs(k), start=(k == 0), stop=(k == KD - 1))
                last.then_inc(S["proj_mm"], 1)

            def feat(w, c0):
                return lambda k: w[:, k, c0:c0 + P]

            def toks(src, b):
                return lambda k: src[:, k, b * P:(b + 1) * P]

            def alltoks(src):
                return lambda k: src[:, k, :]

            def wcols(w, c0, n):
                return lambda k: w[:, k, c0:c0 + n]

            i = AT["in_qkv"]
            pe.wait_ge(S[f"stream_loaded{i % 3}"], 16 * (i // 3 + 1))
            project(0, [(m * T, T, feat(w_qkv, m * P), alltoks(hT)) for m in range(2)])
            project(1, [(m * T, T, feat(w_qkv, 256 + m * P), alltoks(hT)) for m in range(2)])
            project(2, [(m * T, T, toks(hT, m), wcols(w_qkv, 256, 256)) for m in range(2)])
            project(3, [(m * T, T, toks(hTc, m), wcols(w_qkv, 256, 256)) for m in range(2)])
            for c, (src, b) in enumerate(rows_of):
                project(4 + c, [(0, 512, toks(src, b), wcols(w_qkv, 512, 512))])
            pe.wait_ge(S["proj_mm"], 8)
            pe.sem_inc(S["stream_used"], 1)
            i = AT["in_og"]
            pe.wait_ge(S[f"stream_loaded{i % 3}"], 16 * (i // 3 + 1))
            for b in range(NB):
                project(8 + b, [(0, 512, toks(hT, b), wcols(w_og, 0, 512))])
            project(10, [(16 * c, 16, toks(src, b), wcols(w_og, 512, 16)) for c, (src, b) in enumerate(rows_of)])
            pe.wait_ge(S["proj_mm"], 11)
            pe.sem_inc(S["stream_used"], 1)
            i = AT["in_conv"]
            pe.wait_ge(S[f"stream_loaded{i % 3}"], 16 * (i // 3 + 1))
            for m in range(4):
                project(11 + m, [(0, T, feat(w_conv, m * P), alltoks(hT)), (T, T, feat(w_conv, 512 + m * P), alltoks(hT))])

            pe.wait_ge(S["lf_ready"], 1)
            for d in range(2):
                mm(PS[0][:, 16 * d:16 * d + 16], tri[:, d, :], LF[:, :, d, :], start=True, stop=True)
            mm(PS[0][:, 32:64], ones[:], LF.rearrange("p c d h -> p (c d h)"), start=True, stop=True).then_inc(S["gate_mm"], 1)
            pe.wait_ge(S["u_ready"], 4)
            pe.sem_inc(S["stream_used"], 1)
            ada("ada2")

            for g in range(8):
                pe.wait_ge(S["diag_ready"], g + 1)
                if g >= 2:
                    pe.wait_ge(S["rows_done"], g - 1)
                mm(PS[1 + g % 2][:, :], ones[:], diag[:, g % 2, :, :].rearrange("p h t -> p (h t)"),
                   start=True, stop=True).then_inc(S["row_mm"], 1)

            for j in range(3):
                for d in range(2):
                    n = 2 * j + d
                    pe.wait_ge(S["kw_ready"], n + 1)
                    if j:
                        pe.wait_ge(S["state_done"], n - 1)
                    for h in range(HEADS):
                        half = slice(64 * (h % 2), 64 * (h % 2) + 64)
                        last = mm(PS[3 + d][half, (h // 2) * 129:(h // 2) * 129 + 129], kw[:, n, h * DK:(h + 1) * DK],
                                  v1[:, STATE_CHUNK[j][d], h, :], start=True, stop=True)
                    last.then_inc(S["state_mm"], 1)

            pe.wait_ge(S["rows_done"], 8)
            for r in range(2):
                half = slice(64 * r, 64 * r + 64)
                for c in range(2):
                    for hp in range(2):
                        last = mm(PS[r][:, (2 * c + hp) * P:(2 * c + hp + 1) * P], kT[half, hp, c * P:(c + 1) * P],
                                  qT[half, hp, c * P:(c + 1) * P], start=True, stop=True)
                last.then_inc(S["qk_mm"], 1)
            ada("ada3")

            pe.wait_ge(S["qk_ready"], 2)
            pe.wait_ge(S["state_done"], 6)
            for gi in range(4):
                c, d = gi // 2, gi % 2
                pe.wait_ge(S["diagm_ready"], gi + 1)
                mm(PS[gi % 2][:, :], ones[:], diag[:, gi % 2, :, :].rearrange("p h t -> p (h t)"),
                   start=True, stop=True).then_inc(S["mrow_mm"], 1)
                pe.wait_ge(S["sT_ready"], gi + 1)
                for h in range(HEADS):
                    hp, half = h // 2, slice(64 * (h % 2), 64 * (h % 2) + 64)
                    at = slice((h % 2) * 129, (h % 2) * 129 + 129)
                    mm(PS[(2, 4)[hp]][:, at], dt4[:, h, :], v1[:, c, h, :], start=True, stop=True)
                    last = mm(PS[(3, 7)[h % 2]][:, hp * 129:hp * 129 + 129], qT[half, hp, c * P:(c + 1) * P],
                              state[half, 0 if c == d else 1, d, hp, :], start=True, stop=True)
                last.then_inc(S["out_mm"], 1)
            ada("ada4")

            pe.wait_ge(S["hm_ready"], 4)
            pe.wait_ge(S["conv_ready"], 4)
            for i in range(4):
                last = mm(PS[2][:, 0:T], ones[:], cacc[:, i, :], start=(i == 0), stop=(i == 3))
            last.then_inc(S["cmean_mm"], 1)
            ada("ada5")
            pe.wait_ge(S["csq_ready"], 1)
            for i in range(4):
                last = mm(PS[3][:, 0:T], ones[:], cacc[:, i, :], start=(i == 0), stop=(i == 3))
            last.then_inc(S["cvar_mm"], 1)

            pe.wait_ge(S["hn_ready"], 1)
            for b in range(NB):
                for h in range(HEADS):
                    last = tr(PS[b][:, h * P:(h + 1) * P], hm[:, b, h * P:(h + 1) * P], ident[:])
                last.then_inc(S["hmT"], 1)
            for n in ("adb0", "adb1", "adb2", "adb3", "adb4", "adb5"):
                ada(n)

            pe.wait_ge(S["mixT_m"], 2)
            pe.wait_ge(S["mixT_conv"], 4)
            i = AT["w_out"]
            pe.wait_ge(S[f"stream_loaded{i % 3}"], 16 * (i // 3 + 1))
            for b in range(NB):
                for h in range(2):
                    for k in range(KD):
                        last = mm(PS[2 * b + h][:, :], mixT[:, k, b * P:(b + 1) * P], w_o[:, k, h * 512:(h + 1) * 512],
                                  start=(k == 0), stop=(k == KD - 1))
            last.then_inc(S["stream_used"], 1)

            def modulated(n, src):
                pe.wait_ge(S["xnorm_ready"], n + 3)
                for k in range(KD):
                    for b in range(NB):
                        last = tr(PS[k // 2][:, (k % 2) * T + b * P:(k % 2) * T + (b + 1) * P],
                                  src[:, b, k * P:(k + 1) * P], ident[:])
                    if k % 2:
                        last.then_inc(S["modT"], 1)
                pe.wait_ge(S["h_ready"], KD * (n + 2))

            def routed(L, w, ne):
                pe.wait_ge(S["wr_loaded"], 16 if L == 1 else 48)
                for b in range(NB):
                    for k in range(KD):
                        last = mm(PS[4][:, b * ne:(b + 1) * ne], hT[:, k, b * P:(b + 1) * P], w[:, k, :],
                                  start=(k == 0), stop=(k == KD - 1))
                last.then_inc(S["router_mm"], 1)
                for b in range(NB):
                    for k in range(KD):
                        last = tr(PS[2 * b + k // 4][:, (k % 4) * P:(k % 4 + 1) * P], hT[:, k, b * P:(b + 1) * P], ident[:])
                        if k % 4 == 3:
                            last.then_inc(S["backT"], 1)

            def ranks(L, ne):
                pe.wait_ge(S["mask_ready"], L)
                at = 256
                mm(PS[4][:, at:at + ne], tri[:, 0, :], mask[:, 0, 0:ne], start=True, stop=True)
                mm(PS[4][:, at + ne:at + 2 * ne], tri[:, 0, :], mask[:, 1, 0:ne], start=True, stop=False)
                mm(PS[4][:, at + ne:at + 2 * ne], ones[:], mask[:, 0, 0:ne], start=False, stop=True)
                for j in range(P // ne):
                    for b in range(NB):
                        last = mm(PS[4][j * ne:(j + 1) * ne, 384:385], mask[:, b, 0:ne], ones[:, 0:1], start=(b == 0), stop=(b == NB - 1))
                last.then_inc(S["rank_mm"], 1)

            def over_list(L):
                pe.wait_ge(S["over_made"], 2 * L - 1)
                mm(PS[7][:, 0:1], tri[:, 0, :], over_flag, start=True, stop=True)
                mm(PS[7][:, 1:2], ones[:], over_flag, start=True, stop=True).then_inc(S["over_mm"], 1)
                pe.wait_ge(S["over_made"], 2 * L)
                mm(PS[7][:, 32:64], Sw[:, 1, 0, :], over_pick, start=True, stop=True)
                mm(PS[7][:, 64:96], Sw[:, 1, 1, :], over_pick, start=True, stop=True).then_inc(S["over_mm"], 1)
                pe.wait_ge(S["over_known"], L)

            def experts(L, G, NG, F, GU, gateup_pieces, down_pieces):
                DN = GU // 2 if GU > 1 else 1
                pre, cap, before = f"e{L}_", P // G, (L - 1) * NG1

                def gather_rows(done):
                    for k in range(KD):
                        for q in range(NB * 3):
                            b, part = q // 3, q % 3
                            last = mm(PS[4 + k // 4][:, (k % 4) * P:(k % 4 + 1) * P], hs[:, part, b, k * P:(k + 1) * P],
                                      Sb[:, b, :], start=(q == 0), stop=(q == NB * 3 - 1))
                        if k % 4 == 3:
                            last.then_inc(done, 1)

                def gather(n):
                    pe.wait_ge(S["x_S"], 2 * (n + before) + 2)
                    gather_rows(S["x_gather"])

                def add_rows():
                    for b in range(NB):
                        for h in range(2):
                            last = mm(PS[2 * b + h][:, :], Ct[:, b * P:(b + 1) * P], Y[:, h * 512:(h + 1) * 512],
                                      start=False, stop=False)
                    return last

                def combine(g):
                    pe.wait_ge(S["x_Ct"], (g + before) + 1)
                    pe.wait_ge(S["x_Y"], 2 * (g + before) + 2)
                    return add_rows()

                def body(g, par, first=False, last=False):
                    pe.wait_ge(S["x_hTe"], 2 * (g + before) + 2)
                    for sem, need, bank, ks, view in gateup_pieces(g, par):
                        pe.wait_ge(sem, need)
                        for kk, k in enumerate(ks):
                            for j in range(G):
                                m = mm(PS[bank][j * cap:(j + 1) * cap, :], hTe[:, k, j * cap:(j + 1) * cap], view[:, j, kk, :],
                                       start=(k == 0), stop=(k == KD - 1))
                        m.then_inc(S[pre + "gateup"], 1)
                    if not first:
                        combine(g - 1)
                    pe.wait_ge(S["x_act"], (g + before) + 1)
                    for f in range(F // P):
                        m = tr(PS[6][:, f * P:(f + 1) * P], av[:, f * P:(f + 1) * P], ident[:])
                    m.then_inc(S["x_turned"], 1)
                    for b in range(NB):
                        m = tr(PS[7][:, b * P:(b + 1) * P], Sw[:, par, b, :], ident[:])
                    m.then_inc(S["x_turned"], 1)
                    if not last:
                        gather(g + 1)
                    pe.wait_ge(S["x_aT"], (g + before) + 1)
                    pe.wait_ge(S["x_Ct"], (g + before) + 1)
                    for sem, need, cs, view in down_pieces(g, par):
                        pe.wait_ge(sem, need)
                        for cc, c in enumerate(cs):
                            for h in range(2):
                                for j in range(G):
                                    m = mm(PS[6 + h][j * cap:(j + 1) * cap, :], aT[:, c, j * cap:(j + 1) * cap],
                                           view[:, j, cc, h * 512:(h + 1) * 512], start=(c == 0), stop=(c == F // P - 1))
                        m.then_inc(S[pre + "down"], 1)

                gather(0)
                over_list(L)
                body(0, 0, first=True)
                with pe.Fori(0, NG // 2 - 1) as i:
                    body(2 * i + 1, 1)
                    body(2 * i + 2, 0)
                body(NG - 1, 1, last=True)
                combine(NG - 1).then_inc(S["over_done"], 1)

                count, items, most = over_counts(pe, L)
                wg, wu, wd = over_weights(F)
                with pe.Fori(0, most) as i:
                    with pe.If(i < count):
                        n = i + items
                        pe.wait_ge(S["over_slots"], 6 * n + 4)
                        gather_rows(S["over_gather"])
                        pe.wait_ge(S["over_hTe"], 2 * n + 2)
                        pe.wait_ge(S["over_loaded"], 48 * n + 48)
                        for bank, w in ((4, wg), (5, wu)):
                            for k in range(KD):
                                m = mm(PS[bank][:, 0:F], hTe[:, k, :], w[:, k, :], start=(k == 0), stop=(k == KD - 1))
                            m.then_inc(S["over_gateup"], 1)
                        pe.wait_ge(S["over_act"], n + 1)
                        for f in range(F // P):
                            m = tr(PS[6][:, f * P:(f + 1) * P], av[:, f * P:(f + 1) * P], ident[:])
                        m.then_inc(S["over_turned"], 1)
                        pe.wait_ge(S["over_slots"], 6 * n + 6)
                        for b in range(NB):
                            m = tr(PS[7][:, b * P:(b + 1) * P], Sw[:, 0, b, :], ident[:])
                        m.then_inc(S["over_turned"], 1)
                        pe.wait_ge(S["over_copied"], 2 * n + 2)
                        for c in range(F // P):
                            for h in range(2):
                                m = mm(PS[6 + h][:, :], aT[:, c, :], wd[:, c, h * 512:(h + 1) * 512], start=(c == 0), stop=(c == F // P - 1))
                        m.then_inc(S["over_down"], 1)
                        pe.wait_ge(S["over_Y"], 2 * n + 2)
                        add_rows().then_inc(S["over_done"], 1)
                for n in range(4):
                    m = mm(PS[n][:, :], zeros[:, 0:P // 2].bitcast(BF16), outer(ones[:].bitcast(BF16), 2), start=False, stop=True)
                m.then_inc(S["y_done"], 1)

            modulated(0, xn)
            routed(1, wr, E1)
            i = AT["shared"]
            pe.wait_ge(S[f"stream_loaded{i % 3}"], 16 * (i // 3 + 3))
            for b in range(NB):
                for k in range(KD):
                    last = mm(PS[5 + b][:, :], hT[:, k, b * P:(b + 1) * P], sh_gu[:, k, :], start=(k == 0), stop=(k == KD - 1))
                last.then_inc(S["sh_gateup"], 1)
            pe.wait_ge(S["route_sig"], 1)
            ranks(1, E1)
            pe.wait_ge(S["sh_act"], 2)
            for b in range(NB):
                for f in range(2):
                    last = tr(PS[7][:, f * T + b * P:f * T + (b + 1) * P], a_sh[:, b, f * P:(f + 1) * P], ident[:])
            last.then_inc(S["sh_turned"], 1)
            pe.wait_ge(S["hs_ready"], 4)
            pe.wait_ge(S["sh_aT"], 1)
            for b in range(NB):
                for h in range(2):
                    for f in range(2):
                        last = mm(PS[2 * b + h][:, :], aT_sh[:, f, b * P:(b + 1) * P], sh_dn[:, f, h * 512:(h + 1) * 512],
                                  start=(f == 0), stop=False)
            last.then_inc(S["stream_used"], 1)
            pe.wait_ge(S["rank_ready"], 1)
            experts(1, G1, NG1, F1, 1,
                    lambda g, par: [(S[f"e1_gu{par}"], 32 * (g + 2 - par), 4, range(KD), gu1[par])],
                    lambda g, par: [(S[f"e1_dn{par}"], 16 * (g + 2 - par), range(2), dn1[par])])

            modulated(1, xn)
            pe.wait_ge(S["bias_loaded"], 16)
            for q in range(4):
                mm(PS[q][:, :], flip[:], TBr[:, 2 * q:2 * q + 2, :].rearrange("p h j -> p (h j)"), start=True, stop=True)\
                    .then_inc(S["tb_mm"], 1)

            def loaded2(i):
                pe.wait_ge(S[f"stream2_loaded{i % 2}"], 16 * (i // 2 + 1) if i != 5 else 48)

            loaded2(0)
            for m in range(8):
                bank = 4 + m // 2 % 4
                for k in range(KD):
                    last = mm(PS[bank][:, (m % 2) * T:(m % 2 + 1) * T], w2k[0][:, k, m * P:(m + 1) * P], hT[:, k, :],
                              start=(k == 0), stop=(k == KD - 1))
                if m == 7:
                    last.then_inc(S["stream2_used"], 1)
                elif m % 2:
                    last.then_inc(S["qk2_mm"], 1)
            loaded2(1)
            pe.wait_ge(S["tb_flipped"], 4)
            for n in range(4):
                w0, b = n // 2 * 512, n % 2
                for k in range(KD):
                    last = mm(PS[n][:, :], hT[:, k, b * P:(b + 1) * P], w2k[1][:, k, w0:w0 + 512], start=(k == 0), stop=(k == KD - 1))
                last.then_inc(S["stream2_used"] if n == 3 else S["vu2_mm"], 1)
            pe.wait_ge(S["qk2_ready"], 4)
            for n in range(8):
                half, b, h = n // 4, n // 2 % 2, n % 2
                if n % 4 == 0:
                    loaded2(2 + half)
                if n == 4:
                    pe.wait_ge(S["vu2_ready"], 4)
                for k in range(KD):
                    last = mm(PS[(4 + n) % 8][:, :], hT[:, k, b * P:(b + 1) * P], w2k[2 + half][:, k, h * 512:(h + 1) * 512],
                              start=(k == 0), stop=(k == KD - 1))
                last.then_inc(S["stream2_used"] if n % 4 == 3 else S["zg_mm"], 1)

            pe.wait_ge(S["zg_biased"], 4)
            pe.wait_ge(S["band_loaded"], 32)
            for gq in range(4):
                for b in range(NB):
                    last = mm(PS[4 + gq][:, 0:T], u2[:, b, gq * P:(gq + 1) * P], band[:, gq, b, :], start=(b == 0), stop=(b == 1))
                last.then_inc(S["pool_mm"], 1)
            pe.wait_ge(S["poolw_loaded"], 16)
            for gq in range(4):
                pe.wait_ge(S["pool_ready"], gq + 1)
                mm(PS[4 + gq][:, T:2 * T], poolw[:, gq, :], dT2[:, gq, :], start=True, stop=True).then_inc(S["pool_mm"], 1)

            pe.wait_ge(S["zg_biased"], 8)
            pe.wait_ge(S["pool_ready"], 8)

            def scores(h):
                half, hp = slice(64 * (h % 2), 64 * (h % 2) + 64), h // 2
                if h >= 2:
                    pe.wait_ge(S["score_taken"], h - 1)
                mm(PS[h % 2][:, 0:P], qT2[half, hp, 0:P], kT2[half, hp, 0:P], start=True, stop=True)
                mm(PS[h % 2][:, P:P + T], qT2[half, hp, P:T], kT2[half, hp, :], start=True, stop=True).then_inc(S["score_mm"], 1)

            def attend(h):
                half, hp = slice(64 * (h % 2), 64 * (h % 2) + 64), h // 2
                pe.wait_ge(S["prob_ready"], h + 1)
                for n in range(3):
                    last = tr(PS[2 + h % 2][:, n * P:(n + 1) * P], pexp[:, h % 2, n * P:(n + 1) * P], ident[:])
                last.then_inc(S["probT"], 1)
                pe.wait_ge(S["pT_ready"], h + 1)
                mm(PS[4 + hp][half, 0:T], vv2[:, 0, h * DH2:(h + 1) * DH2], pT[:, h % 2, 0:T], start=True, stop=False,
                   skip_group_check=True)
                mm(PS[4 + hp][half, P:T], vv2[:, 1, h * DH2:(h + 1) * DH2], pT[:, h % 2, T:T + P], start=False, stop=True,
                   skip_group_check=True).then_inc(S["attn_mm"], 1)

            scores(0)
            for h in range(HEADS2):
                if h + 1 < HEADS2:
                    scores(h + 1)
                attend(h)

            loaded2(4)
            pe.wait_ge(S["stream2_loaded0"], 16 * 4)
            pe.wait_ge(S["attn_done"], 1)
            for br, src in ((0, oT2), (1, plT2)):
                for n in range(4):
                    b, h = n // 2, n % 2
                    for k in range(4):
                        last = mm(PS[4 * br + n][:, :], src[:, k, b * P:(b + 1) * P], w2k[4][:, 4 * br + k, h * 512:(h + 1) * 512],
                                  start=(k == 0), stop=(k == 3))
            last.then_inc(S["stream2_used"], 1)
            pe.wait_ge(S["mixed_ready"], 1)
            for k in range(KD):
                for b in range(NB):
                    last = tr(PS[k // 2][:, (k % 2) * T + b * P:(k % 2) * T + (b + 1) * P], xn[:, b, k * P:(k + 1) * P], ident[:])
                if k % 2:
                    last.then_inc(S["mixedT_mm"], 1)
            pe.wait_ge(S["mixedT_ready"], 4)
            pe.wait_ge(S["stream2_loaded1"], 16 * 3)
            for n in range(4):
                b, h = n // 2, n % 2
                for k in range(KD):
                    last = mm(PS[4 + n][:, :], hT[:, k, b * P:(b + 1) * P], w2k[5][:, k, h * 512:(h + 1) * 512],
                              start=(k == 0), stop=(k == KD - 1))
            last.then_inc(S["stream2_used"], 1)

            modulated(2, xn)
            routed(2, wr2, 36)
            pe.wait_ge(S["zraw_ready"], 1)
            ranks(2, E2)
            pe.wait_ge(S["hs_ready"], 8)
            for n in range(4):
                mm(PS[n][:, :], zeros[:], hT[:, 0:2, :].rearrange("p k t -> p (k t)"), start=True, stop=False)
            pe.wait_ge(S["rank_ready"], 2)
            experts(2, G2, NG2, F2, 4,
                    lambda g, par: [(S["e2_piece0"], 64 * (2 * g + 1), 4, range(0, 4), gu2[0]),
                                    (S["e2_piece1"], 64 * (2 * g + 1), 4, range(4, 8), gu2[1]),
                                    (S["e2_piece2"], 64 * (2 * g + 1), 5, range(0, 4), gu2[2]),
                                    (S["e2_piece0"], 64 * (2 * g + 2), 5, range(4, 8), gu2[0])],
                    lambda g, par: [(S["e2_piece1"], 64 * (2 * g + 2), range(0, 2), dn2[1]),
                                    (S["e2_piece2"], 64 * (2 * g + 2), range(2, 4), dn2[2])])

        @block.vector
        def _(dve):
            v = nc.vector
            step = Steps(dve, S["dve_step"])

            dve.wait_ge(S["vecT"], 1)
            step(v.tensor_copy(convw[:], PS[0][:, 256:380]), wait=False)
            step(v.tensor_copy(adab[:].rearrange("p b n -> p (b n)"), PS[0][:, 128:224]))
            step(v.tensor_copy(cols[:], PS[0][:, 0:N_COLS]), S["cols_ready"])
            dve.wait_ge(S["consts"], 1)
            step(v.tensor_tensor(sel3[:], ident[:, 0:3], ident[:, 32:35], ALU.add))
            step(v.tensor_tensor(sel3[:], sel3[:], ident[:, 64:67], ALU.add))
            step(v.tensor_tensor(sel3[:], sel3[:], ident[:, 96:99], ALU.add))
            step(v.tensor_copy(selrow[:, 0, :], sel3[:, 0:1].to_broadcast([P, P])))
            step(v.tensor_copy(selrow[:, 1, :], sel3[:, 2:3].to_broadcast([P, P])), S["sel_ready"])

            dve.wait_ge(S["norm_sq"], 4)
            step(v.tensor_scalar(st[:, 4:8], st[:, 0:4], 1.0 / D, EPS, ALU.mult, ALU.add), S["norm_ms"])
            dve.wait_ge(S["norm_root"], 1)
            step(v.reciprocal(st[:, 4:8], st[:, 4:8]))
            for n, src, dst in ((0, x, xn), (1, ctxt, ctxt)):
                for b in range(NB):
                    ins = v.tensor_scalar(dst[:, b, :], src[:, b, :], st[:, 4 + 2 * n + b:5 + 2 * n + b], None, ALU.mult)
                    step(ins, S["xnorm_ready"] if b else None)

            dve.wait_ge(S["ada_ready"], ada_done[2])
            mixmod = modc[:, 0, 0:2, :, :].rearrange("p s k v -> p (s k) v")
            step(v.tensor_tensor(mixmod, mixmod, inner(adab[:, 0, 0:16], 3), ALU.add))
            for n in range(2):
                step(v.scalar_tensor_tensor(out=am[:, n, :], in0=modc[:, 0, 1, :, n], scalar=1.0,
                                            in1=cols[:, C_GPRE:C_GPRE + 8], op0=ALU.add, op1=ALU.mult),
                     S["am_ready"] if n else None)
            for k in range(KD):
                dve.wait_ge(S["modT"], k // 2 + 1)
                step(v.tensor_scalar(hT[:, k, :], PS[k // 2][:, (k % 2) * T:(k % 2 + 1) * T], am[:, 0, k:k + 1],
                                     modc[:, 0, 0, k, 0:1], ALU.mult, ALU.add), S["h_ready"], wait=False)

            dve.wait_ge(S["row_loaded"], 112)
            step(v.tensor_scalar(rowb[:, 0:256], rowb[:, 0:256], DK ** -0.5, None, ALU.mult))
            step(v.tensor_tensor(small[:, 344:360], rowb[:, 1280:1296], small[:, 344:360], ALU.add))
            ev = S["proj_ev"]
            dve.wait_ge(S["proj_mm"], 1)
            for m in range(2):
                step(v.tensor_scalar(qT[:, m, :], PS[0][:, m * T:(m + 1) * T], cols[:, C_BQK + m:C_BQK + m + 1], None, ALU.add),
                     ev if m else None, wait=False)
            dve.wait_ge(S["proj_mm"], 2)
            for m in range(2):
                step(v.tensor_scalar(kT[:, m, :], PS[1][:, m * T:(m + 1) * T], cols[:, C_BQK + 2 + m:C_BQK + 3 + m],
                                     DK ** -0.5, ALU.add, ALU.mult), ev if m else None, wait=False)
            for n in range(2):
                dve.wait_ge(S["proj_mm"], 3 + n)
                step(v.scalar_tensor_tensor(out=knat[:, 2 * n:2 * n + 2, :], in0=PS[2 + n][:].rearrange("p (b n) -> p b n", b=2),
                                            scalar=DK ** -0.5, in1=outer(rowb[:, 0:256], 2), op0=ALU.mult, op1=ALU.add), ev, wait=False)
            for c in range(4):
                dve.wait_ge(S["proj_mm"], 5 + c)
                step(v.tensor_tensor(v1[:, c, :, 0:DV], PS[(4 + c) % 5][:].rearrange("p (h n) -> p h n", h=HEADS),
                                     rowb[:, 256:768].rearrange("p (h n) -> p h n", h=HEADS), ALU.add), ev, wait=False)
            for b in range(NB):
                dve.wait_ge(S["proj_mm"], 9 + b)
                step(v.tensor_tensor(osig[:, b, :], PS[(8 + b) % 5][:], rowb[:, 768:1280], ALU.add), ev)
            dve.sem_inc(S["o_ready"], 1)
            dve.wait_ge(S["proj_mm"], 11)
            step(v.tensor_tensor(G, PS[0][:, 0:64].rearrange("p (c n) -> p c n", c=4), outer(small[:, 344:360], 4), ALU.add), ev)
            gv = G.rearrange("p c (d f h) -> p c d f h", d=2, f=2)
            li, lf = gv[:, :, :, 0, :], gv[:, :, :, 1, :]
            step(v.scalar_tensor_tensor(out=lft, in0=lf, scalar=-1.0, in1=lf, op0=ALU.mult, op1=ALU.min), S["exp_in"])
            for i in range(4):
                dve.wait_ge(S["usig_ready"], i + 1)
                step(v.scalar_tensor_tensor(out=upad[:, i, :, HALO:HALO + ROW],
                                            in0=PS[(11 + i) % 5][:, 0:T].rearrange("p (r t) -> p r t", r=ROWS),
                                            scalar=cols[:, C_BCONV + i:C_BCONV + i + 1],
                                            in1=usig[:, i, :].rearrange("p (r t) -> p r t", r=ROWS),
                                            op0=ALU.add, op1=ALU.mult), S["u_ready"])
            dve.wait_ge(S["exp_out"], 1)
            step(v.scalar_tensor_tensor(out=LF, in0=lf, scalar=0.0, in1=lft, op0=ALU.min, op1=ALU.subtract), S["lf_ready"])

            dve.wait_ge(S["gate_mm"], 1)
            b4 = b_.rearrange("p (c d h) -> p c d h", c=4, d=2)
            for d in range(2):
                step(v.tensor_copy(b4[:, :, d, :], PS[0][:, 16 * d:16 * d + 16].rearrange("p (c h) -> p c h", c=4)))
            step(v.tensor_copy(bt_, PS[0][:, 32:64]))
            step(v.tensor_tensor(r_.rearrange("p (c d h) -> p c d h", c=4, d=2), li, b4, ALU.subtract))

            def diagonal(col, buf, sem):
                step(v.tensor_tensor(diag[:, buf, :, :], outer(ident[:], 4), inner(col, P), ALU.mult), sem, wait=False)

            dve.wait_ge(S["proj_mm"], 15)
            diagonal(r_[:, 0:4], 0, S["diag_ready"])
            for g in range(8):
                if g < 7:
                    if g >= 1:
                        dve.wait_ge(S["row_mm"], g)
                    diagonal(r_[:, 4 * g + 4:4 * g + 8], (g + 1) % 2, S["diag_ready"])
                dve.wait_ge(S["row_mm"], g + 1)
                bank = PS[1 + g % 2][:].rearrange("p (h s) -> p h s", h=4)
                if g < 4:
                    step(v.tensor_tensor(dt4, bank, outer(mneg[:, g % 2, :], 4), ALU.add))
                    step(v.tensor_reduce(cmax[:, 4 * g:4 * g + 4], dt4, AX_X, ALU.max))
                step(v.tensor_reduce(rmax[:, 4 * g:4 * g + 4], bank, AX_X, ALU.max), S["rows_done"])
            step(v.tensor_tensor(wst, r_, rmax, ALU.subtract), S["exp_in"])

            step(v.memset(m_run[:, 0:8], 0.0))
            for j in range(3):
                m = m_run[:, 8 * j:8 * j + 8]
                a_log, e_log = dae[:, 16 * j:16 * j + 8], dae[:, 16 * j + 8:16 * j + 16]
                for d in range(2):
                    at = STATE_CHUNK[j][d] * 8 + 4 * d
                    q = slice(4 * d, 4 * d + 4)
                    step(v.tensor_tensor(mx_[:, q], m[:, q], rmax[:, at:at + 4], ALU.max))
                    step(v.tensor_tensor(e_log[:, q], rmax[:, at:at + 4], mx_[:, q], ALU.subtract))
                    step(v.tensor_tensor(m_run[:, 8 * j + 8 + 4 * d:8 * j + 12 + 4 * d], bt_[:, at:at + 4], mx_[:, q], ALU.add))
                step(v.tensor_tensor(a_log, m, mx_, ALU.subtract), S["exp_in"] if j == 2 else None)
            dve.wait_ge(S["exp_out"], 2)
            for j in range(3):
                for d in range(2):
                    c = STATE_CHUNK[j][d]
                    step(v.tensor_tensor(kw[:, 2 * j + d, :].rearrange("p (h n) -> p h n", h=HEADS),
                                         knat[:, c, :].rearrange("p (h n) -> p h n", h=HEADS),
                                         inner(wst[:, 8 * c + 4 * d:8 * c + 4 * d + 4], DK), ALU.mult), S["kw_ready"], wait=False)
            for c in range(2):
                for d in range(2):
                    prev = m_run[:, (16 if c == d else 24) + 4 * d:(16 if c == d else 24) + 4 * d + 4]
                    q = slice(8 * c + 4 * d, 8 * c + 4 * d + 4)
                    step(v.tensor_tensor(m_t[:, q], prev, cmax[:, q], ALU.max))
                    step(v.tensor_tensor(ee[:, q], prev, m_t[:, q], ALU.subtract))
            step(v.scalar_tensor_tensor(out=ee[:, 16:32], in0=b_[:, 0:16], scalar=-1.0, in1=m_t, op0=ALU.mult,
                                        op1=ALU.subtract), S["exp_in"])
            dve.wait_ge(S["exp_out"], 3)
            for half in range(2):
                q = slice(64 * half, 64 * half + 64)
                step(v.tensor_copy(ae2[q, :], dae[q, :].rearrange("p (n r) -> p n r", r=2)[:, :, half]))
            for j in range(3):
                for d in range(2):
                    dve.wait_ge(S["state_mm"], 2 * j + d + 1)
                    local = PS[3 + d][:, 0:258].rearrange("p (h n) -> p h n", h=2)
                    a_ = inner(ae2[:, 8 * j + 2 * d:8 * j + 2 * d + 2], 129)
                    e_ = inner(ae2[:, 8 * j + 4 + 2 * d:8 * j + 6 + 2 * d], 129)
                    if j == 0:
                        step(v.tensor_tensor(state[:, 0, d, :, :], local, e_, ALU.mult), S["state_done"])
                    else:
                        step(v.tensor_tensor(stmp, local, e_, ALU.mult))
                        step(v.tensor_tensor(state[:, j - 1, d, :, :], state[:, 0, d, :, :], a_, ALU.mult))
                        step(v.tensor_tensor(state[:, j - 1, d, :, :], state[:, j - 1, d, :, :], stmp, ALU.add), S["state_done"])

            dve.wait_ge(S["exp_out"], 4)
            for gi in range(4):
                c, d = gi // 2, gi % 2
                diagonal(m_t[:, 4 * gi:4 * gi + 4], gi % 2, S["diagm_ready"])
                dve.wait_ge(S["mrow_mm"], gi + 1)
                for h in range(HEADS):
                    at = 8 * c + 4 * d + h
                    step(v.scalar_tensor_tensor(out=dt4[:, h, :], in0=PS[gi % 2][:, h * P:(h + 1) * P], scalar=r_[:, at:at + 1],
                                                in1=mbig[:, d, :], op0=ALU.subtract, op1=ALU.max),
                         S["exp_in"] if h == HEADS - 1 else None)
                dve.wait_ge(S["exp_out"], gi + 5)
                step(v.tensor_tensor(dt4, dt4, qk[:, c, :, :], ALU.mult), S["sT_ready"])
                dve.wait_ge(S["out_mm"], gi + 1)
                for h in range(HEADS):
                    hp, q = h // 2, slice((h % 2) * 129, (h % 2) * 129 + 129)
                    at = 8 * c + 4 * d + h
                    step(v.tensor_scalar(nd[:, h, :], PS[(3, 7)[h % 2]][:, hp * 129:hp * 129 + 129], ee[:, at:at + 1], None, ALU.mult))
                    step(v.tensor_tensor(nd[:, h, :], nd[:, h, :], PS[(2, 4)[hp]][:, q], ALU.add))
                step(v.scalar_tensor_tensor(out=den, in0=nd[:, :, DV], scalar=-1.0, in1=nd[:, :, DV], op0=ALU.mult, op1=ALU.max))
                step(v.tensor_tensor(den, den, ee[:, 16 + 8 * c + 4 * d:20 + 8 * c + 4 * d], ALU.max))
                step(v.reciprocal(den, den))
                rows = hm[:, c, :].rearrange("p (h n) -> p h n", h=HEADS)
                if d == 0:
                    step(v.tensor_tensor(rows, nd[:, :, 0:DV], inner(den, DV), ALU.mult), S["hm_ready"])
                else:
                    step(v.tensor_tensor(nd[:, :, 0:DV], nd[:, :, 0:DV], inner(den, DV), ALU.mult))
                    step(v.tensor_tensor(rows, rows, nd[:, :, 0:DV], ALU.add), S["hm_ready"])

            hg = hm.rearrange("p b (h n) -> p (b h) n", h=HEADS)
            step(v.tensor_tensor(gsq, hg, hg, ALU.mult))
            step(v.tensor_reduce(st[:, 16:24], gsq, AX_X, ALU.add))
            step(v.tensor_scalar(st[:, 8:16], st[:, 16:24], 1.0 / DV, EPS, ALU.mult, ALU.add), S["norm_ms"])
            dve.wait_ge(S["norm_root"], 2)
            step(v.reciprocal(st[:, 8:16], st[:, 8:16]))
            step(v.tensor_tensor(hg, hg, inner(st[:, 8:16], DV), ALU.mult))
            step(v.tensor_tensor(hm, hm, outer(normg, 2), ALU.mult))
            dve.wait_ge(S["osig_ready"], 1)
            step(v.tensor_tensor(hm, hm, osig, ALU.mult), S["hn_ready"])

            dve.wait_ge(S["cmean_mm"], 1)
            step(v.tensor_scalar(cmean, PS[2][:, 0:T], 1.0 / CONV_C, None, ALU.mult))
            step(v.tensor_tensor(ctmp, cacc, outer(cmean, 4), ALU.subtract))
            step(v.tensor_tensor(cacc, ctmp, ctmp, ALU.mult), S["csq_ready"])
            dve.wait_ge(S["cvar_mm"], 1)
            step(v.tensor_scalar(crstd, PS[3][:, 0:T], 1.0 / CONV_C, EPS, ALU.mult, ALU.add), S["norm_ms"])
            dve.wait_ge(S["norm_root"], 3)
            step(v.reciprocal(crstd, crstd))
            step(v.tensor_tensor(ctmp, ctmp, outer(crstd, 4), ALU.mult), S["cn_ready"])
            for b in range(NB):
                dve.wait_ge(S["hmT"], b + 1)
                step(v.tensor_copy(mixT[:, 0:4, b * P:(b + 1) * P], PS[b][:].rearrange("p (h t) -> p h t", h=HEADS)),
                     S["mixT_m"], wait=False)

            dve.wait_ge(S["rowd_loaded"], 96)
            dve.wait_ge(S["ada_ready"], ada_done[12])
            for dst, name, op in ((gate[:, 0, :], "b_mix", ALU.add), (gate[:, 1, :], "b_ffn", ALU.add),
                                  (gate2[:, 0, :], "b_mix2", ALU.add), (gate2[:, 1, :], "b_ffn2", ALU.add),
                                  (gate[:, 0, :], "post_mix", ALU.mult), (gate[:, 1, :], "post_ffn", ALU.mult)):
                step(v.tensor_tensor(dst, dst, rowd[name], op))
            for b, s, at in ((0, 2, 24), (1, 0, 0), (1, 2, 24)):
                part = modc[:, b, s:s + 2, :, :].rearrange("p s k v -> p (s k) v")
                step(v.tensor_tensor(part, part, inner(adab[:, b, at:at + 16], 3), ALU.add))
            dve.sem_inc(S["gates_made"], 1)

            def root_mean_square():
                n = step.n[S["norm_ms"]] - 3
                dve.sem_inc(S["norm_in"], 1)
                dve.wait_ge(S["norm_sq"], 2 * n + 6)
                step(v.tensor_scalar(st[:, 26:28], st[:, 24:26], 1.0 / D, EPS, ALU.mult, ALU.add), S["norm_ms"])
                dve.wait_ge(S["norm_root"], n + 4)
                step(v.reciprocal(st[:, 26:28], st[:, 26:28]))

            def modulated(n, blk, sec, vec, g0, dst=xn):
                root_mean_square()
                for b in range(NB):
                    step(v.tensor_scalar(dst[:, b, :], x[:, b, :], st[:, 26 + b:27 + b], None, ALU.mult), S["xnorm_ready"] if b else None)
                step(v.scalar_tensor_tensor(out=am[:, 0, :], in0=modc[:, blk, sec + 1, :, vec], scalar=1.0,
                                            in1=cols[:, g0:g0 + 8], op0=ALU.add, op1=ALU.mult))
                for k in range(KD):
                    dve.wait_ge(S["modT"], 8 + 4 * n + k // 2 + 1)
                    step(v.tensor_scalar(hT[:, k, :], PS[k // 2][:, (k % 2) * T:(k % 2 + 1) * T], am[:, 0, k:k + 1],
                                         modc[:, blk, sec, k, vec:vec + 1], ALU.mult, ALU.add), S["h_ready"], wait=False)

            def add_branch(gate_row, norm):
                if norm:
                    root_mean_square()
                for b in range(NB):
                    if norm:
                        step(v.scalar_tensor_tensor(out=xn[:, b, :], in0=xn[:, b, :], scalar=st[:, 26 + b:27 + b],
                                                    in1=gate_row, op0=ALU.mult, op1=ALU.mult))
                    else:
                        step(v.tensor_tensor(xn[:, b, :], xn[:, b, :], gate_row, ALU.mult))
                    step(v.tensor_tensor(x[:, b, :], x[:, b, :], xn[:, b, :], ALU.add))

            def split_h(L):
                for n in range(4):
                    b, q = n // 2, slice((n % 2) * 512, (n % 2) * 512 + 512)
                    dve.wait_ge(S["backT"], 4 * (L - 1) + n + 1)
                    step(v.tensor_copy(hs[:, 0, b, q], PS[n][:]))
                    step(v.tensor_tensor(xn[:, b, q], PS[n][:], hs[:, 0, b, q], ALU.subtract), S["hs_ready"])
                    step(v.tensor_copy(hs[:, 1, b, q], xn[:, b, q]))
                    step(v.tensor_tensor(xn[:, b, q], xn[:, b, q], hs[:, 1, b, q], ALU.subtract))
                    step(v.tensor_copy(hs[:, 2, b, q], xn[:, b, q]))

            def make_ranks(L, ne):
                cap = (CAP1, CAP2)[L - 1]
                step(v.tensor_reduce(over_idx, tri[:, 1, :], AX_X, ALU.add))
                step(v.memset(over_from, float(cap)))
                for j in range(1, P // ne):
                    past = tri[:, 1, j * ne:j * ne + 1]
                    step(v.scalar_tensor_tensor(out=over_idx, in0=past, scalar=-float(ne), in1=over_idx, op0=ALU.mult, op1=ALU.add))
                    step(v.scalar_tensor_tensor(out=over_from, in0=past, scalar=float(P), in1=over_from, op0=ALU.mult, op1=ALU.add))
                step(v.tensor_copy(Sw[:, 1, 0, :], over_idx.to_broadcast([P, P])))
                step(v.tensor_copy(Sw[:, 1, 1, :], over_from.to_broadcast([P, P])))
                dve.wait_ge(S["rank_mm"], L)
                step(v.tensor_tensor(over_flag, PS[4][:, 384:385], over_from, ALU.is_gt), S["over_made"])
                cum = PS[4][:, 256:256 + NB * ne].rearrange("p (b e) -> p b e", b=NB)
                step(v.tensor_tensor(rank[:, :, 0:ne], cum, mask[:, :, 0:ne], ALU.mult))
                step(v.tensor_scalar(rank[:, :, 0:ne], rank[:, :, 0:ne], -1.0, None, ALU.add), S["rank_ready"])

            def over_list(L):
                dve.wait_ge(S["over_mm"], 2 * L - 1)
                step(v.tensor_tensor(over_place, PS[7][:, 0:1], over_flag, ALU.mult))
                step(v.tensor_scalar(over_place, over_place, -1.0, None, ALU.add))
                step(v.tensor_tensor(over_pick, iota[:, 0:32], over_place.to_broadcast([P, 32]), ALU.is_equal), S["over_made"])
                dve.wait_ge(S["over_mm"], 2 * L)
                step(v.tensor_copy(over_expert, PS[7][:, 32:64]))
                step(v.tensor_copy(over_start, PS[7][:, 64:96]))
                step(v.tensor_copy(over_count[L - 1], PS[7][:, 1:2]), S["over_known"])

            def experts(L, G, NG, F, GU):
                pre, cap, before = f"e{L}_", P // G, (L - 1) * NG1

                def slots(n, par):
                    for b in range(NB):
                        v.tensor_tensor(Sb[:, b, :].rearrange("p (e s) -> p e s", e=G), outer(iota[:, 0:cap], G),
                                        inner(rank[:, b, bass.ds(n * G, G)], cap), ALU.is_equal).then_inc(S["x_S"], 1)
                    dve.wait_ge(S["x_S"], 2 * (n + before) + 2)
                    for b in range(NB):
                        v.tensor_tensor(Sw[:, par, b, :].rearrange("p (e s) -> p e s", e=G),
                                        Sb[:, b, :].rearrange("p (e s) -> p e s", e=G),
                                        inner(wts[:, b, bass.ds(n * G, G)], cap), ALU.mult).then_inc(S["x_Sw"], 1)

                def body(g, par, last=False):
                    dve.wait_ge(S["x_Sw"], 2 * (g + before) + 2)
                    if not last:
                        dve.wait_ge(S["x_gather"], 2 * (g + before) + 2)
                        slots(g + 1, 1 - par)
                    dve.wait_ge(S["x_sg"], (g + before) + 1)
                    dve.wait_ge(S[pre + "gateup"], GU * g + GU)
                    up = PS[4][:, F:2 * F] if L == 1 else PS[5][:, 0:F]
                    v.tensor_tensor(av[:, 0:F], sg[:, 0:F], up, ALU.mult).then_inc(S["x_act"], 1)
                    dve.wait_ge(S["x_turned"], 2 * (g + before) + 1)
                    v.tensor_copy(aT[:, 0:F // P, :], PS[6][:, 0:F].rearrange("p (f s) -> p f s", f=F // P)).then_inc(S["x_aT"], 1)
                    dve.wait_ge(S["x_turned"], 2 * (g + before) + 2)
                    v.tensor_copy(Ct, PS[7][:, 0:T]).then_inc(S["x_Ct"], 1)

                slots(0, 0)
                over_list(L)
                body(0, 0)
                with dve.Fori(0, NG // 2 - 1) as i:
                    body(2 * i + 1, 1)
                    body(2 * i + 2, 0)
                body(NG - 1, 1, last=True)

                count, items, most = over_counts(dve, L)
                with dve.Fori(0, most) as i:
                    with dve.If(i < count):
                        n = i + items
                        expert = dve.value_load(over_expert[0:1, bass.ds(i, 1)], min_val=1, max_val=(E1, E2)[L - 1]) - 1
                        dve.wait_ge(S["over_done"], n + L)
                        for b in range(NB):
                            v.tensor_tensor(over_shift[:, b:b + 1], rank[:, b, bass.ds(expert, 1)], over_start[:, bass.ds(i, 1)],
                                            ALU.subtract).then_inc(S["over_slots"], 1)
                        dve.wait_ge(S["over_slots"], 6 * n + 2)
                        for b in range(NB):
                            v.tensor_tensor(Sb[:, b, :], iota[:], over_shift[:, b:b + 1].to_broadcast([P, P]),
                                            ALU.is_equal).then_inc(S["over_slots"], 1)
                        dve.wait_ge(S["over_slots"], 6 * n + 4)
                        for b in range(NB):
                            v.tensor_tensor(Sw[:, 0, b, :], Sb[:, b, :], wts[:, b, bass.ds(expert, 1)].to_broadcast([P, P]),
                                            ALU.mult).then_inc(S["over_slots"], 1)
                        dve.wait_ge(S["over_sg"], n + 1)
                        dve.wait_ge(S["over_gateup"], 2 * n + 2)
                        v.tensor_tensor(av[:, 0:F], sg[:, 0:F], PS[5][:, 0:F], ALU.mult).then_inc(S["over_act"], 1)
                        dve.wait_ge(S["over_turned"], 2 * n + 1)
                        v.tensor_copy(aT[:, 0:F // P, :], PS[6][:, 0:F].rearrange("p (f s) -> p f s", f=F // P))\
                            .then_inc(S["over_copied"], 1)
                        dve.wait_ge(S["over_turned"], 2 * n + 2)
                        v.tensor_copy(Ct, PS[7][:, 0:T]).then_inc(S["over_copied"], 1)

            def sums_out(n):
                dve.wait_ge(S["y_done"], n)
                for b in range(NB):
                    for h in range(2):
                        step(v.tensor_copy(xn[:, b, h * 512:(h + 1) * 512], PS[2 * b + h][:]))

            dve.wait_ge(S["stream_used"], AT["w_out"] + 1)
            for b in range(NB):
                for h in range(2):
                    q = slice(h * 512, (h + 1) * 512)
                    step(v.tensor_tensor(xn[:, b, q], PS[2 * b + h][:], rowv[:, q], ALU.add))
            add_branch(gate[:, 0, :], True)
            modulated(0, 0, 2, 0, C_GFFN)
            dve.wait_ge(S["route_sig"], 1)
            step(v.tensor_tensor(tmpr, sel, outer(brt[:, 0:E1], NB), ALU.add))
            for b in range(NB):
                step(v.max(max8[:, b, :], tmpr[:, b, :]))
                step(v.match_replace(mask[:, b, :], max8[:, b, :], tmpr[:, b, :], NEG))
            step(v.tensor_tensor(mask, mask, tmpr, ALU.not_equal), S["mask_ready"])
            step(v.tensor_tensor(wts, mask, sel, ALU.mult))
            step(v.tensor_reduce(st[:, 28:30], wts, AX_X, ALU.add))
            step(v.reciprocal(st[:, 28:30], st[:, 28:30]))
            for b in range(NB):
                step(v.tensor_scalar(wts[:, b, :], wts[:, b, :], st[:, 28 + b:29 + b], ROUTE_SCALE, ALU.mult, ALU.mult))
            split_h(1)
            for b in range(NB):
                dve.wait_ge(S["sh_sg"], b + 1)
                step(v.tensor_tensor(a_sh[:, b, :], sg_sh[:, b, :], PS[5 + b][:, F1:2 * F1], ALU.mult), S["sh_act"])
            dve.wait_ge(S["sh_turned"], 1)
            step(v.tensor_copy(aT_sh, PS[7][:].rearrange("p (f t) -> p f t", f=2)), S["sh_aT"])
            make_ranks(1, E1)
            experts(1, G1, NG1, F1, 1)
            sums_out(1)
            add_branch(gate[:, 1, :], True)

            modulated(1, 1, 0, 2, C_N1)
            dve.sem_inc(S["x2_ready"], 1)
            for q in range(4):
                dve.wait_ge(S["tb_mm"], q + 1)
                step(v.tensor_copy(TB[:, 2 * q:2 * q + 2, :], PS[q][:].rearrange("p (h j) -> p h j", h=2)), S["tb_flipped"])
            for q in range(4):
                dve.wait_ge(S["qk2_mm"], q + 1) if q < 3 else dve.wait_ge(S["stream2_used"], 1)
                dst = (qT2 if q < 2 else kT2)[:, 2 * (q % 2):2 * (q % 2) + 2, :]
                step(v.tensor_copy(dst, PS[4 + q][:].rearrange("p (m t) -> p m t", m=2)), S["qk2_ready"])
            for n in range(4):
                dve.wait_ge(S["vu2_mm"], n + 1) if n < 3 else dve.wait_ge(S["stream2_used"], 2)
                step(v.tensor_copy((vv2 if n < 2 else u2)[:, n % 2, :], PS[n][:]), S["vu2_ready"])
            dve.wait_ge(S["band_loaded"], 32)
            for n in range(8):
                half, b, h = n // 4, n // 2 % 2, n % 2
                if n % 4 == 3:
                    dve.wait_ge(S["stream2_used"], 3 + half)
                else:
                    dve.wait_ge(S["zg_mm"], 3 * half + n % 4 + 1)
                q = slice(half * D + h * 512, half * D + h * 512 + 512)
                step(v.tensor_tensor(zg[:, b, q], PS[(4 + n) % 8][:], bgrow[:, q], ALU.add), S["zg_biased"])
            for gq in range(4):
                dve.wait_ge(S["pool_mm"], gq + 1)
                step(v.tensor_copy(dT2[:, gq, :], PS[4 + gq][:, 0:T]), S["pool_ready"], wait=False)
            for gq in range(4):
                dve.wait_ge(S["pool_mm"], gq + 5)
                step(v.tensor_scalar(plT2[:, gq, :], PS[4 + gq][:, T:2 * T], cols[:, C_POOLS + gq:C_POOLS + gq + 1], None, ALU.mult),
                     S["pool_ready"])
            dve.sem_inc(S["pool_done"], 1)
            dve.wait_ge(S["tb_ready"], 1)

            def soft_max(h):
                o = h % 2
                dve.wait_ge(S["score_mm"], h + 1)
                step(v.scalar_tensor_tensor(out=pexp[:, o, 0:P], in0=PS[o][:, 0:P], scalar=DH2 ** -0.5, in1=TB[:, h, P:T],
                                            op0=ALU.mult, op1=ALU.add))
                step(v.scalar_tensor_tensor(out=pexp[:, o, P:P + T], in0=PS[o][:, P:P + T], scalar=DH2 ** -0.5, in1=TB[:, h, :],
                                            op0=ALU.mult, op1=ALU.add), S["score_taken"])
                step(v.tensor_reduce(st[:, 2 * o:2 * o + 1], pexp[:, o, 0:P], AX_X, ALU.max))
                step(v.tensor_reduce(st[:, 2 * o + 1:2 * o + 2], pexp[:, o, P:P + T], AX_X, ALU.max))
                step(v.tensor_scalar(st[:, 2 * o:2 * o + 2], st[:, 2 * o:2 * o + 2], -1.0, None, ALU.mult), S["smax_ready"])

            def probabilities(h):
                o = h % 2
                dve.wait_ge(S["sexp_ready"], 2 * h + 2)
                step(v.reciprocal(st[:, 4 + 2 * o:6 + 2 * o], st[:, 4 + 2 * o:6 + 2 * o]))
                step(v.tensor_scalar(pexp[:, o, 0:P], pexp[:, o, 0:P], st[:, 4 + 2 * o:5 + 2 * o], None, ALU.mult))
                step(v.tensor_scalar(pexp[:, o, P:P + T], pexp[:, o, P:P + T], st[:, 5 + 2 * o:6 + 2 * o], None, ALU.mult), S["prob_ready"])

            def probs_turned(h):
                dve.wait_ge(S["probT"], h + 1)
                step(v.tensor_copy(pT[:, h % 2, :], PS[2 + h % 2][:, 0:3 * P]), S["pT_ready"])

            soft_max(0)
            for h in range(HEADS2):
                if h + 1 < HEADS2:
                    soft_max(h + 1)
                probabilities(h)
                probs_turned(h)
                if h % 2:
                    dve.wait_ge(S["attn_mm"], h + 1)
                    step(v.tensor_copy(oT2[:, h // 2, :], PS[4 + h // 2][:, 0:T]))
            dve.sem_inc(S["attn_done"], 1)
            dve.wait_ge(S["stream2_used"], 5)
            dve.wait_ge(S["zg_ready"], 8)
            for n in range(4):
                b, h = n // 2, n % 2
                q, q2 = slice(h * 512, h * 512 + 512), slice(D + h * 512, D + h * 512 + 512)
                step(v.tensor_tensor(xn[:, b, q], PS[n][:], zg[:, b, q], ALU.mult))
                step(v.tensor_tensor(zg[:, b, q2], PS[4 + n][:], zg[:, b, q2], ALU.mult))
                step(v.tensor_tensor(xn[:, b, q], xn[:, b, q], zg[:, b, q2], ALU.add), S["zg_done"])
            dve.sem_inc(S["mixed_ready"], 1)
            for q in range(4):
                dve.wait_ge(S["mixedT_mm"], q + 1)
                step(v.tensor_copy(hT[:, 2 * q:2 * q + 2, :], PS[q][:].rearrange("p (k t) -> p k t", k=2)), S["mixedT_ready"])
            dve.wait_ge(S["stream2_used"], 6)
            for b in range(NB):
                for h in range(2):
                    step(v.tensor_copy(xn[:, b, h * 512:(h + 1) * 512], PS[4 + 2 * b + h][:]))
            add_branch(gate2[:, 0, :], False)
            dve.sem_inc(S["x3_ready"], 1)

            modulated(2, 1, 2, 2, C_N2)
            dve.wait_ge(S["router_mm"], 2)
            zz = tmpr.rearrange("p b e -> p (b e)")[:, 0:72].rearrange("p (b n) -> p b n", b=NB)
            step(v.tensor_tensor(zz, PS[4][:, 0:72].rearrange("p (b n) -> p b n", b=NB), outer(brt[:, 64:100], NB), ALU.add), S["zraw_ready"])
            zgr, zex = zz[:, :, 0:GROUPS2], zz[:, :, GROUPS2:36]
            col = lambda at: rt[:, at:at + NB]
            step(v.tensor_reduce(col(8), zgr, AX_X, ALU.max))
            ge = rt[:, 0:8].rearrange("p (b n) -> p b n", b=NB)
            oh = rt[:, 32:40].rearrange("p (b n) -> p b n", b=NB)
            step(v.tensor_tensor(ge, zgr, inner(col(8), GROUPS2), ALU.subtract), S["zexp_in"])
            dve.wait_ge(S["zexp"], 1)
            step(v.tensor_reduce(col(10), ge, AX_X, ALU.add))
            step(v.reciprocal(col(10), col(10)))
            dve.wait_ge(S["desc_ready"], 1)

            def first_max(dst, src, top, n):
                step(v.tensor_reduce(top, src, AX_X, ALU.max))
                step(v.tensor_tensor(dst, src, inner(top, n), ALU.is_equal))
                step(v.tensor_tensor(dst, dst, outer(desc[:, 0:n], NB), ALU.mult))
                step(v.tensor_reduce(col(12), dst, AX_X, ALU.max))
                step(v.tensor_tensor(dst, dst, inner(col(12), n), ALU.is_equal))

            first_max(oh, zgr, col(14), GROUPS2)
            ohx = sel[:, :, 0:E2]
            step(v.tensor_copy(ohx.rearrange("p b (g e) -> p b g e", g=GROUPS2),
                               oh.unsqueeze(3).to_broadcast([P, NB, GROUPS2, PER_GROUP2])))
            step(v.tensor_tensor(zex, zex, ohx, ALU.mult))
            step(v.tensor_scalar(ohx, ohx, -1.0, -NEG, ALU.add, ALU.mult))
            step(v.tensor_tensor(zex, zex, ohx, ALU.add))
            one, two = mask[:, :, 0:E2], mask[:, :, E2:2 * E2]
            first_max(one, zex, col(16), E2)
            step(v.tensor_scalar(ohx, one, 2 * NEG, None, ALU.mult))
            step(v.tensor_tensor(zex, zex, ohx, ALU.add))
            first_max(two, zex, col(18), E2)
            step(v.tensor_tensor(col(24), col(18), col(16), ALU.subtract), S["zexp_in"])
            dve.wait_ge(S["zexp"], 2)
            step(v.tensor_scalar(col(20), col(24), 1.0, None, ALU.add))
            step(v.reciprocal(col(20), col(20)))
            step(v.tensor_tensor(col(20), col(20), col(10), ALU.mult))
            step(v.tensor_tensor(col(22), col(20), col(24), ALU.mult))
            w2 = wts[:, :, 0:E2]
            step(v.tensor_tensor(w2, one, inner(col(20), E2), ALU.mult))
            step(v.tensor_tensor(ohx, two, inner(col(22), E2), ALU.mult))
            step(v.tensor_tensor(w2, w2, ohx, ALU.add))
            step(v.tensor_tensor(one, one, two, ALU.add), S["mask_ready"])
            split_h(2)
            make_ranks(2, E2)
            experts(2, G2, NG2, F2, 4)
            sums_out(2)
            add_branch(gate2[:, 1, :], False)
            root_mean_square()
            dve.wait_ge(S["normf_loaded"], 16)
            for b in range(NB):
                step(v.scalar_tensor_tensor(out=xn[:, b, :], in0=x[:, b, :], scalar=st[:, 26 + b:27 + b], in1=rowf,
                                            op0=ALU.mult, op1=ALU.mult), S["out_ready"])



INPUTS = ["x", "c", "ctx", "c_ctx", "w_ada", "b_ada", "g_pre_mix", "g_post_mix", "g_pre_ffn", "g_post_ffn", "w_in", "b_in",
          "b_gate", "mlstm_norm_g", "conv_w", "conv_b", "conv_ln_g", "conv_ln_b", "w_out", "b_out", "w_router",
          "b_router", "we_gate", "we_up", "we_down", "ws_gate", "ws_up", "ws_down", "c_2", "w_ada_2", "b_ada_2",
          "norm1_g_2", "w_in_2", "b_gate_2", "rel_bias_2", "pool_w_2", "pool_scale_2", "w_branch_attn_2",
          "w_branch_pool_2", "w_out_2", "norm2_g_2", "w_router_group_2", "b_router_group_2", "w_router_expert_2",
          "b_router_expert_2", "w_expert_gate_2", "w_expert_up_2", "w_expert_down_2", "norm_f_g_2"]


def kernel(**inputs):
    import concourse.bacc as bacc
    from concourse.bass_utils import run_bass_kernel_spmd as run

    nc = bacc.Bacc("TRN2", target_bir_lowering=False, num_devices=1)
    arrays, aps = {}, {}
    for name in INPUTS:
        a = np.ascontiguousarray(inputs[name])
        arrays["in_" + name] = a
        aps[name] = nc.dram_tensor("in_" + name, a.shape, mybir.dt.from_np(a.dtype), kind="ExternalInput").ap()
    for name, a in shape_constants().items():
        arrays["const_" + name] = a
        aps[name] = nc.dram_tensor("const_" + name, a.shape, F32, kind="ExternalInput").ap()
    out = nc.dram_tensor("out", (1, T, D), F32, kind="ExternalOutput").ap()
    two_block_network(nc, aps, out)
    return run(nc, [arrays], core_ids=[0]).results[0]["out"]
```

```python
import concourse.bass as bass
from concourse import mybir
from contextlib import ExitStack
import numpy as np

F32 = mybir.dt.float32
BF16 = mybir.dt.bfloat16
I32 = mybir.dt.int32
ALU = mybir.AluOpType
ACT = mybir.ActivationFunctionType
AX_X = mybir.AxisListType.X

P = 128
T = 256
NB = T // P
D = 1024
KD = D // P
EPS = 1e-6
NEG = -1e30

HEADS, DK, DV = 4, 64, 128
TAPS, CONV_C, ROW, ROWS = 31, 512, 64, 4
HALO = TAPS // 2
SPLIT_TAP = 15
E1, F1, TOP1, ROUTE_SCALE = 64, 256, 8, 2.5
HEADS2, DH2 = 8, 64
POOL_WINDOWS = (2, 4, 8, 16)
GROUPS2, PER_GROUP2, E2, F2 = 4, 8, 32, 512
BUCKETS, MAX_DIST = 32, 128

G1, G2 = 2, 4
CAP1, CAP2 = P // G1, P // G2
NG1, NG2 = E1 // G1, E2 // G2
OVER1, OVER2 = T * TOP1 // (CAP1 + 1), T * 2 // (CAP2 + 1)
LIST = 36

BUFN = 8192
ITEMS = ["ada0", "ada1", "in_qkv", "ada2", "in_og", "ada3", "in_conv", "ada4", "ada5",
         "adb0", "adb1", "adb2", "adb3", "adb4", "adb5", "w_out", "shared"]
AT = {n: i for i, n in enumerate(ITEMS)}
ITEMS2 = ["in2_qk", "in2_vu", "in2_ga", "in2_gp", "branches", "w_out2"]
AT2 = {n: i for i, n in enumerate(ITEMS2)}

C_C, C_CTX, C_2, C_GPRE, C_GFFN, C_N1, C_N2 = 0, 8, 16, 24, 32, 40, 48
C_CONVB, C_LNG, C_LNB, C_POOLS, C_BQK, C_BCONV, N_COLS = 56, 60, 64, 68, 72, 76, 84

STATE_CHUNK = ((2, 3), (3, 2), (0, 1))
ADA = [n for n in ITEMS if n[:2] == "ad"]
ada_done = [sum(2 if n[3] in "25" else 1 for n in ADA[:k]) for k in range(len(ADA) + 1)]


def shape_constants():
    i = np.arange(T + P - 1)
    dist = np.maximum(T - 1 - i, 0)
    exact = BUCKETS // 2
    nf = np.maximum(dist, 1).astype(np.float32)
    large = exact + (np.log(nf / np.float32(exact)) / np.float32(np.log(MAX_DIST / exact))
                     * np.float32(BUCKETS - exact)).astype(np.int32)
    bucket = np.where(dist < exact, dist, np.minimum(large, BUCKETS - 1))
    onehot = (bucket[None, :] == np.arange(BUCKETS)[:, None]).astype(np.float32)
    s, t = np.arange(T)[:, None], np.arange(T)[None, :]
    band = np.stack([((s <= t) & (s > t - w)) / np.minimum(t + 1, w) - (s == t) for w in POOL_WINDOWS])
    return {"bucket": onehot, "band": band.astype(np.float32)}


class Steps:

    def __init__(self, eng, own):
        self.eng, self.own, self.n = eng, own, {}

    def __call__(self, ins, sem=None, wait=True):
        sem = self.own if sem is None else sem
        self.n[sem] = self.n.get(sem, 0) + 1
        ins.then_inc(sem, 1)
        if wait:
            self.eng.wait_ge(sem, self.n[sem])


class Sems(dict):

    def __init__(self, nc, ctx):
        self.nc, self.ctx = nc, ctx

    def __missing__(self, name):
        self[name] = self.ctx.enter_context(self.nc.semaphore(name))
        return self[name]


def outer(ap, n):
    return ap.unsqueeze(1).to_broadcast([ap.shape[0], n, ap.shape[1]])


def inner(ap, n):
    return ap.unsqueeze(2).to_broadcast([ap.shape[0], ap.shape[1], n])


def two_block_network(nc, A, out):
    ctx = ExitStack()
    with ctx:
        S = Sems(nc, ctx)
        bias_dram = nc.dram_tensor("bias_by_distance", (HEADS2, T + P - 1), F32).ap()

        def sb(name, shape, dt=F32):
            return ctx.enter_context(nc.sbuf_tensor(name, shape, dt))

        W = sb("W", [P, 3 * BUFN])
        BUF = [W[:, i * BUFN:(i + 1) * BUFN] for i in range(3)]
        x = sb("x", [P, NB, D])
        hT = sb("hT", [P, KD, T])
        xn = sb("xn", [P, NB, D])
        gate = sb("gate", [P, 2, D])
        gate2 = sb("gate2", [P, 2, D])
        cols = sb("cols", [P, N_COLS])
        adab = sb("adab", [P, 2, 48])
        convw = sb("convw", [P, TAPS * 4])
        sc = sb("sc", [P, KD, 32])
        modc = sb("modc", [P, 2, 4, KD, 3])
        ada_rows = sb("ada_rows", [P, D])
        ident = sb("ident", [P, P])
        ones = sb("ones", [P, P])
        zeros = sb("zeros", [P, P])
        tri = sb("tri", [P, 2, P])
        iota = sb("iota", [P, P])
        selrow = sb("selrow", [P, 2, P])
        small = sb("small", [P, 480])
        flip = sb("flip", [P, P])
        brt = sb("brt", [P, 104])
        am = sb("am", [P, 2, KD])

        NS = 14784
        scr = sb("scr", [P, NS])

        class Carve:
            def __init__(self, base=0):
                self.at = base

            def __call__(self, *shape, dt=F32):
                n = int(np.prod(shape))
                words = n if dt != BF16 else (n + 1) // 2
                ap = scr[:, self.at:self.at + words]
                self.at += words
                assert self.at <= NS, self.at
                if dt != F32:
                    ap = ap.bitcast(dt)
                if len(shape) == 1:
                    return ap
                names = "abcde"[:len(shape)]
                kw = {c: s for c, s in zip(names[1:], shape[1:])}
                return ap.rearrange(f"p ({' '.join(names)}) -> p {' '.join(names)}", **kw)

        cv = Carve()
        hT_words = hT[:].rearrange("p a b -> p (a b)")
        ctxt = cv(NB, D)
        hTc = cv(KD, T)
        hTc_words = hTc.rearrange("p a b -> p (a b)")
        qT = cv(2, T)
        kT = cv(2, T)
        knat = cv(4, 256)
        v1 = cv(4, HEADS, DV + 1)
        osig = cv(NB, 512)
        upad = cv(4, ROWS, ROW + 2 * HALO)
        rowb = cv(1296)
        normg = cv(512)
        G = cv(4, 16)
        LF = cv(4, 2, 4)
        lft = cv(4, 2, 4)
        wst = cv(32)
        mneg = cv(2, P)
        mbig = cv(2, P)
        convt = cv(2, T)
        rowv = cv(D)
        vecs = hTc_words[:, 0:3 * P].rearrange("p (c n) -> p c n", c=3)
        relb = hTc_words[0:BUCKETS, 400:408]
        onehot = hTc_words[0:BUCKETS, 512:512 + T + P - 1]
        biasrow = hTc_words[0:HEADS2, 1024:1024 + T + P - 1]
        mixT = ctxt.rearrange("p a b -> p (a b)").rearrange("p (k t) -> p k t", k=KD)
        kw = hTc_words[:, 0:6 * 256].rearrange("p (c n) -> p c n", c=6)
        dt4 = hTc_words[:, 1536:2048].rearrange("p (h t) -> p h t", h=HEADS)
        dts = [dt4, hTc_words[:, 0:512].rearrange("p (h t) -> p h t", h=HEADS)]
        diag = hT_words[:, 0:1024].rearrange("p (b h t) -> p b h t", b=2, h=HEADS)
        cacc = hT_words[:, 1024:2048].rearrange("p (c t) -> p c t", c=4)
        hm = xn[:, 0, :].rearrange("p (b n) -> p b n", b=NB)
        qk = xn[:, 1, :].rearrange("p (c h t) -> p c h t", c=2, h=HEADS)
        usig = xn[:, 1, :].rearrange("p (c t) -> p c t", c=4)
        state = rowb[:, 0:1032].rearrange("p (w d h n) -> p w d h n", w=2, d=2, h=2)
        stmp = rowb[:, 1032:1290].rearrange("p (h n) -> p h n", h=2)
        cacc2 = rowb[:, 1032:1288]
        knat_words = knat.rearrange("p a b -> p (a b)")
        nd = knat_words[:, 0:516].rearrange("p (h n) -> p h n", h=HEADS)
        gsq = knat_words.rearrange("p (g n) -> p g n", n=P)
        ctmp = upad.rearrange("p a b c -> p (a b c)")[:, 0:1024].rearrange("p (c t) -> p c t", c=4)
        iota_i = convt[:, 0, 0:P].bitcast(I32)
        cmean, crstd = convt[:, 0, :], convt[:, 1, :]

        r_ = small[:, 0:32]
        b_ = small[:, 32:64]
        bt_ = small[:, 64:96]
        rmax = small[:, 96:128]
        cmax = small[:, 128:144]
        m_t = small[:, 144:160]
        m_run = small[:, 160:192]
        mx_ = small[:, 192:200]
        dae = small[:, 200:248]
        ae2 = small[:, 248:272]
        ee = small[:, 272:304]
        den = small[:, 304:308]
        st = small[:, 308:340]
        sel16 = small[:, 360:376]
        sel3 = sel16[:, 0:3]
        onec = small[:, 340:341]

        rowd = {"b_mix": scr[:, 4096:5120], "post_mix": scr[:, 5120:6144], "b_ffn": scr[:, 6144:7168],
                "post_ffn": scr[:, 7168:8192], "b_mix2": scr[:, 8208:9232], "b_ffn2": hT_words[:, 0:1024]}

        ce = Carve()
        hs = ce(3, NB, D, dt=BF16)
        hs_quarter = [[hs[:, part, n // 2, :].rearrange("t (k p) -> t p k", k=KD)[:, n % 2 * 64:n % 2 * 64 + 64, :] for n in range(4)]
                      for part in range(3)]
        left = [xn[:, n // 2, n % 2 * 512:n % 2 * 512 + 512].rearrange("t (p k) -> t p k", k=KD) for n in range(4)]
        hTe = ce(KD, P)
        Sb = ce(NB, P, dt=BF16)
        Sw = ce(2, NB, P)
        Ct = ce(T)
        sg = ce(512)
        av = ce(512)
        aT = ce(4, P)
        Y = ce(D)
        mask = ce(NB, E1)
        wts = ce(NB, E1)
        rank = ce(NB, E1)
        sel = ce(NB, E1)
        tmpr = ce(NB, E1)
        max8 = ce(NB, 8)
        a_sh = ce(NB, F1)
        sg_sh = ce(NB, F1)
        aT_sh = ce(2, T)
        wr = ce(KD, E1)
        rt = ce(64)
        desc = ce(E1)
        over_row = tmpr.rearrange("p b e -> p (b e)")
        over_expert = over_row[:, 0:LIST].bitcast(I32)
        over_start = over_row[:, LIST:2 * LIST]
        over_pick = over_row[:, 2 * LIST:3 * LIST]
        over_idx, over_from, over_flag, over_place = (rt[:, c:c + 1] for c in (40, 41, 42, 43))
        over_shift = rt[:, 44:44 + NB]
        over_count = [small[:, 342 + n:343 + n].bitcast(I32) for n in range(2)]
        wr2 = gate[:, 1, 0:KD * 36].rearrange("p (k n) -> p k n", k=KD)

        c2 = Carve()
        qT2 = c2(4, T)
        kT2 = c2(4, T)
        vv2 = c2(NB, 512)
        u2 = c2(NB, 512)
        zg = c2(NB, 2 * D)
        oT2 = c2(4, T)
        dT2 = c2(4, T)
        plT2 = c2(4, T)
        poolw = c2(4, P)
        pexp = c2(2, 384)
        pT = c2(2, 384)
        TB = BUF[2][:, 0:2048].rearrange("p (h j) -> p h j", h=HEADS2)
        TBr = zg.rearrange("p b d -> p (b d)")[:, 0:2048].rearrange("p (h j) -> p h j", h=HEADS2)
        rowf = gate[:, 0, :]
        band = BUF[2][:, 2048:4096].rearrange("p (g s t) -> p g s t", g=4, s=NB)
        bgrow = BUF[2][:, 4096:6144]
        w2buf = [BUF[i % 2] for i in range(len(ITEMS2))]
        w2k = [w.rearrange("p (k n) -> p k n", k=KD) for w in w2buf]

        PS = [ctx.enter_context(nc.psum_tensor(f"PS{i}", [P, 512], F32)) for i in range(8)]

        def ada_item(n):
            return (0, int(n[3])) if n[:3] == "ada" else (1, int(n[3]))

        def is_gate(n):
            return ada_item(n)[1] in (2, 5)

        def col_at(n):
            s = ada_item(n)[1]
            return {0: 0, 1: 1, 3: 2, 4: 3}[s]

        gu1 = [BUF[s].rearrange("p (e c k n) -> p e c k n", e=G1, c=2, k=KD) for s in range(2)]
        dn1 = [BUF[2][:, s * 4096:(s + 1) * 4096].rearrange("p (e c n) -> p e c n", e=G1, c=2) for s in range(2)]
        gu2 = [BUF[s].rearrange("p (e k n) -> p e k n", e=G2, k=4) for s in range(3)]
        dn2 = [BUF[s].rearrange("p (e c n) -> p e c n", e=G2, c=2) for s in range(3)]

        wv = {n: BUF[i % 3] for n, i in AT.items()}
        ada_w = {n: wv[n].rearrange("p (k n) -> p k n", k=KD) for n in ITEMS if n[:3] in ("ada", "adb")}
        w_qkv = wv["in_qkv"].rearrange("p (k n) -> p k n", k=KD)
        w_og = wv["in_og"][:, 0:KD * 528].rearrange("p (k n) -> p k n", k=KD)
        w_conv = wv["in_conv"].rearrange("p (k n) -> p k n", k=KD)
        w_o = wv["w_out"].rearrange("p (k n) -> p k n", k=KD)
        sh_gu = wv["shared"][:, 0:4096].rearrange("p (k n) -> p k n", k=KD)
        sh_dn = wv["shared"][:, 4096:6144].rearrange("p (c n) -> p c n", c=2)

        def over_weights(L, s):
            F = (F1, F2)[L - 1]
            wide, tall = KD * F, F // P * D
            at = (W[:, s * BUFN:s * BUFN + wide], W[:, s * BUFN + wide:s * BUFN + 2 * wide],
                  W[:, s * BUFN + 2 * wide:s * BUFN + 2 * wide + tall]) if L == 1 else (BUF[0][:, 0:wide], BUF[1][:, 0:wide], BUF[2][:, 0:tall])
            return [w.rearrange("p (k n) -> p k n", k=k) for w, k in zip(at, (KD, KD, F // P))]

        def over_items(eng, L, item):
            eng.wait_ge(S["over_known"], L)
            most = (OVER1, OVER2)[L - 1]
            count = eng.value_load(over_count[L - 1][0:1, :], min_val=0, max_val=most)
            if L == 1:
                for s in range(3):
                    with eng.If(count > s):
                        item(s, s, s)
                with eng.If(count > 3):
                    with eng.Fori(1, (most + 2) // 3) as t:
                        for s in range(3):
                            with eng.If(3 * t + s < count):
                                item(3 * t + s, 3 * t + s, s)
            else:
                with eng.If(count > 0):
                    before = eng.value_load(over_count[0][0:1, :], min_val=0, max_val=OVER1)
                    with eng.Fori(0, most) as i:
                        with eng.If(i < count):
                            item(i, i + before, 0)
            return count

        block = ctx.enter_context(nc.Block())

        @block.sync
        def _(sp):
            def vec(tile, at, ap, n):
                sp.dma_start(vecs[at:at + n, tile, :], ap.rearrange("(k p) -> k p", p=P)).then_inc(S["vec_loaded"], 16)


            def row(dst, ap):
                sp.dma_start(dst, ap.partition_broadcast(P)).then_inc(S["row_loaded"], 16)

            def rows(ap):
                return ap.rearrange("(k p) n -> p k n", p=P)

            def long_rows(ap, k):
                return ap.rearrange("(p k) n -> p k n", k=k)

            for n, i in AT.items():
                if i == 1:
                    sp.dma_start(x[:], A["x"][0].rearrange("(b p) d -> p b d", p=P)).then_inc(S["x_loaded"], 16)
                    vec(0, C_CONVB, A["conv_b"][0], 4)
                    vec(0, C_LNG, A["conv_ln_g"][0], 4)
                    vec(0, C_LNB, A["conv_ln_b"][0], 4)
                    vec(0, C_POOLS, A["pool_scale_2"][0], 4)
                    vec(0, C_BQK, A["b_in"][0][0:512], 4)
                    vec(0, C_BCONV, A["b_in"][0][1552:2576], 8)
                    vec(1, 0, A["b_ada"][0], 48)
                    vec(1, 48, A["b_ada_2"][0], 48)
                    sp.dma_start(vecs[0:TAPS * 4, 2, :], A["conv_w"][0].rearrange("t (c p) -> (t c) p", p=P)).then_inc(S["vec_loaded"], 16)
                if i == 2:
                    sp.dma_start(ctxt, A["ctx"][0].rearrange("(b p) d -> p b d", p=P)).then_inc(S["ctx_loaded"], 16)
                if i == 3:
                    row(rowb, A["b_in"][0][256:1552])
                    row(normg, A["mlstm_norm_g"][0].rearrange("h d -> (h d)"))
                    row(rowv, A["b_out"][0])
                    row(brt[:, 0:64], A["b_router"][0])
                    row(brt[:, 64:68], A["b_router_group_2"][0])
                    row(brt[:, 68:100], A["b_router_expert_2"][0])
                    row(small[:, 344:360], A["b_gate"][0].rearrange("a b -> (a b)"))
                if i >= 3:
                    sp.wait_ge(S["stream_used"], i - 2)
                loaded = S[f"stream_loaded{i % 3}"]
                if n[:3] in ("ada", "adb"):
                    b, s = ada_item(n)
                    w = A["w_ada_2" if b else "w_ada"][0]
                    sp.dma_start(ada_w[n], rows(w[:, s * D:(s + 1) * D])).then_inc(loaded, 16)
                elif n == "in_qkv":
                    sp.dma_start(w_qkv, rows(A["w_in"][0][:, 0:1024])).then_inc(loaded, 16)
                elif n == "in_og":
                    sp.dma_start(w_og, rows(A["w_in"][0][:, 1024:1552])).then_inc(loaded, 16)
                elif n == "in_conv":
                    sp.dma_start(w_conv, rows(A["w_in"][0][:, 1552:2576])).then_inc(loaded, 16)
                elif n == "w_out":
                    sp.dma_start(w_o, rows(A["w_out"][0])).then_inc(loaded, 16)
                else:
                    sp.dma_start(sh_gu[:, :, 0:F1], rows(A["ws_gate"][0])).then_inc(loaded, 16)
                    sp.dma_start(sh_gu[:, :, F1:2 * F1], rows(A["ws_up"][0])).then_inc(loaded, 16)
                    sp.dma_start(sh_dn, rows(A["ws_down"][0])).then_inc(loaded, 16)
            def load_gu1(g, s, members=range(G1)):
                for e in members:
                    for c, name in enumerate(("we_gate", "we_up")):
                        sp.dma_start(gu1[s][:, e, c, :, :], long_rows(A[name][0, g * G1 + e], KD)).then_inc(S[f"e1_gu{s}"], 16)

            def load_dn1(g, s):
                for e in range(G1):
                    sp.dma_start(dn1[s][:, e, :, :], long_rows(A["we_down"][0, g * G1 + e], F1 // P)).then_inc(S[f"e1_dn{s}"], 16)

            sp.wait_ge(S["stream_used"], AT["w_out"] + 1)
            load_gu1(0, 0)
            load_dn1(0, 0)
            load_dn1(1, 1)
            sp.wait_ge(S["sh_gateup"], NB)
            load_gu1(1, 1, [0])
            sp.wait_ge(S["stream_used"], AT["shared"] + 1)
            load_gu1(1, 1, [1])
            with sp.Fori(0, NG1 // 2 - 1) as i:
                for s in range(2):
                    sp.wait_ge(S["e1_gateup"], 2 * i + s + 1)
                    load_gu1(2 * i + 2 + s, s)
                    sp.wait_ge(S["e1_down"], 2 * i + s + 1)
                    load_dn1(2 * i + 2 + s, s)

            def over_loads(L, names):
                def item(i, n, s):
                    expert = sp.value_load(over_expert[0:1, bass.ds(i, 1)], min_val=1, max_val=(E1, E2)[L - 1]) - 1
                    if L == 2:
                        sp.wait_ge(S["over_done"], n + 2)
                    elif not isinstance(i, int):
                        sp.wait_ge(S["over_done"], n - 1)
                    else:
                        sp.wait_ge(*((S["e1_gateup"], NG1 - 1), (S["e1_gateup"], NG1), (S["e1_down"], NG1))[s])
                    for dst, name in zip(over_weights(L, s), names):
                        sp.dma_start(dst, long_rows(A[name][0, expert], dst.shape[1])).then_inc(S[f"over_loaded{s}" if L == 1 else "over_loaded"], 16)
                return over_items(sp, L, item)

            count = over_loads(1, ("we_gate", "we_up", "we_down"))
            with sp.If(count > 0):
                sp.wait_ge(S["y_done"], 4)

            for n, i in AT2.items():
                if i < 2:
                    sp.wait_ge(S["e1_gateup"], NG1 - 1 + i)
                else:
                    sp.wait_ge(S["stream2_used"], i - 1)
                loaded = S[f"stream2_loaded{i % 2}"]
                if i < 4:
                    sp.dma_start(w2k[i], rows(A["w_in_2"][0][:, i * D:(i + 1) * D])).then_inc(loaded, 16)
                elif n == "branches":
                    sp.dma_start(w2k[i][:, 0:4, :], rows(A["w_branch_attn_2"][0])).then_inc(loaded, 16)
                    sp.dma_start(w2k[i][:, 4:8, :], rows(A["w_branch_pool_2"][0])).then_inc(loaded, 16)
                else:
                    sp.dma_start(w2k[i], rows(A["w_out_2"][0])).then_inc(loaded, 16)
                if i == 0:
                    sp.wait_ge(S["e1_down"], NG1)
                    sp.dma_start(band, A["band"].rearrange("g (b p) t -> p g b t", p=P)).then_inc(S["band_loaded"], 16)
                    sp.dma_start(bgrow, A["b_gate_2"][0].partition_broadcast(P)).then_inc(S["band_loaded"], 16)

            def load2(g, q):
                kind, half = q // 2, q % 2
                w = A[("w_expert_gate_2", "w_expert_up_2", "w_expert_down_2")[kind]]
                for e in range(G2):
                    if kind < 2:
                        src = long_rows(w[0, g * G2 + e], KD)[:, 4 * half:4 * half + 4, :]
                        dst = gu2[q % 3][:, e, :, :]
                    else:
                        src = long_rows(w[0, g * G2 + e], F2 // P)[:, 2 * half:2 * half + 2, :]
                        dst = dn2[q % 3][:, e, :, :]
                    sp.dma_start(dst, src).then_inc(S[f"e2_piece{q % 3}"], 16)

            sp.wait_ge(S["stream2_used"], 5)
            load2(0, 0)
            sp.wait_ge(S["attn_done"], 1)
            load2(0, 2)
            sp.wait_ge(S["stream2_used"], 6)
            load2(0, 1)
            for q in range(3, 6):
                sp.wait_ge(S["e2_gateup"], q - 2)
                load2(0, q)
            with sp.Fori(0, NG2 - 1) as g:
                for q in range(6):
                    if q < 1:
                        sp.wait_ge(S["e2_gateup"], 4 * g + 4)
                    elif q < 3:
                        sp.wait_ge(S["e2_down"], 2 * g + q)
                    else:
                        sp.wait_ge(S["e2_gateup"], 4 * g + 4 + q - 2)
                    load2(g + 1, q)

            over_loads(2, ("w_expert_gate_2", "w_expert_up_2", "w_expert_down_2"))

            for b in range(NB):
                sp.wait_ge(S["out_ready"], b + 1)
                sp.dma_start(out[0][b * P:(b + 1) * P, :], xn[:, b, :]).then_inc(S["stored"], 16)
            sp.wait_ge(S["stored"], 16 * NB)

        @block.gpsimd
        def _(pool):
            step = Steps(pool, S["pool_step"])
            g = nc.gpsimd
            step(g.memset(ones[:], 1.0), wait=False)
            step(g.memset(zeros[:], 0.0), wait=False)
            step(g.memset(ident[:], 0.0), wait=False)
            step(g.memset(mneg, 0.0), wait=False)
            step(g.memset(mbig, 0.0), wait=False)
            step(g.memset(sc[:], 0.0), wait=False)
            step(g.memset(onec, 1.0), wait=False)
            step(g.memset(upad, 0.0), wait=False)
            step(g.memset(v1[:, :, :, DV:DV + 1], 1.0))

            def keep(out_, in_, base, mult, stepf, fill, op=ALU.is_ge, wait=True):
                step(g.affine_select(out=out_, in_=in_, compare_op=op, fill=fill, base=base,
                                     pattern=[[stepf, P]], channel_multiplier=mult), wait=wait)

            keep(ident[:], ident[:], 0, 1, -1, 1.0, ALU.not_equal, wait=False)
            keep(tri[:, 0, :], ones[:], 0, -1, 1, 0.0, wait=False)
            keep(tri[:, 1, :], ones[:], 0, 1, -1, 0.0, wait=False)
            keep(mneg[:, 0, :], mneg[:, 0, :], 0, 1, -1, NEG, wait=False)
            keep(mneg[:, 1, :], mneg[:, 1, :], 0, -1, 1, NEG, wait=False)
            keep(mbig[:, 0, :], mbig[:, 0, :], 0, -1, 1, 1e4, wait=False)
            keep(mbig[:, 1, :], mbig[:, 1, :], 0, 1, -1, 1e4, wait=False)
            step(g.iota(iota_i, pattern=[[1, P]], base=0, channel_multiplier=0))
            step(g.memset(flip[:], 0.0))
            keep(flip[:], flip[:], 1 - P, 1, 1, 1.0, ALU.not_equal)
            step(g.tensor_copy(iota[:], iota_i), S["consts"])

            pool.wait_ge(S["u_ready"], 4)
            for i, taps in ((3, TAPS), (2, SPLIT_TAP)):
                acc = cacc[:, i, :].rearrange("p (r t) -> p r t", r=ROWS)
                step(g.tensor_scalar(acc, upad[:, i, :, 0:ROW], convw[:, i:i + 1], cols[:, C_CONVB + i:C_CONVB + i + 1], ALU.mult, ALU.add))
                for j in range(1, taps):
                    tmp = convt[:, j % 2, :].rearrange("p (r t) -> p r t", r=ROWS)
                    step(g.tensor_scalar(tmp, upad[:, i, :, j:j + ROW], convw[:, 4 * j + i:4 * j + i + 1], None, ALU.mult))
                    step(g.tensor_tensor(acc, acc, tmp, ALU.add), S["conv_ready"] if j == taps - 1 else None)
            pool.wait_ge(S["hn_ready"], 1)
            for name, src in (("b_mix", A["b_ada"][0][2 * D:3 * D]), ("post_mix", A["g_post_mix"][0]),
                              ("b_ffn", A["b_ada"][0][5 * D:6 * D]), ("post_ffn", A["g_post_ffn"][0]),
                              ("b_mix2", A["b_ada_2"][0][2 * D:3 * D]), ("b_ffn2", A["b_ada_2"][0][5 * D:6 * D])):
                pool.dma_start(rowd[name], src.partition_broadcast(P)).then_inc(S["rowd_loaded"], 16)
            pool.wait_ge(S["gates_made"], 1)
            pool.wait_ge(S["mixT_conv"], 4)
            pool.dma_start(wr, A["w_router"][0].rearrange("(k p) n -> p k n", p=P)).then_inc(S["wr_loaded"], 16)

            pool.wait_ge(S["x2_ready"], 1)
            pool.wait_ge(S["bias_stored"], 16)
            pool.dma_start(TBr, bass.AP(bias_dram.tensor, 0, [[1, P], [T + P - 1, HEADS2], [1, T]])).then_inc(S["bias_loaded"], 16)
            pool.dma_start(rowf, A["norm_f_g_2"].partition_broadcast(P)).then_inc(S["poolw_loaded"], 16)
            pool.dma_start(poolw, A["pool_w_2"][0].rearrange("g c d -> c g d")).then_inc(S["poolw_loaded"], 16)
            for dst, name in ((wr2[:, :, 0:4], "w_router_group_2"), (wr2[:, :, 4:36], "w_router_expert_2")):
                pool.dma_start(dst, A[name][0].rearrange("(k p) n -> p k n", p=P)).then_inc(S["wr_loaded"], 16)
            pool.wait_ge(S["tb_flipped"], 4)
            step(g.affine_select(out=TB, in_=TB, compare_op=ALU.is_ge, fill=NEG, base=P, pattern=[[0, HEADS2], [-1, T]],
                                 channel_multiplier=1), S["tb_ready"])
            pool.wait_ge(S["x3_ready"], 1)
            step(g.tensor_scalar(desc, iota[:, 0:E1], -1.0, float(E1), ALU.mult, ALU.add), S["desc_ready"])

        @block.scalar
        def _(act):
            a = nc.scalar
            step = Steps(act, S["act_step"])

            def vec(tile, at, ap, n):
                act.dma_start(vecs[at:at + n, tile, :], ap.rearrange("(k p) -> k p", p=P)).then_inc(S["vec_loaded"], 16)

            vec(0, C_C, A["c"][0], 8)
            vec(0, C_CTX, A["c_ctx"], 8)
            vec(0, C_2, A["c_2"][0], 8)
            vec(0, C_GPRE, A["g_pre_mix"][0], 8)
            vec(0, C_GFFN, A["g_pre_ffn"][0], 8)
            vec(0, C_N1, A["norm1_g_2"][0], 8)
            vec(0, C_N2, A["norm2_g_2"][0], 8)
            act.dma_start(relb, A["rel_bias_2"]).then_inc(S["rel_loaded"], 16)
            act.dma_start(onehot, A["bucket"]).then_inc(S["rel_loaded"], 16)

            act.wait_ge(S["bias_mm"], 1)
            step(a.copy(biasrow, PS[7][0:HEADS2, 0:T + P - 1]))
            act.dma_start(bias_dram, biasrow).then_inc(S["bias_stored"], 16)
            act.wait_ge(S["consts"], 1)
            act.wait_ge(S["cols_ready"], 1)
            for v in range(3):
                step(a.activation(sc[:, :, v], cols[:, 8 * v:8 * v + 8], ACT.Silu), S["sc_ready"], wait=False)

            def ada(n):
                i, k = AT[n], ADA.index(n)
                act.wait_ge(S["stream_used"], i + 1)
                for h in range(2):
                    step(a.copy(ada_rows[:, h * 512:(h + 1) * 512], PS[5 + h][:]), S["ada_rows_ready"], wait=False)
                act.wait_ge(S["ada_summed"], k + 1)
                b, s = ada_item(n)
                if is_gate(n):
                    dst = gate if b == 0 else gate2
                    for h in range(2):
                        step(a.copy(dst[:, s // 3, h * 512:(h + 1) * 512], PS[5 + h][:]), S["ada_ready"], wait=False)
                else:
                    step(a.copy(modc[:, b, col_at(n), :, :].rearrange("p k v -> p (k v)"), PS[5][:, 0:24]),
                         S["ada_ready"], wait=False)
            for n, (src, loaded) in enumerate(((x, "x_loaded"), (ctxt, "ctx_loaded"))):
                act.wait_ge(S[loaded], 16)
                for b in range(NB):
                    step(a.activation(hT_words[:, b * D:(b + 1) * D], src[:, b, :], ACT.Square,
                                      accum_out=st[:, 2 * n + b:2 * n + b + 1]), S["norm_sq"])
                act.wait_ge(S["norm_ms"], n + 1)
                mean = st[:, 4 + 2 * n:6 + 2 * n]
                step(a.activation(mean, mean, ACT.Sqrt), S["norm_root"])
                if n == 0:
                    ada("ada0")

            ada("ada1")

            act.wait_ge(S["bias_stored"], 16)
            for k in range(KD):
                act.wait_ge(S["modT"], 5 + k // 2)
                act.wait_ge(S["am_ready"], 1)
                step(a.activation(hTc[:, k, :], PS[4 + k // 2][:, (k % 2) * T:(k % 2 + 1) * T], ACT.Identity, scale=am[:, 1, k:k + 1], bias=modc[:, 0, 0, k, 1:2]),
                     S["hTc_ready"], wait=False)

            ada("ada2")
            ada("ada3")
            for i in range(4):
                act.wait_ge(S["proj_mm"], 13 + i)
                act.wait_ge(S["modT"], 8)
                step(a.activation(usig[:, i, :], PS[(12 + i) % 5][:, T:2 * T], ACT.Sigmoid,
                                  bias=cols[:, C_BCONV + 4 + i:C_BCONV + 5 + i]), S["usig_ready"], wait=False)
            act.wait_ge(S["proj_ev"], 10)
            step(a.activation(osig, osig, ACT.Sigmoid), S["osig_ready"], wait=False)
            act.wait_ge(S["exp_in"], 1)
            step(a.activation(lft, lft, ACT.Exp))
            step(a.activation(lft, lft, ACT.Ln, bias=onec), S["exp_out"])
            ada("ada4")
            for n in (2, 3):
                act.wait_ge(S["exp_in"], n)
                step(a.activation(wst if n == 2 else dae, wst if n == 2 else dae, ACT.Exp), S["exp_out"])
            ada("ada5")
            act.wait_ge(S["exp_in"], 4)
            step(a.activation(ee, ee, ACT.Exp), S["exp_out"])
            ada("adb0")
            act.wait_ge(S["qk_mm"], 2)
            for r in range(2):
                step(a.copy(qk.rearrange("p c (q r) t -> p c q r t", r=2)[:, :, :, r, :],
                            PS[r][:].rearrange("p (c q t) -> p c q t", c=2, q=2)), S["qk_ready"], wait=False)
            ada("adb1")
            for gi, n in enumerate((None, "adb2", "adb3", "adb4", "adb5")):
                if gi < 4:
                    act.wait_ge(S["exp_in"], gi + 5)
                    step(a.activation(dts[gi % 2], dts[gi % 2], ACT.Exp, scale=-1.0), S["exp_out"])
                if gi:
                    ada(n)
            act.wait_ge(S["norm_ms"], 3)
            step(a.activation(st[:, 8:16], st[:, 8:16], ACT.Sqrt), S["norm_root"])
            act.wait_ge(S["norm_ms"], 4)
            step(a.activation(crstd, crstd, ACT.Sqrt), S["norm_root"])
            for i in range(4):
                act.wait_ge(S["cn_ready"], 1)
                step(a.activation(mixT[:, 4 + i, :], ctmp[:, i, :], ACT.Silu, scale=cols[:, C_LNG + i:C_LNG + i + 1],
                                  bias=cols[:, C_LNB + i:C_LNB + i + 1]), S["mixT_conv"], wait=False)

            def norm(n, src):
                for b in range(NB):
                    act.wait_ge(S["norm_in"], 2 * n + b + 1)
                    step(a.activation(ada_rows[:], src[:, b, :], ACT.Square, accum_out=st[:, 24 + b:25 + b]), S["norm_sq"])
                    act.wait_ge(S["norm_ms"], 2 * n + b + 5)
                    step(a.activation(st[:, 26 + b:27 + b], st[:, 26 + b:27 + b], ACT.Sqrt), S["norm_root"])

            def split_h(L, part):
                for n in range(4):
                    if part == 0:
                        act.wait_ge(S["backT"], 4 * (L - 1) + n + 1)
                    else:
                        act.wait_ge(S["hs_left"], 8 * (L - 1) + 4 * (part - 1) + n + 1)
                    a.copy(hs_quarter[part][n], PS[n][:].rearrange("t (p k) -> t p k", k=KD) if part == 0 else left[n]).then_inc(S["hs_part"], 1)

            def experts(L, G, NG, F, GU):
                DN = GU // 2 if GU > 1 else 1
                pre, before = f"e{L}_", (L - 1) * NG1

                def rows_out(n):
                    for q in range(2):
                        act.wait_ge(S["x_gather"], 2 * (n + before) + 1 + q)
                        a.copy(hTe[:, 4 * q:4 * q + 4, :], PS[4 + q][:].rearrange("p (k s) -> p k s", k=4)).then_inc(S["x_hTe"], 1)

                def body(g, last=False):
                    act.wait_ge(S[pre + "gateup"], GU * g + max(GU // 2, 1))
                    a.activation(sg[:, 0:F], PS[4][:, 0:F], ACT.Silu).then_inc(S["x_sg"], 1)
                    if not last:
                        rows_out(g + 1)
                    act.wait_ge(S[pre + "down"], DN * g + DN)
                    for h in range(2):
                        a.copy(Y[:, h * 512:(h + 1) * 512], PS[6 + h][:]).then_inc(S["x_Y"], 1)

                rows_out(0)
                body(0)
                with act.Fori(0, NG // 2 - 1) as i:
                    body(2 * i + 1)
                    body(2 * i + 2)
                body(NG - 1, last=True)

                def item(i, n, s):
                    for q in range(2):
                        act.wait_ge(S["over_gather"], 2 * n + 1 + q)
                        a.copy(hTe[:, 4 * q:4 * q + 4, :], PS[4 + q][:].rearrange("p (k s) -> p k s", k=4)).then_inc(S["over_hTe"], 1)
                    act.wait_ge(S["over_gateup"], 2 * n + 1)
                    a.activation(sg[:, 0:F], PS[4][:, 0:F], ACT.Silu).then_inc(S["over_sg"], 1)
                    act.wait_ge(S["over_down"], n + 1)
                    for h in range(2):
                        a.copy(Y[:, h * 512:(h + 1) * 512], PS[6 + h][:]).then_inc(S["over_Y"], 1)
                over_items(act, L, item)

            norm(0, xn)
            norm(1, x)
            act.wait_ge(S["router_mm"], 1)
            step(a.copy(ada_rows[0:E1, 0:T], PS[4][0:E1, 0:T]), S["ada_rows_ready"], wait=False)
            act.wait_ge(S["router_mm"], 2)
            step(a.activation(sel, PS[4][:, 0:NB * E1].rearrange("p (b e) -> p b e", b=NB), ACT.Sigmoid), S["route_sig"])
            for part in range(3):
                split_h(1, part)
            for b in range(NB):
                act.wait_ge(S["sh_gateup"], b + 1)
                step(a.activation(sg_sh[:, b, :], PS[6 + b][:, 0:F1], ACT.Silu), S["sh_sg"], wait=False)
            experts(1, G1, NG1, F1, 1)
            norm(2, xn)

            norm(3, x)
            for h in range(HEADS2):
                act.wait_ge(S["smax_ready"], h + 1)
                for b in range(NB):
                    q = slice(0, P) if b == 0 else slice(P, P + T)
                    step(a.activation(pexp[:, h % 2, q], pexp[:, h % 2, q], ACT.Exp, bias=st[:, 2 * (h % 2) + b:2 * (h % 2) + b + 1],
                                      accum_out=st[:, 4 + 2 * (h % 2) + b:5 + 2 * (h % 2) + b]), S["sexp_ready"])
            for n in range(8):
                act.wait_ge(S["zg_biased"], n + 1)
                half, b, h = n // 4, n // 2 % 2, n % 2
                q = slice(half * D + h * 512, half * D + h * 512 + 512)
                step(a.activation(zg[:, b, q], zg[:, b, q], ACT.Sigmoid), S["zg_ready"], wait=False)
            norm(4, x)
            act.wait_ge(S["router_mm"], 3)
            step(a.copy(ada_rows[0:36, 0:T], PS[4][0:36, 0:T]), S["ada_rows_ready"], wait=False)
            act.wait_ge(S["zexp_in"], 1)
            step(a.activation(rt[:, 0:8], rt[:, 0:8], ACT.Exp), S["zexp"])
            split_h(2, 0)
            act.wait_ge(S["zexp_in"], 2)
            step(a.activation(rt[:, 24:26], rt[:, 24:26], ACT.Exp), S["zexp"])
            split_h(2, 1)
            split_h(2, 2)
            experts(2, G2, NG2, F2, 4)
            norm(5, x)



        @block.tensor
        def _(pe):
            mm, tr = nc.tensor.matmul, nc.tensor.transpose

            pe.wait_ge(S["vec_loaded"], 16 * 16)
            pe.wait_ge(S["consts"], 1)
            tr(PS[0][:, 0:N_COLS], vecs[0:N_COLS, 0, :], ident[0:N_COLS, 0:N_COLS])
            tr(PS[0][:, 128:224], vecs[0:96, 1, :], ident[0:96, 0:96])
            tr(PS[0][:, 256:380], vecs[0:TAPS * 4, 2, :], ident[0:TAPS * 4, 0:TAPS * 4]).then_inc(S["vecT"], 1)
            pe.wait_ge(S["rel_loaded"], 32)
            mm(PS[7][0:HEADS2, 0:T + P - 1], relb, onehot, start=True, stop=True).then_inc(S["bias_mm"], 1)

            def ada_parts(n):
                i, k = AT[n], ADA.index(n)
                pe.wait_ge(S[f"stream_loaded{i % 3}"], 16 * (i // 3 + 1))
                if k:
                    pe.wait_ge(S["ada_ready"], ada_done[k])
                for h in range(2):
                    for kk in range(2):
                        for j in range(4):
                            last = mm(PS[5 + h][32 * j:32 * j + 32, :], sc[:, 2 * j + kk, :],
                                      ada_w[n][:, 2 * j + kk, h * 512:(h + 1) * 512], start=(kk == 0), stop=(kk == 1))
                last.then_inc(S["stream_used"], 1)

            def ada_sums(n):
                k = ADA.index(n)
                pe.wait_ge(S["ada_rows_ready"], 2 * (k + 1))
                b, s = ada_item(n)
                if is_gate(n):
                    for h in range(2):
                        last = mm(PS[5 + h][:, :], selrow[:, b, :], ada_rows[:, h * 512:(h + 1) * 512], start=True, stop=True)
                else:
                    for j in range(KD):
                        last = mm(PS[5][:, 3 * j:3 * j + 3], ada_rows[:, j * P:(j + 1) * P], sel3, start=True, stop=True)
                last.then_inc(S["ada_summed"], 1)

            def ada(n):
                ada_parts(n)
                ada_sums(n)

            pe.wait_ge(S["sc_ready"], 3)
            pe.wait_ge(S["sel_ready"], 1)
            ada("ada0")
            for n, src in enumerate((xn, ctxt)):
                if n:
                    ada("ada1")
                    pe.wait_ge(S["ada_ready"], ada_done[2])
                pe.wait_ge(S["xnorm_ready"], n + 1)
                for k in range(KD):
                    for b in range(NB):
                        last = tr(PS[4 * n + k // 2][:, (k % 2) * T + b * P:(k % 2) * T + (b + 1) * P],
                                  src[:, b, k * P:(k + 1) * P], ident[:])
                    if k % 2:
                        last.then_inc(S["modT"], 1)

            pe.wait_ge(S["h_ready"], KD)
            rows_of = [(hT, 0), (hT, 1), (hTc, 0), (hTc, 1)]

            def project(t, parts, signal=None):
                if t >= 5:
                    pe.wait_ge(S["proj_ev"], t - 4)
                for at, n, lhs, rhs in parts:
                    for k in range(KD):
                        last = mm(PS[t % 5][:, at:at + n], lhs(k), rhs(k), start=(k == 0), stop=(k == KD - 1))
                last.then_inc(S["proj_mm"], 1)

            def feat(w, c0):
                return lambda k: w[:, k, c0:c0 + P]

            def toks(src, b):
                return lambda k: src[:, k, b * P:(b + 1) * P]

            def alltoks(src):
                return lambda k: src[:, k, :]

            def wcols(w, c0, n):
                return lambda k: w[:, k, c0:c0 + n]

            i = AT["in_qkv"]
            pe.wait_ge(S[f"stream_loaded{i % 3}"], 16 * (i // 3 + 1))
            project(0, [(m * T, T, feat(w_qkv, m * P), alltoks(hT)) for m in range(2)])
            project(1, [(m * T, T, feat(w_qkv, 256 + m * P), alltoks(hT)) for m in range(2)])
            pe.wait_ge(S["hTc_ready"], KD)
            project(2, [(m * T, T, toks(hTc, m), wcols(w_qkv, 256, 256)) for m in range(2)])
            pe.wait_ge(S["proj_ev"], 2)
            for m in range(2):
                for b in range(NB):
                    last = tr(PS[3][:, b * T + m * P:b * T + (m + 1) * P], kT[:, m, b * P:(b + 1) * P], ident[:])
            last.then_inc(S["proj_mm"], 1)
            for c, (src, b) in enumerate(rows_of):
                project(4 + c, [(0, 512, toks(src, b), wcols(w_qkv, 512, 512))])
            pe.wait_ge(S["proj_mm"], 8)
            pe.sem_inc(S["stream_used"], 1)
            ada("ada2")
            i = AT["in_og"]
            pe.wait_ge(S[f"stream_loaded{i % 3}"], 16 * (i // 3 + 1))
            for b in range(NB):
                project(8 + b, [(0, 512, toks(hT, b), wcols(w_og, 0, 512))])
            pe.wait_ge(S["proj_ev"], 6)
            for kk in range(4):
                for j in range(4):
                    last = mm(PS[0][32 * j:32 * j + 16, 0:T], w_og[:, 2 * kk + j % 2, 512:528], (hT, hTc)[j // 2][:, 2 * kk + j % 2, :],
                              start=(kk == 0), stop=(kk == 3))
            last.then_inc(S["proj_mm"], 1)
            pe.wait_ge(S["proj_ev"], 11)
            for c in range(4):
                half, b = slice(64 * (c // 2), 64 * (c // 2) + 64), c % 2
                last = mm(PS[(1, 7)[c // 2]][:, 16 * b:16 * b + 16], ada_rows[half, b * P:(b + 1) * P], sel16[half, :], start=True, stop=True)
            last.then_inc(S["proj_mm"], 1)
            pe.wait_ge(S["proj_mm"], 12)
            pe.sem_inc(S["stream_used"], 1)
            ada("ada3")
            i = AT["in_conv"]
            pe.wait_ge(S[f"stream_loaded{i % 3}"], 16 * (i // 3 + 1))
            for m in range(4):
                project(12 + m, [(0, T, feat(w_conv, m * P), alltoks(hT)), (T, T, feat(w_conv, 512 + m * P), alltoks(hT))])

            pe.wait_ge(S["proj_mm"], 16)
            pe.sem_inc(S["stream_used"], 1)
            ada("ada4")
            pe.wait_ge(S["lf_ready"], 1)
            for d in range(2):
                mm(PS[0][:, 16 * d:16 * d + 16], tri[:, d, :], LF[:, :, d, :], start=True, stop=True)
            mm(PS[0][:, 32:64], ones[:], LF.rearrange("p c d h -> p (c d h)"), start=True, stop=True).then_inc(S["gate_mm"], 1)

            for g in range(8):
                pe.wait_ge(S["diag_ready"], g + 1)
                if g >= 2:
                    pe.wait_ge(S["rows_done"], g - 1)
                mm(PS[1 + g % 2][:, :], ones[:], diag[:, g % 2, :, :].rearrange("p h t -> p (h t)"),
                   start=True, stop=True).then_inc(S["row_mm"], 1)

            ada("ada5")

            for j in range(3):
                for d in range(2):
                    n = 2 * j + d
                    pe.wait_ge(S["kw_ready"], n + 1)
                    if j:
                        pe.wait_ge(S["state_done"], n - 1)
                    for h in range(HEADS):
                        half = slice(64 * (h % 2), 64 * (h % 2) + 64)
                        last = mm(PS[3 + d][half, (h // 2) * 129:(h // 2) * 129 + 129], kw[:, n, h * DK:(h + 1) * DK],
                                  v1[:, STATE_CHUNK[j][d], h, :], start=True, stop=True)
                    last.then_inc(S["state_mm"], 1)
                if j == 0:
                    ada("adb0")

            pe.wait_ge(S["rows_done"], 8)
            for r in range(2):
                half = slice(64 * r, 64 * r + 64)
                for c in range(2):
                    for hp in range(2):
                        last = mm(PS[r][:, (2 * c + hp) * P:(2 * c + hp + 1) * P], kT[half, hp, c * P:(c + 1) * P],
                                  qT[half, hp, c * P:(c + 1) * P], start=True, stop=True)
                last.then_inc(S["qk_mm"], 1)
            ada("adb1")

            def seen_largest(gi):
                pe.wait_ge(S["diagm_ready"], gi + 1)
                mm(PS[gi % 2][:, :], ones[:], diag[:, gi % 2, :, :].rearrange("p h t -> p (h t)"),
                   start=True, stop=True).then_inc(S["mrow_mm"], 1)

            pe.wait_ge(S["qk_ready"], 2)
            pe.wait_ge(S["state_done"], 6)
            seen_largest(0)
            seen_largest(1)
            for gi, n in enumerate(("adb2", "adb3", "adb4", "adb5")):
                c, d = gi // 2, gi % 2
                ada_parts(n)
                pe.wait_ge(S["sT_ready"], gi + 1)
                if gi:
                    pe.wait_ge(S["hm_ready"], gi)
                for h in range(HEADS):
                    hp, half = h // 2, slice(64 * (h % 2), 64 * (h % 2) + 64)
                    at = slice((h % 2) * 129, (h % 2) * 129 + 129)
                    mm(PS[(2, 4)[hp]][:, at], dts[gi % 2][:, h, :], v1[:, c, h, :], start=True, stop=True)
                    last = mm(PS[(3, 7)[h % 2]][:, hp * 129:hp * 129 + 129], qT[half, hp, c * P:(c + 1) * P],
                              state[half, 0 if c == d else 1, d, hp, :], start=True, stop=True)
                last.then_inc(S["out_mm"], 1)
                ada_sums(n)
                if gi < 2:
                    seen_largest(gi + 2)

            pe.wait_ge(S["hm_ready"], 4)
            pe.wait_ge(S["conv_ready"], 1)
            pe.wait_ge(S["conv_taps"], 2 * TAPS + 1)
            for i in range(4):
                last = mm(PS[4][:, 0:T], ones[:], cacc[:, i, :], start=(i == 0), stop=(i == 3))
            last.then_inc(S["cmean_mm"], 1)
            pe.wait_ge(S["hn_ready"], 1)
            pe.wait_ge(S["ada_ready"], ada_done[12])
            for b in range(NB):
                for h in range(HEADS):
                    last = tr(PS[5 + b][:, h * P:(h + 1) * P], hm[:, b, h * P:(h + 1) * P], ident[:])
                last.then_inc(S["hmT"], 1)
            pe.wait_ge(S["csq_ready"], 1)
            for i in range(4):
                last = mm(PS[7][:, 0:T], ones[:], cacc[:, i, :], start=(i == 0), stop=(i == 3))
            last.then_inc(S["cvar_mm"], 1)

            i = AT["w_out"]
            pe.wait_ge(S["mixT_m"], 2)
            pe.wait_ge(S[f"stream_loaded{i % 3}"], 16 * (i // 3 + 1))
            for part in range(2):
                if part:
                    pe.wait_ge(S["mixT_conv"], 4)
                for b in range(NB):
                    for h in range(2):
                        for k in range(4 * part, 4 * part + 4):
                            last = mm(PS[2 * b + h][:, :], mixT[:, k, b * P:(b + 1) * P], w_o[:, k, h * 512:(h + 1) * 512],
                                      start=(k == 0), stop=(k == KD - 1))
                        if part:
                            last.then_inc(S["stream_used"] if b and h else S["proj_mm"], 1)

            def modulated(n, src):
                pe.wait_ge(S["xnorm_ready"], n + 3)
                for k in range(KD):
                    for b in range(NB):
                        last = tr(PS[k // 2][:, (k % 2) * T + b * P:(k % 2) * T + (b + 1) * P],
                                  src[:, b, k * P:(k + 1) * P], ident[:])
                    if k % 2:
                        last.then_inc(S["modT"], 1)
                pe.wait_ge(S["h_ready"], KD * (n + 2))

            def routed(L, w, ne):
                pe.wait_ge(S["wr_loaded"], 16 if L == 1 else 48)
                for k in range(KD):
                    last = mm(PS[4][0:ne, 0:T], w[:, k, :], hT[:, k, :], start=(k == 0), stop=(k == KD - 1))
                last.then_inc(S["router_mm"], 1)
                for b in range(NB):
                    for k in range(KD):
                        last = tr(PS[2 * b + k // 4][:, (k % 4) * P:(k % 4 + 1) * P], hT[:, k, b * P:(b + 1) * P], ident[:])
                        if k % 4 == 3:
                            last.then_inc(S["backT"], 1)
                    if b == 0:
                        pe.wait_ge(S["ada_rows_ready"], 2 * len(ADA) + L)
                        for n in range(NB):
                            last = tr(PS[4][:, n * ne:(n + 1) * ne], ada_rows[0:ne, n * P:(n + 1) * P], ident[0:ne, 0:ne])
                        last.then_inc(S["router_mm"], 1)

            def ranks(L, ne):
                pe.wait_ge(S["mask_ready"], L)
                at = 256
                mm(PS[4][:, at:at + ne], tri[:, 0, :], mask[:, 0, 0:ne], start=True, stop=True)
                mm(PS[4][:, at + ne:at + 2 * ne], tri[:, 0, :], mask[:, 1, 0:ne], start=True, stop=False)
                mm(PS[4][:, at + ne:at + 2 * ne], ones[:], mask[:, 0, 0:ne], start=False, stop=True)
                for j in range(P // ne):
                    for b in range(NB):
                        last = mm(PS[4][j * ne:(j + 1) * ne, 384:385], mask[:, b, 0:ne], ones[:, 0:1], start=(b == 0), stop=(b == NB - 1))
                last.then_inc(S["rank_mm"], 1)

            def over_list(L):
                pe.wait_ge(S["over_made"], 2 * L - 1)
                mm(PS[7][:, 0:1], tri[:, 0, :], over_flag, start=True, stop=True)
                mm(PS[7][:, 1:2], ones[:], over_flag, start=True, stop=True).then_inc(S["over_mm"], 1)
                pe.wait_ge(S["over_made"], 2 * L)
                mm(PS[7][:, LIST:2 * LIST], Sw[:, 1, 0, :], over_pick, start=True, stop=True)
                mm(PS[7][:, 2 * LIST:3 * LIST], Sw[:, 1, 1, :], over_pick, start=True, stop=True).then_inc(S["over_mm"], 1)

            def experts(L, G, NG, F, GU, gateup_pieces, down_pieces):
                DN = GU // 2 if GU > 1 else 1
                pre, cap, before = f"e{L}_", P // G, (L - 1) * NG1

                def gather_rows(done):
                    for k in range(KD):
                        for q in range(NB * 3):
                            b, part = q // 3, q % 3
                            last = mm(PS[4 + k // 4][:, (k % 4) * P:(k % 4 + 1) * P], hs[:, part, b, k * P:(k + 1) * P],
                                      Sb[:, b, :], start=(q == 0), stop=(q == NB * 3 - 1))
                        if k % 4 == 3:
                            last.then_inc(done, 1)

                def gather(n):
                    pe.wait_ge(S["x_S"], 2 * (n + before) + 2)
                    gather_rows(S["x_gather"])

                def add_rows():
                    for b in range(NB):
                        for h in range(2):
                            last = mm(PS[2 * b + h][:, :], Ct[:, b * P:(b + 1) * P], Y[:, h * 512:(h + 1) * 512],
                                      start=False, stop=False)
                    return last

                def combine(g):
                    pe.wait_ge(S["x_Ct"], (g + before) + 1)
                    pe.wait_ge(S["x_Y"], 2 * (g + before) + 2)
                    return add_rows()

                def body(g, par, first=False, last=False):
                    pe.wait_ge(S["x_hTe"], 2 * (g + before) + 2)
                    for sem, need, bank, ks, view in gateup_pieces(g, par):
                        pe.wait_ge(sem, need)
                        for kk, k in enumerate(ks):
                            for j in range(G):
                                dst = PS[bank][j * cap:(j + 1) * cap, :]
                                m = mm(dst if L == 2 else dst.rearrange("s (c n) -> s c n", c=2), hTe[:, k, j * cap:(j + 1) * cap],
                                       view[:, j, kk, :] if L == 2 else view[:, j, :, kk, :], start=(k == 0), stop=(k == KD - 1))
                        m.then_inc(S[pre + "gateup"], 1)
                    if not first:
                        combine(g - 1)
                    pe.wait_ge(S["x_act"], (g + before) + 1)
                    for f in range(F // P):
                        m = tr(PS[6][:, f * P:(f + 1) * P], av[:, f * P:(f + 1) * P], ident[:])
                    m.then_inc(S["x_turned"], 1)
                    if first:
                        pe.wait_ge(S["over_known"], L)
                    for b in range(NB):
                        m = tr(PS[7][:, b * P:(b + 1) * P], Sw[:, par, b, :], ident[:])
                    m.then_inc(S["x_turned"], 1)
                    if not last:
                        gather(g + 1)
                    pe.wait_ge(S["x_aT"], (g + before) + 1)
                    pe.wait_ge(S["x_Ct"], (g + before) + 1)
                    for sem, need, cs, view in down_pieces(g, par):
                        pe.wait_ge(sem, need)
                        for cc, c in enumerate(cs):
                            for h in range(2):
                                for j in range(G):
                                    m = mm(PS[6 + h][j * cap:(j + 1) * cap, :], aT[:, c, j * cap:(j + 1) * cap],
                                           view[:, j, cc, h * 512:(h + 1) * 512], start=(c == 0), stop=(c == F // P - 1))
                        m.then_inc(S[pre + "down"], 1)

                pe.wait_ge(S["hs_part"], 12 * L)
                gather(0)
                if L == 1:
                    shared_down()
                over_list(L)
                body(0, 0, first=True)
                with pe.Fori(0, NG // 2 - 1) as i:
                    body(2 * i + 1, 1)
                    body(2 * i + 2, 0)
                body(NG - 1, 1, last=True)
                combine(NG - 1).then_inc(S["over_done"], 1)

                def item(i, n, s):
                    wg, wu, wd = over_weights(L, s)
                    pe.wait_ge(S["over_slots"], 6 * n + 4)
                    gather_rows(S["over_gather"])
                    pe.wait_ge(S["over_hTe"], 2 * n + 2)
                    if L == 2:
                        pe.wait_ge(S["over_loaded"], 48 * i + 48)
                    elif isinstance(i, int):
                        pe.wait_ge(S[f"over_loaded{s}"], 48)
                    else:
                        pe.wait_ge(S[f"over_loaded{s}"], 16 * (i - s) + 48)
                    for bank, w in ((4, wg), (5, wu)):
                        for k in range(KD):
                            m = mm(PS[bank][:, 0:F], hTe[:, k, :], w[:, k, :], start=(k == 0), stop=(k == KD - 1))
                        m.then_inc(S["over_gateup"], 1)
                    pe.wait_ge(S["over_slots"], 6 * n + 6)
                    for b in range(NB):
                        m = tr(PS[7][:, b * P:(b + 1) * P], Sw[:, 0, b, :], ident[:])
                    m.then_inc(S["over_turned"], 1)
                    pe.wait_ge(S["over_act"], n + 1)
                    for f in range(F // P):
                        m = tr(PS[6][:, f * P:(f + 1) * P], av[:, f * P:(f + 1) * P], ident[:])
                    m.then_inc(S["over_turned"], 1)
                    pe.wait_ge(S["over_copied"], 2 * n + 2)
                    for c in range(F // P):
                        for h in range(2):
                            m = mm(PS[6 + h][:, :], aT[:, c, :], wd[:, c, h * 512:(h + 1) * 512], start=(c == 0), stop=(c == F // P - 1))
                    m.then_inc(S["over_down"], 1)
                    pe.wait_ge(S["over_Y"], 2 * n + 2)
                    add_rows().then_inc(S["over_done"], 1)
                over_items(pe, L, item)
                for n in range(4):
                    mm(PS[n][:, :], zeros[:, 0:P // 2].bitcast(BF16), outer(ones[:].bitcast(BF16), 2), start=False, stop=True)\
                        .then_inc(S["y_done"], 1)

            modulated(0, xn)
            routed(1, wr, E1)
            def shared_gateup(b):
                for k in range(KD):
                    last = mm(PS[6 + b][:, :], hT[:, k, b * P:(b + 1) * P], sh_gu[:, k, :], start=(k == 0), stop=(k == KD - 1))
                last.then_inc(S["sh_gateup"], 1)

            def shared_down():
                pe.wait_ge(S["sh_act"], 2)
                for b in range(NB):
                    for f in range(2):
                        last = tr(PS[7][:, f * T + b * P:f * T + (b + 1) * P], a_sh[:, b, f * P:(f + 1) * P], ident[:])
                last.then_inc(S["sh_turned"], 1)
                pe.wait_ge(S["hs_left"], 4)
                pe.wait_ge(S["sh_aT"], 1)
                for b in range(NB):
                    for h in range(2):
                        for f in range(2):
                            last = mm(PS[2 * b + h][:, :], aT_sh[:, f, b * P:(b + 1) * P], sh_dn[:, f, h * 512:(h + 1) * 512],
                                      start=(f == 0), stop=False)
                last.then_inc(S["stream_used"], 1)

            i = AT["shared"]
            pe.wait_ge(S[f"stream_loaded{i % 3}"], 16 * (i // 3 + 3))
            shared_gateup(0)
            pe.wait_ge(S["route_sig"], 1)
            ranks(1, E1)
            shared_gateup(1)
            pe.wait_ge(S["rank_ready"], 1)
            experts(1, G1, NG1, F1, 1,
                    lambda g, par: [(S[f"e1_gu{par}"], 32 * (g + 2 - par), 4, range(KD), gu1[par])],
                    lambda g, par: [(S[f"e1_dn{par}"], 16 * (g + 2 - par), range(2), dn1[par])])

            modulated(1, xn)

            def loaded2(i):
                pe.wait_ge(S[f"stream2_loaded{i % 2}"], 16 * (i // 2 + 1) if i != 5 else 48)

            loaded2(0)
            for m in range(8):
                bank = 4 + m // 2 % 4
                for k in range(KD):
                    last = mm(PS[bank][:, (m % 2) * T:(m % 2 + 1) * T], w2k[0][:, k, m * P:(m + 1) * P], hT[:, k, :],
                              start=(k == 0), stop=(k == KD - 1))
                if m == 7:
                    last.then_inc(S["stream2_used"], 1)
                elif m % 2:
                    last.then_inc(S["qk2_mm"], 1)
            loaded2(1)
            for n in range(4):
                w0, b = n // 2 * 512, n % 2
                for k in range(KD):
                    last = mm(PS[n][:, :], hT[:, k, b * P:(b + 1) * P], w2k[1][:, k, w0:w0 + 512], start=(k == 0), stop=(k == KD - 1))
                last.then_inc(S["stream2_used"] if n == 3 else S["vu2_mm"], 1)
            pe.wait_ge(S["bias_loaded"], 16)
            pe.wait_ge(S["qk2_ready"], 4)
            for q in range(4):
                mm(PS[4 + q][:, :], flip[:], TBr[:, 2 * q:2 * q + 2, :].rearrange("p h j -> p (h j)"), start=True, stop=True)\
                    .then_inc(S["tb_mm"], 1)

            pe.wait_ge(S["vu2_ready"], 4)
            pe.wait_ge(S["band_loaded"], 32)
            for gq in range(4):
                pe.wait_ge(S["tb_flipped"], gq + 1)
                for b in range(NB):
                    last = mm(PS[4 + gq][:, 0:T], u2[:, b, gq * P:(gq + 1) * P], band[:, gq, b, :], start=(b == 0), stop=(b == 1))
                last.then_inc(S["pool_mm"], 1)
            pe.wait_ge(S["poolw_loaded"], 32)
            for gq in range(4):
                pe.wait_ge(S["pool_ready"], gq + 1)
                mm(PS[4 + gq][:, T:2 * T], poolw[:, gq, :], dT2[:, gq, :], start=True, stop=True).then_inc(S["pool_mm"], 1)

            def branch_gate(n):
                half, b, h = n // 4, n // 2 % 2, n % 2
                if n % 4 == 0:
                    loaded2(2 + half)
                if n >= 2:
                    pe.wait_ge(S["zg_biased"], n - 1)
                for k in range(KD):
                    last = mm(PS[6 + n % 2][:, :], hT[:, k, b * P:(b + 1) * P], w2k[2 + half][:, k, h * 512:(h + 1) * 512],
                              start=(k == 0), stop=(k == KD - 1))
                last.then_inc(S["stream2_used"] if n % 4 == 3 else S["zg_mm"], 1)

            pe.wait_ge(S["pool_ready"], 8)

            def scores(h):
                half, hp = slice(64 * (h % 2), 64 * (h % 2) + 64), h // 2
                if h >= 2:
                    pe.wait_ge(S["score_taken"], h - 1)
                mm(PS[h % 2][:, 0:P], qT2[half, hp, 0:P], kT2[half, hp, 0:P], start=True, stop=True)
                mm(PS[h % 2][:, P:P + T], qT2[half, hp, P:T], kT2[half, hp, :], start=True, stop=True).then_inc(S["score_mm"], 1)

            def attend(h):
                half, hp = slice(64 * (h % 2), 64 * (h % 2) + 64), h // 2
                o = hp % 2 * T
                pe.wait_ge(S["prob_ready"], h + 1)
                for n in range(3):
                    last = tr(PS[2 + h % 2][:, n * P:(n + 1) * P], pexp[:, h % 2, n * P:(n + 1) * P], ident[:])
                last.then_inc(S["probT"], 1)
                pe.wait_ge(S["pT_ready"], h + 1)
                mm(PS[4 + hp // 2][half, o:o + T], vv2[:, 0, h * DH2:(h + 1) * DH2], pT[:, h % 2, 0:T], start=True, stop=False,
                   skip_group_check=True)
                mm(PS[4 + hp // 2][half, o + P:o + T], vv2[:, 1, h * DH2:(h + 1) * DH2], pT[:, h % 2, T:T + P], start=False, stop=True,
                   skip_group_check=True).then_inc(S["attn_mm"], 1)

            scores(0)
            for h in range(HEADS2):
                if h + 1 < HEADS2:
                    scores(h + 1)
                branch_gate(h)
                attend(h)

            loaded2(4)
            pe.wait_ge(S["stream2_loaded0"], 16 * 4)
            pe.wait_ge(S["attn_done"], 1)
            for n in range(4):
                b, h = n // 2, n % 2
                for br, src in ((0, oT2), (1, plT2)):
                    for k in range(4):
                        last = mm(PS[4 * br + n][:, :], src[:, k, b * P:(b + 1) * P], w2k[4][:, 4 * br + k, h * 512:(h + 1) * 512],
                                  start=(k == 0), stop=(k == 3))
                last.then_inc(S["stream2_used"] if n == 3 else S["proj_mm"], 1)
            pe.wait_ge(S["mixed_ready"], 1)
            for k in range(KD):
                for b in range(NB):
                    last = tr(PS[k // 2][:, (k % 2) * T + b * P:(k % 2) * T + (b + 1) * P], xn[:, b, k * P:(k + 1) * P], ident[:])
                if k % 2:
                    last.then_inc(S["mixedT_mm"], 1)
            pe.wait_ge(S["mixedT_ready"], 4)
            pe.wait_ge(S["stream2_loaded1"], 16 * 3)
            for n in range(4):
                b, h = n // 2, n % 2
                for k in range(KD):
                    last = mm(PS[4 + n][:, :], hT[:, k, b * P:(b + 1) * P], w2k[5][:, k, h * 512:(h + 1) * 512],
                              start=(k == 0), stop=(k == KD - 1))
                last.then_inc(S["stream2_used"] if n == 3 else S["proj_mm"], 1)

            modulated(2, xn)
            routed(2, wr2, 36)
            pe.wait_ge(S["zraw_ready"], 1)
            ranks(2, E2)
            pe.wait_ge(S["hs_left"], 12)
            for n in range(4):
                mm(PS[n][:, :], zeros[:], hT[:, 0:2, :].rearrange("p k t -> p (k t)"), start=True, stop=False)
            pe.wait_ge(S["rank_ready"], 2)
            experts(2, G2, NG2, F2, 4,
                    lambda g, par: [(S["e2_piece0"], 64 * (2 * g + 1), 4, range(0, 4), gu2[0]),
                                    (S["e2_piece1"], 64 * (2 * g + 1), 4, range(4, 8), gu2[1]),
                                    (S["e2_piece2"], 64 * (2 * g + 1), 5, range(0, 4), gu2[2]),
                                    (S["e2_piece0"], 64 * (2 * g + 2), 5, range(4, 8), gu2[0])],
                    lambda g, par: [(S["e2_piece1"], 64 * (2 * g + 2), range(0, 2), dn2[1]),
                                    (S["e2_piece2"], 64 * (2 * g + 2), range(2, 4), dn2[2])])

        @block.vector
        def _(dve):
            v = nc.vector
            step = Steps(dve, S["dve_step"])

            dve.wait_ge(S["vecT"], 1)
            step(v.tensor_copy(convw[:], PS[0][:, 256:380]), wait=False)
            step(v.tensor_copy(adab[:].rearrange("p b n -> p (b n)"), PS[0][:, 128:224]))
            step(v.tensor_copy(cols[:], PS[0][:, 0:N_COLS]), S["cols_ready"])
            dve.wait_ge(S["consts"], 1)
            step(v.tensor_tensor(sel16, ident[:, 0:16], ident[:, 32:48], ALU.add))
            step(v.tensor_tensor(sel16, sel16, ident[:, 64:80], ALU.add))
            step(v.tensor_tensor(sel16, sel16, ident[:, 96:112], ALU.add))
            step(v.tensor_copy(selrow[:, 0, :], sel16[:, 0:1].to_broadcast([P, P])))
            step(v.tensor_copy(selrow[:, 1, :], sel16[:, 2:3].to_broadcast([P, P])), S["sel_ready"])

            for n, src, dst in ((0, x, xn), (1, ctxt, ctxt)):
                dve.wait_ge(S["norm_sq"], 2 * n + 2)
                mean = st[:, 4 + 2 * n:6 + 2 * n]
                step(v.tensor_scalar(mean, st[:, 2 * n:2 * n + 2], 1.0 / D, EPS, ALU.mult, ALU.add), S["norm_ms"])
                dve.wait_ge(S["norm_root"], n + 1)
                step(v.reciprocal(mean, mean))
                for b in range(NB):
                    ins = v.tensor_scalar(dst[:, b, :], src[:, b, :], st[:, 4 + 2 * n + b:5 + 2 * n + b], None, ALU.mult)
                    step(ins, S["xnorm_ready"] if b else None)

            dve.wait_ge(S["ada_ready"], ada_done[2])
            mixmod = modc[:, 0, 0:2, :, :].rearrange("p s k v -> p (s k) v")
            step(v.tensor_tensor(mixmod, mixmod, inner(adab[:, 0, 0:16], 3), ALU.add))
            for n in range(2):
                step(v.scalar_tensor_tensor(out=am[:, n, :], in0=modc[:, 0, 1, :, n], scalar=1.0,
                                            in1=cols[:, C_GPRE:C_GPRE + 8], op0=ALU.add, op1=ALU.mult),
                     S["am_ready"] if n else None)
            for k in range(KD):
                dve.wait_ge(S["modT"], k // 2 + 1)
                step(v.tensor_scalar(hT[:, k, :], PS[k // 2][:, (k % 2) * T:(k % 2 + 1) * T], am[:, 0, k:k + 1],
                                     modc[:, 0, 0, k, 0:1], ALU.mult, ALU.add), S["h_ready"], wait=False)

            dve.wait_ge(S["row_loaded"], 112)
            step(v.tensor_scalar(rowb[:, 0:256], rowb[:, 0:256], DK ** -0.5, None, ALU.mult))
            step(v.tensor_tensor(small[:, 344:360], rowb[:, 1280:1296], small[:, 344:360], ALU.add))
            ev = S["proj_ev"]
            dve.wait_ge(S["proj_mm"], 1)
            for m in range(2):
                step(v.tensor_scalar(qT[:, m, :], PS[0][:, m * T:(m + 1) * T], cols[:, C_BQK + m:C_BQK + m + 1], None, ALU.add),
                     ev if m else None, wait=False)
            dve.wait_ge(S["proj_mm"], 2)
            for m in range(2):
                step(v.tensor_scalar(kT[:, m, :], PS[1][:, m * T:(m + 1) * T], cols[:, C_BQK + 2 + m:C_BQK + 3 + m],
                                     DK ** -0.5, ALU.add, ALU.mult), ev if m else None, wait=False)
            dve.wait_ge(S["proj_mm"], 3)
            step(v.scalar_tensor_tensor(out=knat[:, 2:4, :], in0=PS[2][:].rearrange("p (b n) -> p b n", b=2),
                                        scalar=DK ** -0.5, in1=outer(rowb[:, 0:256], 2), op0=ALU.mult, op1=ALU.add), ev, wait=False)
            dve.wait_ge(S["proj_mm"], 4)
            step(v.tensor_copy(knat[:, 0:2, :], PS[3][:].rearrange("p (b n) -> p b n", b=2)), ev, wait=False)
            for c in range(4):
                dve.wait_ge(S["proj_mm"], 5 + c)
                step(v.tensor_tensor(v1[:, c, :, 0:DV], PS[(4 + c) % 5][:].rearrange("p (h n) -> p h n", h=HEADS),
                                     rowb[:, 256:768].rearrange("p (h n) -> p h n", h=HEADS), ALU.add), ev, wait=False)
            for b in range(NB):
                dve.wait_ge(S["proj_mm"], 9 + b)
                step(v.tensor_tensor(osig[:, b, :], PS[(8 + b) % 5][:], rowb[:, 768:1280], ALU.add), ev)
            dve.wait_ge(S["proj_mm"], 11)
            for j in range(4):
                step(v.tensor_copy(ada_rows[32 * j:32 * j + 16, 0:T], PS[0][32 * j:32 * j + 16, 0:T]), ev if j == 3 else None)
            dve.wait_ge(S["proj_mm"], 12)
            for n, bank in enumerate((1, 7)):
                step(v.tensor_tensor(G[:, 2 * n:2 * n + 2, :], PS[bank][:, 0:32].rearrange("p (c n) -> p c n", c=2),
                                     outer(small[:, 344:360], 2), ALU.add), ev if n else None)
            gv = G.rearrange("p c (d f h) -> p c d f h", d=2, f=2)
            li, lf = gv[:, :, :, 0, :], gv[:, :, :, 1, :]
            step(v.scalar_tensor_tensor(out=lft, in0=lf, scalar=-1.0, in1=lf, op0=ALU.mult, op1=ALU.min), S["exp_in"])
            for i in range(4):
                dve.wait_ge(S["usig_ready"], i + 1)
                step(v.scalar_tensor_tensor(out=upad[:, i, :, HALO:HALO + ROW],
                                            in0=PS[(12 + i) % 5][:, 0:T].rearrange("p (r t) -> p r t", r=ROWS),
                                            scalar=cols[:, C_BCONV + i:C_BCONV + i + 1],
                                            in1=usig[:, i, :].rearrange("p (r t) -> p r t", r=ROWS),
                                            op0=ALU.add, op1=ALU.mult), S["u_ready"])
            def conv_taps(j0, j1):
                for j in range(j0, j1):
                    for i in range(2):
                        acc = cacc[:, i, :].rearrange("p (r t) -> p r t", r=ROWS)
                        w, src = convw[:, 4 * j + i:4 * j + i + 1], upad[:, i, :, j:j + ROW]
                        if j == 0:
                            ins = v.tensor_scalar(acc, src, w, cols[:, C_CONVB + i:C_CONVB + i + 1], ALU.mult, ALU.add)
                        else:
                            dve.wait_ge(S["conv_taps"], 2 * j + i - 1)
                            ins = v.scalar_tensor_tensor(out=acc, in0=src, scalar=w, in1=acc, op0=ALU.mult, op1=ALU.add)
                        ins.then_inc(S["conv_taps"], 1)

            def split_taps(j0, j1):
                acc = cacc2.rearrange("p (r t) -> p r t", r=ROWS)
                for j in range(j0, j1):
                    w, src = convw[:, 4 * j + 2:4 * j + 3], upad[:, 2, :, j:j + ROW]
                    if j == SPLIT_TAP:
                        step(v.tensor_scalar(acc, src, w, None, ALU.mult))
                    else:
                        step(v.scalar_tensor_tensor(out=acc, in0=src, scalar=w, in1=acc, op0=ALU.mult, op1=ALU.add))

            dve.wait_ge(S["exp_out"], 1)
            step(v.scalar_tensor_tensor(out=LF, in0=lf, scalar=0.0, in1=lft, op0=ALU.min, op1=ALU.subtract), S["lf_ready"])

            dve.wait_ge(S["osig_ready"], 1)
            step(v.tensor_tensor(osig, osig, outer(normg, 2), ALU.mult))
            dve.wait_ge(S["proj_mm"], 16)
            conv_taps(0, 5)
            dve.wait_ge(S["gate_mm"], 1)
            b4 = b_.rearrange("p (c d h) -> p c d h", c=4, d=2)
            for d in range(2):
                step(v.tensor_copy(b4[:, :, d, :], PS[0][:, 16 * d:16 * d + 16].rearrange("p (c h) -> p c h", c=4)))
            step(v.tensor_copy(bt_, PS[0][:, 32:64]))
            step(v.tensor_tensor(r_.rearrange("p (c d h) -> p c d h", c=4, d=2), li, b4, ALU.subtract))

            def diagonal(col, buf, sem):
                step(v.tensor_tensor(diag[:, buf, :, :], outer(ident[:], 4), inner(col, P), ALU.mult), sem, wait=False)

            diagonal(r_[:, 0:4], 0, S["diag_ready"])
            for g in range(8):
                if g < 7:
                    if g >= 1:
                        dve.wait_ge(S["row_mm"], g)
                    diagonal(r_[:, 4 * g + 4:4 * g + 8], (g + 1) % 2, S["diag_ready"])
                dve.wait_ge(S["row_mm"], g + 1)
                bank = PS[1 + g % 2][:].rearrange("p (h s) -> p h s", h=4)
                if g < 4:
                    step(v.tensor_tensor(dt4, bank, outer(mneg[:, g % 2, :], 4), ALU.add))
                    step(v.tensor_reduce(cmax[:, 4 * g:4 * g + 4], dt4, AX_X, ALU.max))
                step(v.tensor_reduce(rmax[:, 4 * g:4 * g + 4], bank, AX_X, ALU.max), S["rows_done"])
            step(v.tensor_tensor(wst, r_, rmax, ALU.subtract), S["exp_in"])

            step(v.memset(m_run[:, 0:8], 0.0))
            for j in range(3):
                m = m_run[:, 8 * j:8 * j + 8]
                a_log, e_log = dae[:, 16 * j:16 * j + 8], dae[:, 16 * j + 8:16 * j + 16]
                for d in range(2):
                    at = STATE_CHUNK[j][d] * 8 + 4 * d
                    q = slice(4 * d, 4 * d + 4)
                    step(v.tensor_tensor(mx_[:, q], m[:, q], rmax[:, at:at + 4], ALU.max))
                    step(v.tensor_tensor(e_log[:, q], rmax[:, at:at + 4], mx_[:, q], ALU.subtract))
                    step(v.tensor_tensor(m_run[:, 8 * j + 8 + 4 * d:8 * j + 12 + 4 * d], bt_[:, at:at + 4], mx_[:, q], ALU.add))
                step(v.tensor_tensor(a_log, m, mx_, ALU.subtract), S["exp_in"] if j == 2 else None)
            conv_taps(5, 8)
            dve.wait_ge(S["exp_out"], 2)
            for j in range(3):
                for d in range(2):
                    c = STATE_CHUNK[j][d]
                    step(v.tensor_tensor(kw[:, 2 * j + d, :].rearrange("p (h n) -> p h n", h=HEADS),
                                         knat[:, c, :].rearrange("p (h n) -> p h n", h=HEADS),
                                         inner(wst[:, 8 * c + 4 * d:8 * c + 4 * d + 4], DK), ALU.mult), S["kw_ready"], wait=False)
            for c in range(2):
                for d in range(2):
                    prev = m_run[:, (16 if c == d else 24) + 4 * d:(16 if c == d else 24) + 4 * d + 4]
                    q = slice(8 * c + 4 * d, 8 * c + 4 * d + 4)
                    step(v.tensor_tensor(m_t[:, q], prev, cmax[:, q], ALU.max))
                    step(v.tensor_tensor(ee[:, q], prev, m_t[:, q], ALU.subtract))
            step(v.scalar_tensor_tensor(out=ee[:, 16:32], in0=b_[:, 0:16], scalar=-1.0, in1=m_t, op0=ALU.mult,
                                        op1=ALU.subtract), S["exp_in"])
            conv_taps(8, 10)
            dve.wait_ge(S["exp_out"], 3)
            for half in range(2):
                q = slice(64 * half, 64 * half + 64)
                step(v.tensor_copy(ae2[q, :], dae[q, :].rearrange("p (n r) -> p n r", r=2)[:, :, half]))
            conv_taps(10, 13)
            for j in range(3):
                for d in range(2):
                    dve.wait_ge(S["state_mm"], 2 * j + d + 1)
                    local = PS[3 + d][:, 0:258].rearrange("p (h n) -> p h n", h=2)
                    a_ = inner(ae2[:, 8 * j + 2 * d:8 * j + 2 * d + 2], 129)
                    e_ = inner(ae2[:, 8 * j + 4 + 2 * d:8 * j + 6 + 2 * d], 129)
                    if j == 0:
                        step(v.tensor_tensor(state[:, 0, d, :, :], local, e_, ALU.mult), S["state_done"])
                    else:
                        step(v.tensor_tensor(stmp, local, e_, ALU.mult))
                        step(v.tensor_tensor(state[:, j - 1, d, :, :], state[:, 0, d, :, :], a_, ALU.mult))
                        step(v.tensor_tensor(state[:, j - 1, d, :, :], state[:, j - 1, d, :, :], stmp, ALU.add), S["state_done"])

            def seen(gi):
                c, d = gi // 2, gi % 2
                dve.wait_ge(S["mrow_mm"], gi + 1)
                for h in range(HEADS):
                    at = 8 * c + 4 * d + h
                    step(v.scalar_tensor_tensor(out=dts[gi % 2][:, h, :], in0=PS[gi % 2][:, h * P:(h + 1) * P], scalar=r_[:, at:at + 1],
                                                in1=mbig[:, d, :], op0=ALU.subtract, op1=ALU.max),
                         S["exp_in"] if h == HEADS - 1 else None, wait=False)
                if gi < 2:
                    diagonal(m_t[:, 4 * gi + 8:4 * gi + 12], gi, S["diagm_ready"])

            for gi in range(2):
                diagonal(m_t[:, 4 * gi:4 * gi + 4], gi, S["diagm_ready"])
            conv_taps(13, 15)
            dve.wait_ge(S["exp_out"], 4)
            seen(0)
            for gi in range(4):
                c, d = gi // 2, gi % 2
                if gi < 3:
                    seen(gi + 1)
                dve.wait_ge(S["exp_out"], gi + 5)
                step(v.tensor_tensor(dts[gi % 2], dts[gi % 2], qk[:, c, :, :], ALU.mult), S["sT_ready"])
                conv_taps(15 + 4 * gi, 19 + 4 * gi)
                split_taps(SPLIT_TAP + 4 * gi, SPLIT_TAP + 4 * gi + 4)
                dve.wait_ge(S["out_mm"], gi + 1)
                for h in range(HEADS):
                    hp, at = h // 2, 8 * c + 4 * d + h
                    step(v.tensor_scalar(nd[:, h, :], PS[(3, 7)[h % 2]][:, hp * 129:hp * 129 + 129], ee[:, at:at + 1], None, ALU.mult),
                         wait=h == HEADS - 1)
                for h in range(HEADS):
                    q = slice((h % 2) * 129, (h % 2) * 129 + 129)
                    step(v.tensor_tensor(nd[:, h, :], nd[:, h, :], PS[(2, 4)[h // 2]][:, q], ALU.add), wait=h == HEADS - 1)
                step(v.scalar_tensor_tensor(out=den, in0=nd[:, :, DV], scalar=-1.0, in1=nd[:, :, DV], op0=ALU.mult, op1=ALU.max))
                step(v.tensor_tensor(den, den, ee[:, 16 + 8 * c + 4 * d:20 + 8 * c + 4 * d], ALU.max))
                step(v.reciprocal(den, den))
                rows = hm[:, c, :].rearrange("p (h n) -> p h n", h=HEADS)
                if d == 0:
                    step(v.tensor_tensor(rows, nd[:, :, 0:DV], inner(den, DV), ALU.mult), S["hm_ready"])
                else:
                    step(v.tensor_tensor(nd[:, :, 0:DV], nd[:, :, 0:DV], inner(den, DV), ALU.mult))
                    step(v.tensor_tensor(rows, rows, nd[:, :, 0:DV], ALU.add), S["hm_ready"])

            dve.wait_ge(S["conv_ready"], 2)
            step(v.tensor_tensor(cacc[:, 2, :], cacc[:, 2, :], cacc2, ALU.add), S["conv_taps"])
            hg = hm.rearrange("p b (h n) -> p (b h) n", h=HEADS)
            step(v.tensor_tensor(gsq, hg, hg, ALU.mult))
            step(v.tensor_reduce(st[:, 16:24], gsq, AX_X, ALU.add))
            step(v.tensor_scalar(st[:, 8:16], st[:, 16:24], 1.0 / DV, EPS, ALU.mult, ALU.add), S["norm_ms"])
            dve.wait_ge(S["norm_root"], 3)
            step(v.reciprocal(st[:, 8:16], st[:, 8:16]))
            step(v.tensor_tensor(hg, hg, inner(st[:, 8:16], DV), ALU.mult))
            step(v.tensor_tensor(hm, hm, osig, ALU.mult), S["hn_ready"])

            dve.wait_ge(S["cmean_mm"], 1)
            step(v.tensor_scalar(cmean, PS[4][:, 0:T], 1.0 / CONV_C, None, ALU.mult))
            step(v.tensor_tensor(ctmp, cacc, outer(cmean, 4), ALU.subtract))
            step(v.tensor_tensor(cacc, ctmp, ctmp, ALU.mult), S["csq_ready"])
            for b in range(NB):
                dve.wait_ge(S["hmT"], b + 1)
                step(v.tensor_copy(mixT[:, 0:4, b * P:(b + 1) * P], PS[5 + b][:].rearrange("p (h t) -> p h t", h=HEADS)),
                     S["mixT_m"], wait=False)
            dve.wait_ge(S["cvar_mm"], 1)
            step(v.tensor_scalar(crstd, PS[7][:, 0:T], 1.0 / CONV_C, EPS, ALU.mult, ALU.add), S["norm_ms"])
            dve.wait_ge(S["norm_root"], 4)
            step(v.reciprocal(crstd, crstd))
            step(v.tensor_tensor(ctmp, ctmp, outer(crstd, 4), ALU.mult), S["cn_ready"])

            dve.wait_ge(S["rowd_loaded"], 96)
            dve.wait_ge(S["ada_ready"], ada_done[12])
            for dst, name, op in ((gate[:, 0, :], "b_mix", ALU.add), (gate[:, 1, :], "b_ffn", ALU.add),
                                  (gate2[:, 0, :], "b_mix2", ALU.add), (gate2[:, 1, :], "b_ffn2", ALU.add),
                                  (gate[:, 0, :], "post_mix", ALU.mult), (gate[:, 1, :], "post_ffn", ALU.mult)):
                step(v.tensor_tensor(dst, dst, rowd[name], op))
            for b, s, at in ((0, 2, 24), (1, 0, 0), (1, 2, 24)):
                part = modc[:, b, s:s + 2, :, :].rearrange("p s k v -> p (s k) v")
                step(v.tensor_tensor(part, part, inner(adab[:, b, at:at + 16], 3), ALU.add))
            dve.sem_inc(S["gates_made"], 1)

            norms = []

            def next_norm():
                norms.append(len(norms))
                return norms[-1]

            def root_mean_square(n, b):
                dve.wait_ge(S["norm_sq"], 5 + 2 * n + b)
                step(v.tensor_scalar(st[:, 26 + b:27 + b], st[:, 24 + b:25 + b], 1.0 / D, EPS, ALU.mult, ALU.add), S["norm_ms"])
                dve.wait_ge(S["norm_root"], 5 + 2 * n + b)
                step(v.reciprocal(st[:, 26 + b:27 + b], st[:, 26 + b:27 + b]))

            def add_branch(gate_row):
                n = next_norm()
                for b in range(NB):
                    root_mean_square(n, b)
                    step(v.scalar_tensor_tensor(out=xn[:, b, :], in0=xn[:, b, :], scalar=st[:, 26 + b:27 + b],
                                                in1=gate_row, op0=ALU.mult, op1=ALU.mult))
                    step(v.tensor_tensor(x[:, b, :], x[:, b, :], xn[:, b, :], ALU.add), S["norm_in"])

            def add_product(gate_row, n, bank):
                b, q = n // 2, slice(n % 2 * 512, n % 2 * 512 + 512)
                step(v.tensor_tensor(xn[:, b, q], bank[:], gate_row[:, q], ALU.mult))
                step(v.tensor_tensor(x[:, b, q], x[:, b, q], xn[:, b, q], ALU.add), S["norm_in"] if n % 2 else None)

            def modulated(n, blk, sec, vec, g0):
                norm = next_norm()
                for b in range(NB):
                    root_mean_square(norm, b)
                    step(v.tensor_scalar(xn[:, b, :], x[:, b, :], st[:, 26 + b:27 + b], None, ALU.mult), S["xnorm_ready"] if b else None)
                step(v.scalar_tensor_tensor(out=am[:, 0, :], in0=modc[:, blk, sec + 1, :, vec], scalar=1.0,
                                            in1=cols[:, g0:g0 + 8], op0=ALU.add, op1=ALU.mult))
                for k in range(KD):
                    dve.wait_ge(S["modT"], 8 + 4 * n + k // 2 + 1)
                    step(v.tensor_scalar(hT[:, k, :], PS[k // 2][:, (k % 2) * T:(k % 2 + 1) * T], am[:, 0, k:k + 1],
                                         modc[:, blk, sec, k, vec:vec + 1], ALU.mult, ALU.add), S["h_ready"], wait=False)

            def left_of_h(L, part):
                for n in range(4):
                    dve.wait_ge(S["hs_part"], 12 * (L - 1) + 4 * part + n + 1)
                    step(v.tensor_tensor(left[n], PS[n][:].rearrange("t (p k) -> t p k", k=KD) if part == 0 else left[n],
                                         hs_quarter[part][n], ALU.subtract),
                         S["hs_left"], wait=False)

            def over_rows(L, ne):
                cap = (CAP1, CAP2)[L - 1]
                step(v.tensor_reduce(over_idx, tri[:, 1, :], AX_X, ALU.add))
                step(v.memset(over_from, float(cap)))
                for j in range(1, P // ne):
                    past = tri[:, 1, j * ne:j * ne + 1]
                    step(v.scalar_tensor_tensor(out=over_idx, in0=past, scalar=-float(ne), in1=over_idx, op0=ALU.mult, op1=ALU.add))
                    step(v.scalar_tensor_tensor(out=over_from, in0=past, scalar=float(P), in1=over_from, op0=ALU.mult, op1=ALU.add))
                step(v.tensor_copy(Sw[:, 1, 0, :], over_idx.to_broadcast([P, P])))
                step(v.tensor_copy(Sw[:, 1, 1, :], over_from.to_broadcast([P, P])))

            def make_ranks(L, ne):
                dve.wait_ge(S["rank_mm"], L)
                step(v.tensor_tensor(over_flag, PS[4][:, 384:385], over_from, ALU.is_gt), S["over_made"])
                cum = PS[4][:, 256:256 + NB * ne].rearrange("p (b e) -> p b e", b=NB)
                step(v.tensor_tensor(rank[:, :, 0:ne], cum, mask[:, :, 0:ne], ALU.mult))
                step(v.tensor_scalar(rank[:, :, 0:ne], rank[:, :, 0:ne], -1.0, None, ALU.add), S["rank_ready"])

            def shared_act():
                for b in range(NB):
                    dve.wait_ge(S["sh_sg"], b + 1)
                    step(v.tensor_tensor(a_sh[:, b, :], sg_sh[:, b, :], PS[6 + b][:, F1:2 * F1], ALU.mult), S["sh_act"])
                dve.wait_ge(S["sh_turned"], 1)
                step(v.tensor_copy(aT_sh, PS[7][:].rearrange("p (f t) -> p f t", f=2)), S["sh_aT"])

            def over_list(L):
                dve.wait_ge(S["over_mm"], 2 * L - 1)
                step(v.tensor_tensor(over_place, PS[7][:, 0:1], over_flag, ALU.mult))
                step(v.tensor_scalar(over_place, over_place, -1.0, None, ALU.add))
                step(v.tensor_tensor(over_pick, iota[:, 0:LIST], over_place.to_broadcast([P, LIST]), ALU.is_equal), S["over_made"])
                dve.wait_ge(S["over_mm"], 2 * L)
                step(v.tensor_copy(over_expert, PS[7][:, LIST:2 * LIST]))
                step(v.tensor_copy(over_start, PS[7][:, 2 * LIST:3 * LIST]))
                step(v.tensor_copy(over_count[L - 1], PS[7][:, 1:2]), S["over_known"])

            def experts(L, G, NG, F, GU):
                pre, cap, before = f"e{L}_", P // G, (L - 1) * NG1

                def slots(n, par):
                    for b in range(NB):
                        v.tensor_tensor(Sb[:, b, :].rearrange("p (e s) -> p e s", e=G), outer(iota[:, 0:cap], G),
                                        inner(rank[:, b, bass.ds(n * G, G)], cap), ALU.is_equal).then_inc(S["x_S"], 1)
                    dve.wait_ge(S["x_S"], 2 * (n + before) + 2)
                    for b in range(NB):
                        v.tensor_tensor(Sw[:, par, b, :].rearrange("p (e s) -> p e s", e=G),
                                        Sb[:, b, :].rearrange("p (e s) -> p e s", e=G),
                                        inner(wts[:, b, bass.ds(n * G, G)], cap), ALU.mult).then_inc(S["x_Sw"], 1)

                def body(g, par, last=False):
                    dve.wait_ge(S["x_Sw"], 2 * (g + before) + 2)
                    if not last:
                        dve.wait_ge(S["x_gather"], 2 * (g + before) + 2)
                        slots(g + 1, 1 - par)
                    dve.wait_ge(S["x_sg"], (g + before) + 1)
                    dve.wait_ge(S[pre + "gateup"], GU * g + GU)
                    up = PS[4][:, F:2 * F] if L == 1 else PS[5][:, 0:F]
                    v.tensor_tensor(av[:, 0:F].rearrange("s (c p) -> s p c", p=P), sg[:, 0:F].rearrange("s (p c) -> s p c", p=P),
                                    up.rearrange("s (p c) -> s p c", p=P), ALU.mult).then_inc(S["x_act"], 1)
                    dve.wait_ge(S["x_turned"], 2 * (g + before) + 1)
                    v.tensor_copy(aT[:, 0:F // P, :], PS[6][:, 0:F].rearrange("p (f s) -> p f s", f=F // P)).then_inc(S["x_aT"], 1)
                    dve.wait_ge(S["x_turned"], 2 * (g + before) + 2)
                    v.tensor_copy(Ct, PS[7][:, 0:T]).then_inc(S["x_Ct"], 1)

                slots(0, 0)
                if L == 1:
                    shared_act()
                over_list(L)
                body(0, 0)
                with dve.Fori(0, NG // 2 - 1) as i:
                    body(2 * i + 1, 1)
                    body(2 * i + 2, 0)
                body(NG - 1, 1, last=True)

                def item(i, n, s):
                    expert = dve.value_load(over_expert[0:1, bass.ds(i, 1)], min_val=1, max_val=(E1, E2)[L - 1]) - 1
                    for b in range(NB):
                        v.tensor_tensor(over_shift[:, b:b + 1], rank[:, b, bass.ds(expert, 1)], over_start[:, bass.ds(i, 1)],
                                        ALU.subtract).then_inc(S["over_slots"], 1)
                    dve.wait_ge(S["over_slots"], 6 * n + 2)
                    for b in range(NB):
                        v.tensor_tensor(Sb[:, b, :], iota[:], over_shift[:, b:b + 1].to_broadcast([P, P]),
                                        ALU.is_equal).then_inc(S["over_slots"], 1)
                    dve.wait_ge(S["over_slots"], 6 * n + 4)
                    for b in range(NB):
                        v.tensor_tensor(Sw[:, 0, b, :], Sb[:, b, :], wts[:, b, bass.ds(expert, 1)].to_broadcast([P, P]),
                                        ALU.mult).then_inc(S["over_slots"], 1)
                    dve.wait_ge(S["over_turned"], 2 * n + 1)
                    v.tensor_copy(Ct, PS[7][:, 0:T]).then_inc(S["over_copied"], 1)
                    dve.wait_ge(S["over_sg"], n + 1)
                    dve.wait_ge(S["over_gateup"], 2 * n + 2)
                    v.tensor_tensor(av[:, 0:F].rearrange("s (c p) -> s p c", p=P), sg[:, 0:F].rearrange("s (p c) -> s p c", p=P),
                                    PS[5][:, 0:F].rearrange("s (p c) -> s p c", p=P), ALU.mult).then_inc(S["over_act"], 1)
                    dve.wait_ge(S["over_turned"], 2 * n + 2)
                    v.tensor_copy(aT[:, 0:F // P, :], PS[6][:, 0:F].rearrange("p (f s) -> p f s", f=F // P))\
                        .then_inc(S["over_copied"], 1)
                over_items(dve, L, item)

            for b in range(NB):
                for h in range(2):
                    dve.wait_ge(S["stream_used"], AT["w_out"] + 1) if b and h else dve.wait_ge(S["proj_mm"], 17 + 2 * b + h)
                    q = slice(h * 512, (h + 1) * 512)
                    step(v.tensor_tensor(xn[:, b, q], PS[2 * b + h][:], rowv[:, q], ALU.add), S["norm_in"] if h else None)
            add_branch(gate[:, 0, :])
            modulated(0, 0, 2, 0, C_GFFN)
            over_rows(1, E1)
            dve.wait_ge(S["route_sig"], 1)
            step(v.tensor_tensor(tmpr, sel, outer(brt[:, 0:E1], NB), ALU.add))
            for b in range(NB):
                step(v.max(max8[:, b, :], tmpr[:, b, :]))
                step(v.match_replace(mask[:, b, :], max8[:, b, :], tmpr[:, b, :], NEG))
            step(v.tensor_tensor(mask, mask, tmpr, ALU.not_equal), S["mask_ready"])
            left_of_h(1, 0)
            step(v.tensor_tensor(wts, mask, sel, ALU.mult))
            step(v.tensor_reduce(st[:, 28:30], wts, AX_X, ALU.add))
            step(v.reciprocal(st[:, 28:30], st[:, 28:30]))
            for b in range(NB):
                step(v.tensor_scalar(wts[:, b, :], wts[:, b, :], st[:, 28 + b:29 + b], ROUTE_SCALE, ALU.mult, ALU.mult))
            left_of_h(1, 1)
            make_ranks(1, E1)
            experts(1, G1, NG1, F1, 1)
            for n in range(4):
                dve.wait_ge(S["y_done"], n + 1)
                step(v.tensor_copy(xn[:, n // 2, n % 2 * 512:n % 2 * 512 + 512], PS[n][:]), S["norm_in"] if n % 2 else None)
            add_branch(gate[:, 1, :])

            modulated(1, 1, 0, 2, C_N1)
            dve.sem_inc(S["x2_ready"], 1)
            for q in range(4):
                dve.wait_ge(S["qk2_mm"], q + 1) if q < 3 else dve.wait_ge(S["stream2_used"], 1)
                dst = (qT2 if q < 2 else kT2)[:, 2 * (q % 2):2 * (q % 2) + 2, :]
                step(v.tensor_copy(dst, PS[4 + q][:].rearrange("p (m t) -> p m t", m=2)), S["qk2_ready"])
            for n in range(4):
                dve.wait_ge(S["vu2_mm"], n + 1) if n < 3 else dve.wait_ge(S["stream2_used"], 2)
                step(v.tensor_copy((vv2 if n < 2 else u2)[:, n % 2, :], PS[n][:]), S["vu2_ready"])
            for q in range(4):
                dve.wait_ge(S["tb_mm"], q + 1)
                step(v.tensor_copy(TB[:, 2 * q:2 * q + 2, :], PS[4 + q][:].rearrange("p (h j) -> p h j", h=2)), S["tb_flipped"])
            for gq in range(4):
                dve.wait_ge(S["pool_mm"], gq + 1)
                step(v.tensor_copy(dT2[:, gq, :], PS[4 + gq][:, 0:T]), S["pool_ready"], wait=False)
            for gq in range(4):
                dve.wait_ge(S["pool_mm"], gq + 5)
                step(v.tensor_scalar(plT2[:, gq, :], PS[4 + gq][:, T:2 * T], cols[:, C_POOLS + gq:C_POOLS + gq + 1], None, ALU.mult),
                     S["pool_ready"])
            dve.wait_ge(S["tb_ready"], 1)

            def soft_max(h):
                o = h % 2
                dve.wait_ge(S["score_mm"], h + 1)
                step(v.scalar_tensor_tensor(out=pexp[:, o, 0:P], in0=PS[o][:, 0:P], scalar=DH2 ** -0.5, in1=TB[:, h, P:T],
                                            op0=ALU.mult, op1=ALU.add))
                step(v.scalar_tensor_tensor(out=pexp[:, o, P:P + T], in0=PS[o][:, P:P + T], scalar=DH2 ** -0.5, in1=TB[:, h, :],
                                            op0=ALU.mult, op1=ALU.add), S["score_taken"])
                step(v.tensor_reduce(st[:, 2 * o:2 * o + 1], pexp[:, o, 0:P], AX_X, ALU.max))
                step(v.tensor_reduce(st[:, 2 * o + 1:2 * o + 2], pexp[:, o, P:P + T], AX_X, ALU.max))
                step(v.tensor_scalar(st[:, 2 * o:2 * o + 2], st[:, 2 * o:2 * o + 2], -1.0, None, ALU.mult), S["smax_ready"])

            def probabilities(h):
                o = h % 2
                dve.wait_ge(S["sexp_ready"], 2 * h + 2)
                step(v.reciprocal(st[:, 4 + 2 * o:6 + 2 * o], st[:, 4 + 2 * o:6 + 2 * o]))
                step(v.tensor_scalar(pexp[:, o, 0:P], pexp[:, o, 0:P], st[:, 4 + 2 * o:5 + 2 * o], None, ALU.mult))
                step(v.tensor_scalar(pexp[:, o, P:P + T], pexp[:, o, P:P + T], st[:, 5 + 2 * o:6 + 2 * o], None, ALU.mult), S["prob_ready"])

            def probs_turned(h):
                dve.wait_ge(S["probT"], h + 1)
                step(v.tensor_copy(pT[:, h % 2, :], PS[2 + h % 2][:, 0:3 * P]), S["pT_ready"])

            def branch_gate(n):
                half, b, h = n // 4, n // 2 % 2, n % 2
                if n % 4 == 3:
                    dve.wait_ge(S["stream2_used"], 3 + half)
                else:
                    dve.wait_ge(S["zg_mm"], 3 * half + n % 4 + 1)
                q = slice(half * D + h * 512, half * D + h * 512 + 512)
                step(v.tensor_tensor(zg[:, b, q], PS[6 + n % 2][:], bgrow[:, q], ALU.add), S["zg_biased"])

            dve.wait_ge(S["band_loaded"], 32)
            soft_max(0)
            for h in range(HEADS2):
                if h + 1 < HEADS2:
                    soft_max(h + 1)
                probabilities(h)
                branch_gate(h)
                probs_turned(h)
                if h % 2:
                    dve.wait_ge(S["attn_mm"], h + 1)
                    step(v.tensor_copy(oT2[:, h // 2, :], PS[4 + h // 4][:, h // 2 % 2 * T:h // 2 % 2 * T + T]))
            dve.sem_inc(S["attn_done"], 1)
            dve.wait_ge(S["zg_ready"], 8)
            for n in range(4):
                b, h = n // 2, n % 2
                dve.wait_ge(S["proj_mm"], 20 + n) if n < 3 else dve.wait_ge(S["stream2_used"], 5)
                q, q2 = slice(h * 512, h * 512 + 512), slice(D + h * 512, D + h * 512 + 512)
                step(v.tensor_tensor(xn[:, b, q], PS[n][:], zg[:, b, q], ALU.mult))
                step(v.tensor_tensor(zg[:, b, q2], PS[4 + n][:], zg[:, b, q2], ALU.mult))
                step(v.tensor_tensor(xn[:, b, q], xn[:, b, q], zg[:, b, q2], ALU.add))
            dve.sem_inc(S["mixed_ready"], 1)
            for q in range(4):
                dve.wait_ge(S["mixedT_mm"], q + 1)
                step(v.tensor_copy(hT[:, 2 * q:2 * q + 2, :], PS[q][:].rearrange("p (k t) -> p k t", k=2)), S["mixedT_ready"])
            for n in range(4):
                dve.wait_ge(S["proj_mm"], 23 + n) if n < 3 else dve.wait_ge(S["stream2_used"], 6)
                add_product(gate2[:, 0, :], n, PS[4 + n])
            dve.sem_inc(S["x3_ready"], 1)

            modulated(2, 1, 2, 2, C_N2)
            over_rows(2, E2)
            dve.wait_ge(S["router_mm"], 4)
            zz = tmpr.rearrange("p b e -> p (b e)")[:, 0:72].rearrange("p (b n) -> p b n", b=NB)
            step(v.tensor_tensor(zz, PS[4][:, 0:72].rearrange("p (b n) -> p b n", b=NB), outer(brt[:, 64:100], NB), ALU.add), S["zraw_ready"])
            zgr, zex = zz[:, :, 0:GROUPS2], zz[:, :, GROUPS2:36]
            col = lambda at: rt[:, at:at + NB]
            step(v.tensor_reduce(col(8), zgr, AX_X, ALU.max))
            ge = rt[:, 0:8].rearrange("p (b n) -> p b n", b=NB)
            oh = rt[:, 32:40].rearrange("p (b n) -> p b n", b=NB)
            step(v.tensor_tensor(ge, zgr, inner(col(8), GROUPS2), ALU.subtract), S["zexp_in"])
            dve.wait_ge(S["zexp"], 1)
            step(v.tensor_reduce(col(10), ge, AX_X, ALU.add))
            step(v.reciprocal(col(10), col(10)))
            dve.wait_ge(S["desc_ready"], 1)

            step(v.tensor_tensor(oh, zgr, inner(col(8), GROUPS2), ALU.is_equal))
            step(v.tensor_tensor(oh, oh, outer(desc[:, 0:GROUPS2], NB), ALU.mult))
            step(v.tensor_reduce(col(12), oh, AX_X, ALU.max))
            step(v.tensor_tensor(oh, oh, inner(col(12), GROUPS2), ALU.is_equal))
            step(v.tensor_scalar(oh, oh, -1.0, -NEG, ALU.add, ALU.mult))
            zl = sel[:, :, 0:E2]
            step(v.tensor_tensor(zl.rearrange("p b (g e) -> p b g e", g=GROUPS2), zex.rearrange("p b (g e) -> p b g e", g=GROUPS2),
                                 oh.unsqueeze(3).to_broadcast([P, NB, GROUPS2, PER_GROUP2]), ALU.add))
            for b in range(NB):
                step(v.max(max8[:, b, :], zl[:, b, :]), wait=b == NB - 1)
            top, second = max8[:, :, 0], max8[:, :, 1]
            step(v.tensor_tensor(col(24), second, top, ALU.subtract), S["zexp_in"])
            step(v.tensor_copy(col(16), top))
            step(v.memset(max8[:, :, 2:8], 3e38))
            one = mask[:, :, 0:E2]
            for b in range(NB):
                step(v.match_replace(one[:, b, :], max8[:, b, :], zl[:, b, :], 2e38), wait=b == NB - 1)
            step(v.tensor_tensor(one, one, zl, ALU.not_equal), S["mask_ready"])
            left_of_h(2, 0)
            dve.wait_ge(S["zexp"], 2)
            step(v.tensor_scalar(col(20), col(24), 1.0, None, ALU.add))
            step(v.reciprocal(col(20), col(20)))
            step(v.tensor_tensor(col(20), col(20), col(10), ALU.mult))
            step(v.tensor_tensor(col(22), col(20), col(24), ALU.mult))
            step(v.tensor_tensor(col(20), col(20), col(22), ALU.subtract))
            w2 = wts[:, :, 0:E2]
            step(v.tensor_tensor(w2, zl, inner(col(16), E2), ALU.is_equal))
            step(v.tensor_tensor(w2, w2, inner(col(20), E2), ALU.mult))
            step(v.tensor_tensor(w2, w2, inner(col(22), E2), ALU.add))
            step(v.tensor_tensor(w2, w2, one, ALU.mult))
            left_of_h(2, 1)
            make_ranks(2, E2)
            experts(2, G2, NG2, F2, 4)
            for n in range(4):
                dve.wait_ge(S["y_done"], 5 + n)
                add_product(gate2[:, 1, :], n, PS[n])
            dve.wait_ge(S["poolw_loaded"], 32)
            norm = next_norm()
            for b in range(NB):
                root_mean_square(norm, b)
                step(v.scalar_tensor_tensor(out=xn[:, b, :], in0=x[:, b, :], scalar=st[:, 26 + b:27 + b], in1=rowf,
                                            op0=ALU.mult, op1=ALU.mult), S["out_ready"])



INPUTS = ["x", "c", "ctx", "c_ctx", "w_ada", "b_ada", "g_pre_mix", "g_post_mix", "g_pre_ffn", "g_post_ffn", "w_in", "b_in",
          "b_gate", "mlstm_norm_g", "conv_w", "conv_b", "conv_ln_g", "conv_ln_b", "w_out", "b_out", "w_router",
          "b_router", "we_gate", "we_up", "we_down", "ws_gate", "ws_up", "ws_down", "c_2", "w_ada_2", "b_ada_2",
          "norm1_g_2", "w_in_2", "b_gate_2", "rel_bias_2", "pool_w_2", "pool_scale_2", "w_branch_attn_2",
          "w_branch_pool_2", "w_out_2", "norm2_g_2", "w_router_group_2", "b_router_group_2", "w_router_expert_2",
          "b_router_expert_2", "w_expert_gate_2", "w_expert_up_2", "w_expert_down_2", "norm_f_g_2"]


def kernel(**inputs):
    import concourse.bacc as bacc
    from concourse.bass_utils import run_bass_kernel_spmd as run

    nc = bacc.Bacc("TRN2", target_bir_lowering=False, num_devices=1)
    arrays, aps = {}, {}
    for name in INPUTS:
        a = np.ascontiguousarray(inputs[name])
        arrays["in_" + name] = a
        aps[name] = nc.dram_tensor("in_" + name, a.shape, mybir.dt.from_np(a.dtype), kind="ExternalInput").ap()
    for name, a in shape_constants().items():
        arrays["const_" + name] = a
        aps[name] = nc.dram_tensor("const_" + name, a.shape, F32, kind="ExternalInput").ap()
    out = nc.dram_tensor("out", (1, T, D), F32, kind="ExternalOutput").ap()
    two_block_network(nc, aps, out)
    return run(nc, [arrays], core_ids=[0]).results[0]["out"]
```
